# Optimizing a Trainium2 kernel written in Bass

```python
import math
import jax, jax.numpy as jnp
from jax import lax
import numpy as np

D_MODEL = 2048
BATCH = 1
SEQ = 256
DEPTH = 1

HEAD_DIM = 128
D_MIX = D_MODEL
RET_WIDTH = D_MIX // 2
FOX_WIDTH = D_MIX - RET_WIDTH
RET_HEADS = RET_WIDTH // HEAD_DIM
FOX_HEADS = FOX_WIDTH // HEAD_DIM
RET_CHUNK = 128
FOX_BLOCK = 128
ROPE_BASE = 10000.0
N_GROUPS = 4
EXPERTS_PER_GROUP = 8
N_EXPERTS = N_GROUPS * EXPERTS_PER_GROUP
TOP_K_FINE = 2
D_EXPERT = D_MODEL // 4
N_MOD = 6
EPS = 1e-6
IN_COLS = 4 * RET_WIDTH + 3 * FOX_WIDTH + FOX_HEADS

kernel_name = "hybrid_retention_fox_hmoe_layer"

def rms_norm(x, w):
    xf = x.astype(jnp.float32)
    y = xf * lax.rsqrt(jnp.mean(xf * xf, axis=-1, keepdims=True) + EPS)
    return y.astype(x.dtype) * w

def head_rms(x):
    xf = x.astype(jnp.float32)
    return (xf * lax.rsqrt(jnp.mean(xf * xf, axis=-1, keepdims=True) + EPS)).astype(x.dtype)

def head_layer_norm(x):
    xf = x.astype(jnp.float32)
    mu = jnp.mean(xf, axis=-1, keepdims=True)
    var = jnp.mean(jnp.square(xf - mu), axis=-1, keepdims=True)
    return ((xf - mu) * lax.rsqrt(var + EPS)).astype(x.dtype)

def split_heads(t, n_heads):
    b, s, _ = t.shape
    return t.reshape(b, s, n_heads, HEAD_DIM).transpose(0, 2, 1, 3)

def merge_heads(t):
    b, h, s, d = t.shape
    return t.transpose(0, 2, 1, 3).reshape(b, s, h * d)

def rope(x, cos, sin):
    x1, x2 = jnp.split(x, 2, axis=-1)
    return jnp.concatenate([x1 * cos - x2 * sin, x1 * sin + x2 * cos], axis=-1)

def retention_chunkwise(q, k, v):
    b, h, s, dh = q.shape
    c = RET_CHUNK
    n = s // c
    log_gamma = jnp.log1p(-jnp.exp2(-5.0 - jnp.arange(h, dtype=jnp.float32)))
    k = k * (dh ** -0.5)
    qc = q.reshape(b, h, n, c, dh)
    kc = k.reshape(b, h, n, c, dh)
    vc = v.reshape(b, h, n, c, dh)
    pos = jnp.arange(c, dtype=jnp.float32)
    diff = pos[:, None] - pos[None, :]
    decay = jnp.where(diff >= 0,
                      jnp.exp(log_gamma[:, None, None] * jnp.maximum(diff, 0.0)[None]),
                      0.0)
    zeta = jnp.exp(log_gamma[:, None] * (c - 1 - pos)[None])
    xi = jnp.exp(log_gamma[:, None] * (pos + 1)[None])
    chunk_decay = jnp.exp(log_gamma * c)
    scores = jnp.einsum('bhnid,bhnjd->bhnij', qc, kc) * decay[None, :, None]
    intra = jnp.einsum('bhnij,bhnjd->bhnid', scores, vc)
    kv = jnp.einsum('bhncd,bhnce->nbhde', kc * zeta[None, :, None, :, None], vc)

    def step(state, kv_n):
        return state * chunk_decay[None, :, None, None] + kv_n, state

    _, prev_states = lax.scan(step, jnp.zeros((b, h, dh, dh), kv.dtype), kv)
    cross = jnp.einsum('bhncd,nbhde->bhnce', qc, prev_states) * xi[None, :, None, :, None]
    return (intra + cross).reshape(b, h, s, dh)

def forgetting_attention(q, k, v, log_f):
    b, h, s, dh = q.shape
    nb = s // FOX_BLOCK
    cum = jnp.cumsum(log_f, axis=-1)
    qb = q.reshape(b, h, nb, FOX_BLOCK, dh).transpose(2, 0, 1, 3, 4)
    cb = cum.reshape(b, h, nb, FOX_BLOCK).transpose(2, 0, 1, 3)
    kpos = jnp.arange(s)
    scale = dh ** -0.5

    def block(args):
        i, q_i, c_i = args
        qpos = i * FOX_BLOCK + jnp.arange(FOX_BLOCK)
        logits = jnp.einsum('bhqd,bhkd->bhqk', q_i, k).astype(jnp.float32) * scale
        logits = logits + c_i[..., :, None] - cum[..., None, :]
        logits = jnp.where(kpos[None, :] <= qpos[:, None], logits, -jnp.inf)
        p = jax.nn.softmax(logits, axis=-1)
        return jnp.einsum('bhqk,bhkd->bhqd', p.astype(v.dtype), v)

    out = lax.map(block, (jnp.arange(nb), qb, cb))
    return out.transpose(1, 2, 0, 3, 4).reshape(b, h, s, dh)

def hybrid_mixer(h, w_in, fox_f_bias, ret_gn_w, fox_qn_w, fox_kn_w, fox_on_w, w_out, cos, sin):
    proj = h @ w_in
    r = RET_WIDTH
    f = FOX_WIDTH
    cuts = [r, 2 * r, 3 * r, 4 * r, 4 * r + f, 4 * r + 2 * f, 4 * r + 3 * f]
    rq, rk, rv, rg, fq, fk, fv, fgl = jnp.split(proj, cuts, axis=-1)
    rq = rope(split_heads(rq, RET_HEADS), cos, sin)
    rk = rope(split_heads(rk, RET_HEADS), cos, sin)
    rv = split_heads(rv, RET_HEADS)
    ret = merge_heads(head_layer_norm(retention_chunkwise(rq, rk, rv))) * ret_gn_w
    ret = jax.nn.silu(rg) * ret
    fq = head_rms(split_heads(fq, FOX_HEADS)) * fox_qn_w
    fk = head_rms(split_heads(fk, FOX_HEADS)) * fox_kn_w
    fv = split_heads(fv, FOX_HEADS)
    log_f = jax.nn.log_sigmoid(fgl.astype(jnp.float32) + fox_f_bias).transpose(0, 2, 1)
    fox = merge_heads(head_rms(forgetting_attention(fq, fk, fv, log_f))) * fox_on_w
    return jnp.concatenate([ret, fox], axis=-1) @ w_out

def hierarchical_moe(h, router_coarse_w, router_coarse_b, router_fine_w, router_fine_b, w1, w3, w2):
    b, s, d = h.shape
    t = h.reshape(b * s, d)
    coarse = (t @ router_coarse_w).astype(jnp.float32) + router_coarse_b
    g_prob, g_idx = lax.top_k(jax.nn.softmax(coarse, axis=-1), 1)
    fine = ((t @ router_fine_w).astype(jnp.float32) + router_fine_b).reshape(-1, N_GROUPS, EXPERTS_PER_GROUP)
    fine_sel = jnp.take_along_axis(fine, g_idx[:, :, None], axis=1)[:, 0]
    f_val, f_idx = lax.top_k(fine_sel, TOP_K_FINE)
    weights = g_prob * jax.nn.softmax(f_val, axis=-1)
    expert_id = g_idx * EXPERTS_PER_GROUP + f_idx
    combine = jnp.sum(jax.nn.one_hot(expert_id, N_EXPERTS, dtype=jnp.float32) * weights[..., None], axis=1)
    combine = combine.astype(t.dtype)

    def expert_step(acc, xs):
        w1_e, w3_e, w2_e, c_e = xs
        y = (jax.nn.silu(t @ w1_e) * (t @ w3_e)) @ w2_e
        return acc + c_e[:, None] * y, None

    acc, _ = lax.scan(expert_step, jnp.zeros_like(t), (w1, w3, w2, combine.T))
    return acc.reshape(b, s, d)

def setup_inputs(seed: int = 0) -> dict:
    key = jax.random.key(seed)
    ks = jax.random.split(key, 24)
    f32 = jnp.float32
    dm = D_MODEL
    nrm = lambda k, shape, sc: jax.random.normal(k, shape, f32) * sc
    gain = lambda k, shape: 1.0 + 0.02 * jax.random.normal(k, shape, f32)
    w_in_main = nrm(ks[2], (DEPTH, dm, IN_COLS - FOX_HEADS), dm ** -0.5)
    w_in_forget = nrm(ks[3], (DEPTH, dm, FOX_HEADS), 0.1 * dm ** -0.5)
    return {
        "x": jax.random.normal(ks[0], (BATCH, SEQ, dm), f32),
        "c": jax.random.normal(ks[1], (BATCH, dm), f32),
        "ada_w": nrm(ks[4], (DEPTH, dm, N_MOD * dm), 0.5 * dm ** -0.5),
        "ada_b": nrm(ks[5], (DEPTH, N_MOD * dm), 0.01),
        "norm_pre_mix": gain(ks[6], (DEPTH, dm)),
        "norm_post_mix": gain(ks[7], (DEPTH, dm)),
        "w_in": jnp.concatenate([w_in_main, w_in_forget], axis=-1),
        "fox_f_bias": 2.0 + 4.0 * jax.random.uniform(ks[8], (DEPTH, FOX_HEADS), f32),
        "ret_gn_w": gain(ks[9], (DEPTH, RET_WIDTH)),
        "fox_qn_w": gain(ks[10], (DEPTH, HEAD_DIM)),
        "fox_kn_w": gain(ks[11], (DEPTH, HEAD_DIM)),
        "fox_on_w": gain(ks[12], (DEPTH, FOX_WIDTH)),
        "w_out": nrm(ks[13], (DEPTH, D_MIX, dm), D_MIX ** -0.5),
        "norm_pre_ffn": gain(ks[14], (DEPTH, dm)),
        "norm_post_ffn": gain(ks[15], (DEPTH, dm)),
        "router_coarse_w": nrm(ks[16], (DEPTH, dm, N_GROUPS), dm ** -0.5),
        "router_coarse_b": nrm(ks[17], (DEPTH, N_GROUPS), 0.01),
        "router_fine_w": nrm(ks[18], (DEPTH, dm, N_EXPERTS), dm ** -0.5),
        "router_fine_b": nrm(ks[19], (DEPTH, N_EXPERTS), 0.01),
        "w1": nrm(ks[20], (DEPTH, N_EXPERTS, dm, D_EXPERT), dm ** -0.5),
        "w3": nrm(ks[21], (DEPTH, N_EXPERTS, dm, D_EXPERT), dm ** -0.5),
        "w2": nrm(ks[22], (DEPTH, N_EXPERTS, D_EXPERT, dm), D_EXPERT ** -0.5),
    }

def reference(x, c, ada_w, ada_b, norm_pre_mix, norm_post_mix, w_in, fox_f_bias, ret_gn_w,
              fox_qn_w, fox_kn_w, fox_on_w, w_out, norm_pre_ffn, norm_post_ffn,
              router_coarse_w, router_coarse_b, router_fine_w, router_fine_b, w1, w3, w2):
    s = x.shape[1]
    inv_freq = ROPE_BASE ** (-jnp.arange(0, HEAD_DIM, 2, dtype=jnp.float32) / HEAD_DIM)
    angle = jnp.arange(s, dtype=jnp.float32)[:, None] * inv_freq[None, :]
    cos = jnp.cos(angle).astype(x.dtype)
    sin = jnp.sin(angle).astype(x.dtype)
    c_act = jax.nn.silu(c)
    for l in range(DEPTH):
        mod = c_act @ ada_w[l] + ada_b[l]
        sh1, sc1, g1, sh2, sc2, g2 = [m[:, None, :] for m in jnp.split(mod, N_MOD, axis=-1)]
        h = rms_norm(x, norm_pre_mix[l]) * (1.0 + sc1) + sh1
        y = hybrid_mixer(h, w_in[l], fox_f_bias[l], ret_gn_w[l], fox_qn_w[l], fox_kn_w[l],
                         fox_on_w[l], w_out[l], cos, sin)
        x = x + g1 * rms_norm(y, norm_post_mix[l])
        h = rms_norm(x, norm_pre_ffn[l]) * (1.0 + sc2) + sh2
        y = hierarchical_moe(h, router_coarse_w[l], router_coarse_b[l], router_fine_w[l],
                             router_fine_b[l], w1[l], w3[l], w2[l])
        x = x + g2 * rms_norm(y, norm_post_ffn[l])
    return x


_drawn_inputs = setup_inputs


def setup_inputs(seed=0):
    import zlib

    import numpy as np

    out = dict(_drawn_inputs(seed))
    spreads = {}
    factors = {'norm_post_ffn': 8.0, 'router_fine_b': 2.976}
    for name, (base, spread) in spreads.items():
        noise = np.random.default_rng([zlib.crc32(name.encode()), seed]).standard_normal(out[name].shape)
        drawn = base * np.exp(spread * noise) if base else spread * noise
        out[name] = __import__('jax').numpy.asarray(drawn.astype(out[name].dtype))
    for name, factor in factors.items():
        out[name] = (out[name] * factor).astype(out[name].dtype)
    return out
```

```python
from contextlib import ExitStack, contextmanager

import numpy as np

import concourse.bass as bass
from concourse import mybir

F32 = mybir.dt.float32
F32R = mybir.dt.float32r
I32 = mybir.dt.int32
U32 = mybir.dt.uint32
ALU = mybir.AluOpType
ACT = mybir.ActivationFunctionType
AX_X = mybir.AxisListType.X

P = 128
S, D = 256, 2048
TT = S // P
KC = D // P
DH = 128
H = 8
HW = H * DH
CH = 512
NT = 7
FE = 512
FQ = FE // P
NG, EG = 4, 8
NE = NG * EG
SLOTS = 64
ROUNDS = S // SLOTS
NP = NE // 2
NV = ROUNDS * NE
EPS = 1e-6
BIG = 1e30
ROPE_BASE = 10000.0
QK_SCALE = float(DH) ** -0.5

T_ID = 0
T_COS = T_ID + P
T_SIN = T_COS + TT * 64
T_MASK = T_SIN + TT * 64
T_TRI = T_MASK + 2 * P
T_IOTA = T_TRI + P
T_SELA = T_IOTA + SLOTS
T_SELB = T_SELA + H
T_QMUL = T_SELB + H
T_QADD = T_QMUL + 1
T_ONE = T_QADD + 1
TABLE = T_ONE + P


def shape_tables():
    t = np.zeros((P, TABLE), np.float32)
    t[:, T_ID:T_ID + P] = np.eye(P, dtype=np.float32)
    inv = np.float32(ROPE_BASE) ** (-np.arange(0, DH, 2, dtype=np.float32) / np.float32(DH))
    angle = np.arange(S, dtype=np.float32)[:, None] * inv[None, :].astype(np.float32)
    for tt in range(TT):
        t[:, T_COS + tt * 64:T_COS + tt * 64 + 64] = np.cos(angle[tt * P:(tt + 1) * P])
        t[:, T_SIN + tt * 64:T_SIN + tt * 64 + 64] = np.sin(angle[tt * P:(tt + 1) * P])
    r = np.arange(P)
    t[:, T_MASK + P:T_MASK + 2 * P] = np.where(r[None, :] <= r[:, None], 0.0, -BIG)
    t[:, T_TRI:T_TRI + P] = r[:, None] < r[None, :]
    t[:, T_IOTA:T_IOTA + SLOTS] = np.arange(SLOTS)
    for h in range(H):
        t[h, T_SELA + h] = 0.0
        t[h, T_SELB + h] = 1.0
        t[H + h, T_SELA + h] = -1.0
    t[0:H, T_QMUL] = 1.0
    t[H:2 * H, T_QADD] = 1.0
    t[:, T_ONE:T_ONE + P] = 1.0
    s = np.arange(P)[:, None]
    q = np.arange(S)[None, :]
    decay = np.zeros((P, H, S), np.float32)
    for h in range(H):
        lg = np.log1p(-np.exp2(-5.0 - h))
        decay[:, h, :] = np.where(q >= s, np.exp(lg * np.maximum(q - s, 0)), 0.0) * QK_SCALE
    return t, decay.reshape(P, H * S)


class Steps:

    def __init__(self, eng, sem):
        self.eng, self.sem, self.n, self.past = eng, sem, 0, 0

    def link(self, ins):
        ins.then_inc(self.sem, 1)
        self.n += 1
        self.eng.wait_ge(self.sem, self.past + self.n)

    @contextmanager
    def loop(self, i, per, count, first=0):
        n0 = self.n
        outer = self.past
        self.past = self.past + (i - first) * per if first else self.past + i * per
        yield
        assert self.n - n0 == per, (self.n - n0, per)
        self.n = n0 + per * count
        self.past = outer


def build(nc, a, table, decay_table, out):
    ctx = ExitStack()

    def sem(name):
        return ctx.enter_context(nc.semaphore(name))

    KB = 256
    base = 17376
    arena = nc.alloc_sbuf_tensor_at("arena", [P, 207 * KB], F32, offset=base)
    split_at = {"wh": (64, 4 * 2 * CH), "wl": (176, 4 * 2 * CH), "hh": (153, KC * S), "hl": (137, KC * S),
                "mh": (144, KC * S), "ml": (160, KC * S)}
    rounded = {n: nc.alloc_sbuf_tensor_at(f"rounded_{n}", [P, cols], F32R, offset=base + kb * 1024)
               for n, (kb, cols) in split_at.items()}
    plain_at = {"w_units": (48, 2 * 4 * CH), "h_columns": (137, KC * S)}
    plain = {n: nc.alloc_sbuf_tensor_at(n, [P, cols], F32, offset=base + kb * 1024) for n, (kb, cols) in plain_at.items()}
    icount = ctx.enter_context(nc.sbuf_tensor("icount", [P, 8], I32))
    etop = ctx.enter_context(nc.sbuf_tensor("etop", [P, 2, 8], U32))
    bank = ctx.enter_context(nc.psum_tensor("bank", [P, 8, CH], F32))

    def at(kb, cols):
        o = int(kb * KB)
        return arena[:, o:o + cols]

    WH, WL = (rounded[n][:, :].rearrange("p (s j n) -> p s j n", s=4, j=2) for n in ("wh", "wl"))
    HH, HL, MH, ML = (rounded[n][:, :].rearrange("p (j s) -> p j s", j=KC) for n in ("hh", "hl", "mh", "ml"))

    X = at(0, TT * D).rearrange("p (t d) -> p t d", t=TT)
    MOD = at(16, 4 * D)
    G1B, SH2B, SC2B, G2B = (MOD[:, i * D:(i + 1) * D] for i in range(4))
    WR = plain["w_units"][:, :].rearrange("p (u j n) -> p u j n", u=2, j=4)
    HRING = at(80, 4 * D).rearrange("p (u n) -> p u n", u=4)
    HACC = at(112, 2 * D).rearrange("p (v n) -> p v n", v=2)
    XS = at(176, TT * D).rearrange("p (t d) -> p t d", t=TT)
    HT = plain["h_columns"][:, :].rearrange("p (j s) -> p j s", j=KC)
    RAW = at(80, TT * NT * HW).rearrange("p (t n) -> p t n", t=TT)
    ARING = at(32, 2 * 4 * CH).rearrange("p (u j n) -> p u j n", u=2, j=4)
    ABIAS = at(171, CH)
    SCR = at(192, 2 * HW).rearrange("p (t n) -> p t n", t=TT)
    GNW = at(28, HW)
    AACC = at(169, CH)
    WF = at(174, KC * 16).rearrange("p (j n) -> p j n", j=KC)
    FG = at(175, S)
    QKT = at(137, 4 * H * S).rearrange("p (a h s) -> p a h s", a=4, h=H)
    MIX = RAW[:, :, 0:2 * HW]
    VRET, GATE, VFOX = (RAW[:, :, i * HW:(i + 1) * HW] for i in (2, 3, 6))
    ST = RAW[:, 0, 4 * HW:4 * HW + 768].rearrange("p (b n) -> p b n", b=2)
    PR = RAW[:, 0, 4 * HW + 768:5 * HW + 256].rearrange("p (b n) -> p b n", b=2)
    PRT = RAW[:, 0, 5 * HW + 256:5 * HW + 768].rearrange("p (b n) -> p b n", b=2)
    FQB = RAW[0:2 * H, 0, 5 * HW + 768:6 * HW]
    ONW = RAW[:, 1, 4 * HW:5 * HW]
    BST = RAW[:, 1, 5 * HW:5 * HW + 16 * 6].rearrange("p (u n) -> p u n", n=6)
    BAG = RAW[:, 1, 5 * HW + 128:5 * HW + 160].rearrange("p (u n) -> p u n", n=2)
    CST = RAW[:, 1, 5 * HW + 256:5 * HW + 512].rearrange("p (a u) -> p a u", a=16)
    CSQ = RAW[:, 1, 5 * HW + 512:5 * HW + 640]
    FKB = at(169, 2 * S).rearrange("p (b s) -> p b s", b=2)
    CRING = at(32, 2 * D).rearrange("p (u n) -> p u n", u=2)
    CC = at(171, KC * 32).rearrange("p (j m) -> p j m", m=32)
    CROW = at(171, CH)
    CBIAS = at(173, CH)
    DEC = at(192, H * S).rearrange("p (h s) -> p h s", h=H)
    NW = at(192, D)
    GRING = at(64, 2 * D).rearrange("p (u n) -> p u n", u=2)
    GC = at(16, KC * 32).rearrange("p (j m) -> p j m", m=32)
    GROW, GBIAS = at(20, CH), at(18, CH)
    NW2 = at(32, D)
    ER = at(80, 6 * 8 * CH).rearrange("p (u n) -> p u n", u=6)
    H2 = at(176, TT * D).rearrange("p (t j q) -> p t j q", t=TT, j=KC)
    YG = at(176, TT * D).rearrange("p (t d) -> p t d", t=TT)
    H2T = at(48, KC * S).rearrange("p (j s) -> p j s", j=KC)
    YACC = at(64, TT * D).rearrange("p (t d) -> p t d", t=TT)
    XT = at(16, KC * P).rearrange("p (j s) -> p j s", j=KC)
    YS = at(24, D)
    SG = at(48, FE)
    HID = at(50, FE)
    HIDT = at(52, FQ * SLOTS).rearrange("p (q s) -> p q s", q=FQ)
    SELG = at(53, TT * P).rearrange("p (t s) -> p t s", t=TT)
    SELC = at(54, TT * P).rearrange("p (t s) -> p t s", t=TT)
    SELT = at(55, S)
    SLOT = at(192, TT * (NV + 2)).rearrange("p (t e) -> p t e", t=TT)
    COEF = at(194, TT * (NV + 2)).rearrange("p (t e) -> p t e", t=TT)
    used = [200 * KB]

    def small(cols):
        used[0] += cols
        assert used[0] <= 207 * KB, used
        return arena[:, used[0] - cols:used[0]]

    TAB = small(TABLE)
    IDENT = TAB[:, T_ID:T_ID + P]
    ONES = TAB[:, T_ONE:T_ONE + P]
    TRI = TAB[:, T_TRI:T_TRI + P]
    IOTA = TAB[:, T_IOTA:T_IOTA + SLOTS]
    CV, CE, CA, NPRE, SH1, A1 = (small(KC) for _ in range(6))
    SS, RS = small(32), small(32)
    QKN, FBIAS, EPSC = small(2), small(1), small(1)
    RWS = small(KC * 36).rearrange("p (j n) -> p j n", j=KC)
    RBS = small(36)
    W = [196 * KB]

    def work(cols):
        W[0] += cols
        return arena[:, W[0] - cols:W[0]]

    LG = work(TT * 36).rearrange("p (t n) -> p t n", t=TT)
    CPAD = work(TT * 8).rearrange("p (t n) -> p t n", t=TT)
    M8 = work(TT * 8).rearrange("p (t n) -> p t n", t=TT)
    F8 = work(TT * 8).rearrange("p (t n) -> p t n", t=TT)
    GE = work(TT * 4).rearrange("p (t n) -> p t n", t=TT)
    FM = work(TT * NE).rearrange("p (t n) -> p t n", t=TT)
    O1 = work(TT * NE).rearrange("p (t n) -> p t n", t=TT)
    O2 = work(TT * NE).rearrange("p (t n) -> p t n", t=TT)
    CW = work(TT * NE).rearrange("p (t n) -> p t n", t=TT)
    MK = work(TT * NE).rearrange("p (t n) -> p t n", t=TT)
    RC = work(TT * 16).rearrange("p (t n) -> p t n", t=TT)
    JUNK = work(8)

    x_v = a["x"][0].rearrange("(t p) d -> p t d", p=P)
    out_v = out[0].rearrange("(t p) d -> p t d", p=P)
    ada_v = a["ada_w"][0].rearrange("(p j) n -> p j n", j=KC)
    win_v = a["w_in"][0].rearrange("(p j) n -> p j n", j=KC)
    wout_v = a["w_out"][0].rearrange("(j p) n -> p j n", p=P)
    w1_v = a["w1"][0].rearrange("e (p j) n -> p e j n", j=KC)
    w3_v = a["w3"][0].rearrange("e (p j) n -> p e j n", j=KC)
    w2_v = a["w2"][0].rearrange("e (p q) n -> p e q n", q=FQ)

    def col(ap):
        return ap.rearrange("a (p n) -> (a p) n", n=1)

    def across(ap, n=P):
        return ap.broadcast_to([n, ap.shape[-1]])

    v_step, s_step = sem("vector_step"), sem("scalar_step")
    tab_in, c_in, x_in, small_in, fgate_in, gnw_in = (sem(n) for n in (
        "table_in", "c_in", "x_in", "small_in", "fgate_in", "gnw_in"))
    dec_in, onw_in, hbias_in, abias_in = sem("decay_in"), sem("onw_in"), sem("hbias_in"), sem("abias_in")
    nw_in = sem("normw_in")
    hring_in = [sem(f"head_rows_in{u}") for u in range(4)]
    aring_in = [sem(f"ada_rows_in{u}") for u in range(2)]
    wr_in = [sem(f"w_unit_in{u}") for u in range(2)]
    crow_in = [sem(f"late_rows_in{u}") for u in range(2)]
    cbias_in, grow_in, gbias_in = sem("sc2_bias_in"), [sem(f"g2_rows_in{u}") for u in range(2)], sem("g2_bias_in")
    nw2_in = sem("norm_post_ffn_in")
    er_in = [sem(f"expert_unit_in{u}") for u in range(6)]
    out_done = sem("out_done")
    zeroed, ce_done, ca_done, hrow_used = sem("zeroed"), sem("c_exp_done"), sem("c_act_done"), sem("head_rows_used")
    xsq_done, xrt_done, xs_done = sem("x_squares_done"), sem("x_root_done"), sem("x_scaled")
    xt_psum, xt_copied = sem("x_transposed"), sem("x_transposes_copied")
    hacc_done, hcol_psum, ht_done = sem("head_sum_done"), sem("head_columns_ready"), sem("h_ready")
    arow_used, abias_used, acc_done = sem("ada_rows_used"), sem("ada_bias_used"), sem("ada_sum_done")
    mod_psum, mod_copied = sem("mod_ready"), sem("mod_copied")
    hi_done, lo_done, part_used, ch_copied = (sem(n) for n in (
        "high_part_done", "low_part_done", "parts_used", "chunk_copied"))
    hh_done, hl_done, ml_done = sem("h_high_done"), sem("h_low_done"), sem("mix_low_done")
    cc_done, late_used, late_psum, late_row, sc2_psum, sc2_copied = (sem(n) for n in (
        "sc2_factors_done", "sc2_rows_used", "sc2_summed", "sc2_row_copied", "sc2_spread", "sc2_copied"))
    gc_done, g_used, g_psum, g_row, g2_psum, g2_copied, g2_done = (sem(n) for n in (
        "g2_factors_done", "g2_rows_used", "g2_summed", "g2_row_copied", "g2_spread", "g2_copied", "g2_done"))
    fg_psum, fg_abs, fg_exp, fg_ln, fg_done = (sem(n) for n in (
        "forget_ready", "forget_abs", "forget_exp", "forget_ln", "forget_done"))
    gate_exp, gnw_used = sem("gate_exp"), sem("gnw_used")
    qk_sq, qk_rt, rope_done, qk_norm = sem("qk_squares"), sem("qk_root"), sem("rope_done"), sem("qk_normed")
    tq_psum, tq_act, tq_dve = sem("qk_transposed"), sem("qk_copied_scalar"), sem("qk_copied_vector")
    fqb_done, fkb_done = sem("query_bias_done"), sem("key_bias_done")
    sc_psum, st_done, lmax_done, exp_done = (sem(n) for n in (
        "scores_ready", "decayed", "max_done", "exp_done"))
    pt_psum, pt_copied, o_psum, o_copied, o_scaled = (sem(n) for n in (
        "probs_transposed", "probs_copied", "heads_out_ready", "ret_out_copied", "fox_out_scaled"))
    bn_done, bn_rt, fsq_done, fo_rt, mix_ret, mix_fox = (sem(n) for n in (
        "bn_done", "bn_root", "fox_squares_done", "fox_root", "ret_mixed", "fox_mixed"))
    mt_psum, mt_copied = sem("mix_transposed"), sem("mix_high_done")
    y_sq, y_rt, nw_used, yg_done, yg_read = (sem(n) for n in ("y_squares", "y_root", "normw_used", "yg_done", "yg_read"))
    x1_done, x1_sq, x1_rt, h2_done = sem("x1_done"), sem("x1_squares"), sem("x1_root"), sem("h2_done")
    h2t_psum, h2t_copied, h2t_dve, lg_psum = sem("h2_transposed"), sem("h2t_copied_scalar"), sem("h2t_copied_vector"), sem("logits_ready")
    cmax_done, cexp_done, fdif_done, fexp_done, mk_done, rank_psum, count_done = (sem(n) for n in (
        "coarse_max", "coarse_exp", "fine_difference", "fine_exp", "mask_done", "ranks_ready", "count_done"))
    selg_done, selc_done = sem("gather_matrix_done"), sem("weight_matrix_done")
    xg_psum, xg_copied, ct_psum, ct_copied = (sem(n) for n in (
        "gathered", "gathered_copied", "weights_transposed", "weights_copied"))
    silu_done, hid_done, hid_seen, hidt_psum, hidt_copied = (sem(n) for n in (
        "silu_done", "hidden_done", "hidden_seen", "hidden_transposed", "hidden_copied"))
    ye_act, ye_dve, er_used = (sem(n) for n in (
        "result_copied_scalar", "result_copied_vector", "expert_unit_used"))
    add_psum, added = sem("addend_ready"), sem("added")
    sum_done, y2_sq, y2_rt, res_done = sem("sum_done"), sem("y2_squares"), sem("y2_root"), sem("out_ready")

    units = [("ret", h, 0) for h in range(H)] + [("fox", h, t) for h in range(H) for t in range(TT)]
    NU = len(units)

    def before(kind, k):
        return sum(u[0] == kind for u in units[:max(k, 0)])

    block = ctx.enter_context(nc.Block())

    @block.sync
    def _(sp):
        sp.dma_start(CV, a["c"].rearrange("b (p j) -> (b p) j", j=KC)).then_inc(c_in, 16)
        sp.dma_start(TAB, table).then_inc(tab_in, 16)

        for v in range(2):
            for u in range(4 if v == 0 else 0):
                sp.dma_start(HRING[:, u, :], ada_v[:, u, 0:D]).then_inc(hring_in[u], 16)
            with sp.Fori(1 - v, 4) as i:
                for u in range(4):
                    sp.wait_ge(hrow_used, 4 * i + (16 * v - 3) + u)
                    sp.dma_start(HRING[:, u, :], ada_v[:, bass.ds(4 * i + u, 1), v * D:(v + 1) * D]).then_inc(hring_in[u], 16)

        def win(chunk, u, first=False):
            if not first:
                sp.wait_ge(lo_done, 8 * chunk + (2 * u - 2))
            sp.dma_start(WR[:, u % 2], win_v[:, 4 * u:4 * u + 4, bass.ds(chunk * CH, CH)]).then_inc(wr_in[u % 2], 16)

        def ada(ps, k, first=False):
            if not first:
                sp.wait_ge(arow_used, 4 * ps + (k - 1))
            sp.dma_start(ARING[:, k % 2], ada_v[:, 4 * k:4 * k + 4, bass.ds(ps * CH + 2 * D, CH)]).then_inc(aring_in[k % 2], 16)

        def abias(ps):
            sp.wait_ge(abias_used, ps)
            sp.dma_start(ABIAS[0:1, :], a["ada_b"][:, bass.ds(ps * CH + 2 * D, CH)]).then_inc(abias_in, 16)

        for u in range(2):
            win(0, u, first=True)
        for k in range(4):
            ada(0, k, first=(k < 2))
        def iteration(it, first):
            for k in range(8):
                if not (first and k < 2):
                    win(2 * it + k // 4, k % 4)
                if k == 0:
                    abias(it + 1)
                if k % 2 == 1:
                    ada(it + 1, k // 2)

        iteration(0, True)
        with sp.Fori(1, 7) as it:
            iteration(it, False)

        def wout(n):
            sp.wait_ge(lo_done, 2 * (56 + n) - 2)
            sp.dma_start(WR[:, n % 2], wout_v[:, 4 * (n % 4):4 * (n % 4) + 4, (n // 4) * CH:(n // 4 + 1) * CH]).then_inc(wr_in[n % 2], 16)

        wout(0)
        wout(1)
        sp.wait_ge(arow_used, 32)
        sp.wait_ge(fg_psum, 1)
        sp.dma_start(CBIAS[0:P:32, :], a["ada_b"][:, 4 * D:5 * D].rearrange("a (g n) -> (a g) n", g=4)).then_inc(cbias_in, 16)
        for j in range(KC):
            if j >= 2:
                sp.wait_ge(late_used, j - 1)
            sp.dma_start(CRING[:, j % 2, :], ada_v[:, j, 4 * D:5 * D]).then_inc(crow_in[j % 2], 16)

        def expert(e, u, halves=(0, 1)):
            if u < 4:
                w13 = ER[:, u].rearrange("p (w j n) -> p w j n", w=2, j=4)
                for w in halves:
                    src = (w1_v, w3_v)[w]
                    sp.dma_start(w13[:, w], src[:, bass.ds(e, 1), 4 * u:4 * u + 4, :].rearrange("p e j n -> p (e j) n")).then_inc(er_in[u], 16)
            else:
                sp.dma_start(ER[:, u].rearrange("p (q n) -> p q n", q=2),
                             w2_v[:, bass.ds(e, 1), 2 * u - 8:2 * u - 6, :].rearrange("p e q n -> p (e q) n")).then_inc(er_in[u], 16)

        sp.wait_ge(mt_psum, 8)
        for n in range(2, 16):
            wout(n)
            if 4 <= n < 12:
                expert(0, (n - 4) // 2, (n % 2,))
        sp.wait_ge(part_used, 8 * 18)
        sp.wait_ge(x1_done, 2)
        sp.dma_start(GBIAS[0:P:32, :], a["ada_b"][:, 5 * D:6 * D].rearrange("a (g n) -> (a g) n", g=4)).then_inc(gbias_in, 16)
        for j in range(KC):
            if j >= 2:
                sp.wait_ge(g_used, j - 1)
            sp.dma_start(GRING[:, j % 2, :], ada_v[:, j, 5 * D:6 * D]).then_inc(grow_in[j % 2], 16)
        expert(0, 4)
        expert(0, 5)
        sp.wait_ge(h2_done, 2)
        sp.dma_start(NW2, across(a["norm_post_ffn"])).then_inc(nw2_in, 16)

        def expert_loop(e, v):
            for u in range(6):
                sp.wait_ge(er_used, 6 * v + (u - 5))
                expert(e, u)

        with sp.Fori(1, NE) as e:
            expert_loop(e, e)
        sp.wait_ge(count_done, 1)
        most = sp.value_load(icount[0:1, 0:1], min_val=0, max_val=S)
        with sp.If(most > SLOTS):
            with sp.Fori(1, ROUNDS) as r:
                with sp.Fori(0, NE) as e:
                    expert_loop(e, NE * r + e)
        for tt in range(TT):
            for half in range(2):
                c = slice(half * HW, (half + 1) * HW)
                sp.wait_ge(res_done, 2 * tt + half + 1)
                sp.dma_start(out_v[:, tt, c], X[:, tt, c]).then_inc(out_done, 16)
        sp.wait_ge(out_done, 64)

    @block.scalar
    def _(act):
        st = Steps(act, s_step)
        for tt in range(TT):
            act.dma_start(X[:, tt, :], x_v[:, tt, :]).then_inc(x_in, 16)
        act.dma_start(NPRE, a["norm_pre_mix"].rearrange("l (p j) -> (l p) j", j=KC)).then_inc(small_in, 16)
        act.dma_start(QKN[:, 0:1], col(a["fox_qn_w"])).then_inc(small_in, 16)
        act.dma_start(QKN[:, 1:2], col(a["fox_kn_w"])).then_inc(small_in, 16)
        for r in range(2):
            act.dma_start(FBIAS[r * H:(r + 1) * H, :], col(a["fox_f_bias"])).then_inc(small_in, 16)
        act.dma_start(RWS[:, :, 0:NG], a["router_coarse_w"][0].rearrange("(p j) n -> p j n", j=KC)).then_inc(small_in, 16)
        act.dma_start(RWS[:, :, NG:36], a["router_fine_w"][0].rearrange("(p j) n -> p j n", j=KC)).then_inc(small_in, 16)
        act.dma_start(RBS[:, 0:NG], across(a["router_coarse_b"])).then_inc(small_in, 16)
        act.dma_start(RBS[:, NG:36], across(a["router_fine_b"])).then_inc(small_in, 16)
        for r in range(2):
            act.dma_start(WF[:, :, r * H:(r + 1) * H], win_v[:, :, NT * HW:NT * HW + H]).then_inc(fgate_in, 16)
        act.dma_start(GNW, across(a["ret_gn_w"])).then_inc(gnw_in, 16)
        act.wait_ge(zeroed, 1)
        act.dma_start(HACC[0:1, 0, :], a["ada_b"][:, 0:D]).then_inc(hbias_in, 16)
        act.dma_start(HACC[0:1, 1, :], a["ada_b"][:, D:2 * D]).then_inc(hbias_in, 16)
        act.dma_start(ABIAS[0:1, :], a["ada_b"][:, 2 * D:2 * D + CH]).then_inc(abias_in, 16)
        act.wait_ge(c_in, 16)
        act.activation(CE, CV, ACT.Exp, scale=-1.0).then_inc(ce_done, 1)
        act.wait_ge(x_in, 32)
        for tt in range(TT):
            act.activation(XS[:, tt, :], X[:, tt, :], ACT.Square, accum_out=SS[:, tt:tt + 1]).then_inc(xsq_done, 1)
        act.wait_ge(zeroed, 2)
        act.wait_ge(xsq_done, 2)
        act.activation(RS[:, 0:2], SS[:, 0:2], ACT.Sqrt, scale=1.0 / D, bias=EPSC).then_inc(xrt_done, 1)
        for g in range(8):
            act.wait_ge(xt_psum, g + 1)
            act.activation(HT[:, 2 * g:2 * g + 2, :], bank[:, g % 4, :], ACT.Copy).then_inc(xt_copied, 1)

        for j in range(KC):
            act.wait_ge(ht_done, j + 1)
            act.activation(HH[:, j, :], HT[:, j, :], ACT.Copy).then_inc(hh_done, 1)

        def high(n, gq):
            if not (isinstance(n, int) and n < 4):
                act.wait_ge(part_used, n - 3)
            if gq % 2 == 0:
                act.wait_ge(wr_in[gq // 2 % 2], (2 * n - 2 * gq) * 2 + (16 * (gq // 4) + 16))
            src = WR[:, gq // 2 % 2, 2 * (gq % 2):2 * (gq % 2) + 2, :]
            act.activation(WH[:, gq % 4], src, ACT.Copy).then_inc(hi_done, 1)

        def chunk_copy(c):
            b = c[1]
            act.wait_ge(part_used, 8 * c[0] + 8)
            act.activation(RAW[:, :, bass.ds(c[0] * CH, CH)], bank[:, 2 * b:2 * b + 2, :], ACT.Copy).then_inc(ch_copied, 1)

        def forget():
            act.wait_ge(fg_abs, 1)
            act.activation(SCR[0:16, 0, S:2 * S], SCR[0:16, 0, 0:S], ACT.Exp, scale=-1.0).then_inc(fg_exp, 1)
            act.wait_ge(fg_exp, 1)
            act.activation(SCR[0:16, 0, 2 * S:3 * S], SCR[0:16, 0, S:2 * S], ACT.Ln, bias=1.0).then_inc(fg_ln, 1)

        def iteration(it, last_gates=False):
            for b in range(2):
                for gq in range(8):
                    high(16 * it + (8 * b + gq), gq)
                    if last_gates and b == 1 and gq == 5:
                        act.wait_ge(fg_done, 1)
                        act.wait_ge(rope_done, 2)
                        act.wait_ge(ch_copied, 8)
                        act.activation(SCR, GATE, ACT.Exp, scale=-1.0).then_inc(gate_exp, 1)
                    if gq == 3:
                        chunk_copy((2 * it + (b - 1), 1 - b))
                    if gq == 1 and b == 1:
                        if isinstance(it, int) and it == 6:
                            act.wait_ge(gnw_used, 1)
                        act.wait_ge(mod_psum, it + 1)
                        act.activation(MOD[:, bass.ds(it * CH, CH)], bank[:, 4, :], ACT.Copy).then_inc(mod_copied, 1)

        for b, gq in [(b, gq) for b in range(2) for gq in range(8)]:
            high(8 * b + gq, gq)
            if b == 0 and gq == 7:
                forget()
            if b == 1 and gq == 3:
                chunk_copy((0, 0))
                act.wait_ge(mod_psum, 1)
                act.activation(MOD[:, 0:CH], bank[:, 4, :], ACT.Copy).then_inc(mod_copied, 1)
        with act.Fori(1, 4) as it:
            iteration(it)
        iteration(4, last_gates=True)
        iteration(5)
        iteration(6)
        chunk_copy((13, 1))
        for gq in range(4):
            high(112 + gq, gq)
        act.wait_ge(qk_sq, 1)
        act.activation(RS[:, 0:32], SS[:, 0:32], ACT.Sqrt, scale=1.0 / DH, bias=EPSC).then_inc(qk_rt, 1)
        act.wait_ge(qk_rt, 1)
        act.dma_start(DEC, decay_table.rearrange("p (h s) -> p h s", h=H)).then_inc(dec_in, 16)
        act.wait_ge(mod_psum, 8)
        act.activation(MOD[:, 7 * CH:8 * CH], bank[:, 4, :], ACT.Copy).then_inc(mod_copied, 1)
        for g in range(0, 16, 2):
            act.wait_ge(tq_psum, g + 1)
            t4, hp = g // 4, g % 4
            dst = QKT[:, t4, 2 * hp:2 * hp + 2, :]
            if t4 < 2:
                act.activation(dst, bank[:, g % 4, :], ACT.Copy).then_inc(tq_act, 1)
            else:
                act.activation(dst, bank[:, g % 4, :], ACT.Copy, scale=QKN[:, t4 - 2:t4 - 1]).then_inc(tq_act, 1)
        act.wait_ge(tq_psum, 16)
        act.dma_start(ONW, across(a["fox_on_w"])).then_inc(onw_in, 16)

        def out_copy(k):
            kind, h, t = units[k]
            if kind == "ret":
                act.wait_ge(o_psum, k + 1)
                act.activation(MIX[:, :, h * DH:(h + 1) * DH], bank[:, 6 + k % 2, 0:2 * P], ACT.Copy).then_inc(o_copied, 1)
            else:
                act.wait_ge(o_scaled, before("fox", k) + 1)
                n = before("fox", k)
                if n:
                    act.wait_ge(fsq_done, n)
                act.activation(CSQ, MIX[:, t, HW + h * DH:HW + (h + 1) * DH], ACT.Square,
                               accum_out=CST[:, 4 + t, h:h + 1]).then_inc(fsq_done, 1)

        for k in range(NU + 2):
            if k < NU and units[k][0] == "fox":
                n = before("fox", k)
                act.wait_ge(lmax_done, n + 1)
                w = P * (units[k][2] + 1)
                act.activation(PR[:, k % 2, 0:w], PR[:, k % 2, 0:w], ACT.Exp, bias=CST[:, 0 + units[k][2], units[k][1]:units[k][1] + 1],
                               accum_out=CST[:, 2 + units[k][2], units[k][1]:units[k][1] + 1]).then_inc(exp_done, 1)
            if k == NU - 6:
                act.wait_ge(bn_done, 1)
                act.activation(CST[:, 6:8, 0:8], BAG[:, :, 1].rearrange("p (t h) -> p t h", t=TT), ACT.Sqrt, bias=EPSC).then_inc(bn_rt, 1)
            if k >= 3:
                out_copy(k - 3)
        out_copy(NU - 1)
        act.wait_ge(fsq_done, 16)
        act.activation(CST[:, 8:10, 0:8], CST[:, 4:6, 0:8], ACT.Sqrt, scale=1.0 / DH, bias=EPSC).then_inc(fo_rt, 1)
        act.wait_ge(late_psum, 1)
        act.activation(CROW, bank[:, 0, :], ACT.Copy).then_inc(late_row, 1)
        act.wait_ge(sc2_psum, 1)
        act.activation(SC2B, bank[:, 0:4, :], ACT.Copy).then_inc(sc2_copied, 1)
        for g in range(8):
            act.wait_ge(mt_psum, g + 1)
            act.activation(MH[:, 2 * g:2 * g + 2, :], bank[:, (g + 4) % 8, :], ACT.Copy).then_inc(mt_copied, 1)

        act.wait_ge(st_done, 8)
        for n, name in enumerate(("norm_post_mix", "norm_pre_ffn")):
            if n:
                act.wait_ge(nw_used, n)
            act.dma_start(NW, across(a[name])).then_inc(nw_in, 16)

        def squares(cc):
            act.wait_ge(part_used, 8 * (14 + cc) + 8)
            for tt in range(TT):
                act.wait_ge(nw_used, 2)
                if 2 * cc + tt:
                    act.wait_ge(y_sq, 2 * cc + tt)
                act.activation(NW[:, 0:CH], bank[:, 2 * cc + tt, :], ACT.Square,
                               accum_out=SS[:, 4 * tt + cc:4 * tt + cc + 1]).then_inc(y_sq, 1)

        for n in range(4, 32):
            high(112 + n, n % 8)
            if n % 8 == 3:
                squares(n // 8 - 1)
        squares(3)
        act.wait_ge(yg_done, 1)
        act.activation(RS[:, 0:2], RS[:, 2:4], ACT.Sqrt, scale=1.0 / D, bias=EPSC).then_inc(y_rt, 1)
        for tt in range(TT):
            act.wait_ge(x1_done, tt + 1)
            if tt:
                act.wait_ge(x1_sq, tt)
            act.activation(NW, X[:, tt, :], ACT.Square, accum_out=RS[:, 4 + tt:5 + tt]).then_inc(x1_sq, 1)
            act.wait_ge(x1_sq, tt + 1)
            act.activation(RS[:, 6 + tt:7 + tt], RS[:, 4 + tt:5 + tt], ACT.Sqrt, scale=1.0 / D, bias=EPSC).then_inc(x1_rt, 1)
        for g in range(0, 8, 2):
            act.wait_ge(h2t_psum, g + 1)
            act.activation(H2T[:, 2 * g:2 * g + 2, :], bank[:, g % 4, :], ACT.Copy).then_inc(h2t_copied, 1)
        act.wait_ge(h2t_psum, 8)
        for tt in range(TT):
            act.wait_ge(cmax_done, tt + 1)
            act.activation(JUNK[:, 0:4], LG[:, tt, 0:NG], ACT.Exp, bias=RC[:, tt, 0:1], accum_out=RC[:, tt, 1:2]).then_inc(cexp_done, 1)
            act.wait_ge(cexp_done, tt + 1)
            act.wait_ge(fdif_done, tt + 1)
            act.activation(RC[:, tt, 4:5], RC[:, tt, 3:4], ACT.Exp).then_inc(fexp_done, 1)

        def gathered(n, g4):
            act.wait_ge(xg_psum, n)
            act.activation(XT[:, 4 * g4:4 * g4 + 4, :], bank[:, g4 % 2, :], ACT.Copy).then_inc(xg_copied, 1)

        def scalar_expert(g, b, v):
            act.wait_ge(er_used, 6 * v + 4)
            act.activation(SG[SLOTS:P, :], bank[0:SLOTS, 2, :], ACT.Silu).then_inc(silu_done, 1)
            if b == 1:
                for g4 in range(4):
                    gathered(4 * g + (5 + g4), g4)
                act.wait_ge(ct_psum, g + 1)
                act.activation(SELT, bank[:, 3, 0:S], ACT.Copy).then_inc(ct_copied, 1)
            act.wait_ge(hidt_psum, v + 1)
            act.activation(HIDT, bank[:, 3, 0:FQ * SLOTS], ACT.Copy).then_inc(hidt_copied, 1)
            act.wait_ge(er_used, 6 * v + 6)
            if b == 0:
                act.wait_ge(add_psum, 8 * g + 8)
            act.activation(YS[SLOTS * b:SLOTS * b + SLOTS, 0:2 * CH], bank[0:SLOTS, 4:6, :], ACT.Copy).then_inc(ye_act, 1)

        def scalar_pair(g):
            for b in range(2):
                scalar_expert(g, b, 2 * g + b)

        def scalar_end():
            act.activation(JUNK[:, 7:8], EPSC, ACT.Sqrt)
            for tt in range(TT):
                act.wait_ge(sum_done, tt + 1)
                act.activation(XT.rearrange("p j s -> p (j s)"), YACC[:, tt, :], ACT.Square, accum_out=RS[:, 8 + tt:9 + tt]).then_inc(y2_sq, 1)
                act.wait_ge(y2_sq, 1 + tt)
                act.activation(RS[:, 10 + tt:11 + tt], RS[:, 8 + tt:9 + tt], ACT.Sqrt, scale=1.0 / D, bias=EPSC).then_inc(y2_rt, 1)

        act.wait_ge(g_psum, 1)
        act.activation(GROW, bank[:, 5, :], ACT.Copy).then_inc(g_row, 1)
        act.wait_ge(g2_psum, 1)
        act.activation(G2B[:, 0:2 * CH], bank[:, 2:4, :], ACT.Copy).then_inc(g2_copied, 1)
        act.activation(G2B[:, 2 * CH:4 * CH], bank[:, 6:8, :], ACT.Copy).then_inc(g2_copied, 1)
        act.activation(JUNK[:, 6:7], EPSC, ACT.Copy).then_inc(ye_act, 1)
        for g4 in range(4):
            gathered(g4 + 1, g4)
        with act.Fori(0, NP) as g:
            scalar_pair(g)
        act.wait_ge(count_done, 1)
        most = act.value_load(icount[0:1, 0:1], min_val=0, max_val=S)
        with act.If(most > SLOTS):
            with act.Fori(NP, ROUNDS * NP) as g:
                scalar_pair(g)
        scalar_end()

    @block.tensor
    def _(pe):
        def mm(o, l, r, start=True, stop=True):
            return pe.matmul(o, l, r, start=start, stop=stop, skip_group_check=True)

        pe.wait_ge(tab_in, 16)
        pe.wait_ge(xs_done, 2)
        for g in range(8):
            if g >= 4:
                pe.wait_ge(xt_copied, g - 3)
            for jj in range(2):
                for tt in range(TT):
                    j = 2 * g + jj
                    last = pe.transpose(bank[:, g % 4, (2 * jj + tt) * P:(2 * jj + tt + 1) * P],
                                        XS[:, tt, :].rearrange("p (q j) -> p j q", j=KC)[:, j, :], IDENT)
            last.then_inc(xt_psum, 1)
        for v in range(2):
            pe.wait_ge(hacc_done, v + 1)
            for j in range(KC):
                last = mm(bank[:, 6 + v, j:j + 1], HACC[:, v, :].rearrange("p (q j) -> p j q", j=KC)[:, j, :], ONES[:, 0:1])
            last.then_inc(hcol_psum, 1)
        pe.wait_ge(fgate_in, 32)
        for j in range(KC):
            pe.wait_ge(ht_done, j + 1)
            mm(bank[0:16, 6, 0:S], WF[:, j, :], HT[:, j, :], start=(j == 0), stop=(j == KC - 1)).then_inc(fg_psum, 1)

        def granule(n, gq, left, b0, first):
            pe.wait_ge(lo_done, n + 1)
            lh, ll = left
            for jj in range(2):
                k = 2 * gq + jj
                if first:
                    pe.wait_ge(hl_done, k + 1)
                for tt in range(TT):
                    o, tok = bank[:, b0 + tt, :], slice(tt * P, (tt + 1) * P)
                    mm(o, lh[:, k, tok], WH[:, gq % 4, jj, :], start=(k == 0), stop=False)
                    mm(o, lh[:, k, tok], WL[:, gq % 4, jj, :], start=False, stop=False)
                    last = mm(o, ll[:, k, tok], WH[:, gq % 4, jj, :], start=False, stop=(k == KC - 1))
            last.then_inc(part_used, 1)

        def project(it, b, first=False):
            if not first:
                pe.wait_ge(ch_copied, 2 * it + (b - 1))
            for gq in range(8):
                granule(16 * it + (8 * b + gq), gq, (HH, HL), 2 * b, first and b == 0)
                if b == 0 and gq == (7 if first else 3):
                    spread(it, first)

        def spread(ps, first=False):
            pe.wait_ge(acc_done, ps + 1)
            if not first:
                pe.wait_ge(mod_copied, ps)
            mm(bank[:, 4, :], ONES, AACC).then_inc(mod_psum, 1)

        for b in range(2):
            project(0, b, True)
        with pe.Fori(1, 7) as it:
            for b in range(2):
                project(it, b)
        spread(7)
        pe.wait_ge(rope_done, 2)
        pe.wait_ge(ch_copied, 14)
        for g in range(16):
            t4, hp = g // 4, g % 4
            if g >= 4:
                if g % 2 == 0:
                    pe.wait_ge(tq_act, (g - 4) // 2 + 1)
                else:
                    pe.wait_ge(tq_dve, (g - 5) // 2 + 1)
            if g == 8:
                pe.wait_ge(qk_norm, 1)
            for hh in range(2):
                for tt in range(TT):
                    o = (0, 1, 4, 5)[t4] * HW + (2 * hp + hh) * DH
                    last = pe.transpose(bank[:, g % 4, (2 * hh + tt) * P:(2 * hh + tt + 1) * P], RAW[:, tt, o:o + DH], IDENT)
            last.then_inc(tq_psum, 1)
        pe.wait_ge(tq_act, 8)
        pe.wait_ge(tq_dve, 8)
        pe.wait_ge(mod_copied, 8)

        def scores(k):
            kind, h, t = units[k]
            sb = bank[:, 4 + k % 2, :]
            if k >= 2:
                pe.wait_ge(st_done if units[k - 2][0] == "ret" else lmax_done, before(units[k - 2][0], k - 1))
            if kind == "ret":
                mm(sb[:, 0:S], QKT[:, 1, h, 0:P], QKT[:, 0, h, :])
                mm(sb[:, S:S + P], QKT[:, 1, h, P:S], QKT[:, 0, h, P:S]).then_inc(sc_psum, 1)
            else:
                w = P * (t + 1)
                pe.wait_ge(fkb_done, h + 1)
                if h == 0:
                    pe.wait_ge(fqb_done, 1)
                mm(sb[:, 0:w], QKT[:, 2, h, t * P:(t + 1) * P], QKT[:, 3, h, 0:w], stop=False)
                mm(sb[:, 0:w], FQB[:, t * P:(t + 1) * P], FKB[0:2 * H, h % 2, 0:w], start=False).then_inc(sc_psum, 1)

        def turn(k):
            kind, h, t = units[k]
            if kind == "fox":
                n = before("fox", k)
                pe.wait_ge(exp_done, n + 1)
                if n >= 2:
                    pe.wait_ge(pt_copied, n - 1)
                for sblk in range(t + 1):
                    last = pe.transpose(bank[:, 2 + k % 2, sblk * P:(sblk + 1) * P], PR[:, k % 2, sblk * P:(sblk + 1) * P], IDENT)
                last.then_inc(pt_psum, 1)

        def values(k):
            kind, h, t = units[k]
            ob = bank[:, 6 + k % 2, :]
            if k >= 2:
                pe.wait_ge(o_copied if units[k - 2][0] == "ret" else o_scaled, before(units[k - 2][0], k - 1))
            if kind == "ret":
                pe.wait_ge(st_done, before("ret", k) + 1)
                v = VRET[:, :, h * DH:(h + 1) * DH]
                mm(ob[:, 0:P], ST[:, k % 2, 0:P], v[:, 0, :])
                mm(ob[:, P:S], ST[:, k % 2, P:S], v[:, 0, :], stop=False)
                mm(ob[:, P:S], ST[:, k % 2, S:S + P], v[:, 1, :], start=False).then_inc(o_psum, 1)
            else:
                n = before("fox", k)
                pe.wait_ge(pt_copied, n + 1)
                for sblk in range(t + 1):
                    last = mm(ob[:, 0:P], PRT[:, k % 2, sblk * P:(sblk + 1) * P], VFOX[:, sblk, h * DH:(h + 1) * DH],
                              start=(sblk == 0), stop=(sblk == t))
                last.then_inc(o_psum, 1)

        def late_rows(j, ring, ready, factors, used, b):
            pe.wait_ge(ready[j % 2], 16 * (j // 2) + 16)
            for g in range(4):
                last = mm(bank[32 * g:32 * g + 32, b, :], factors[:, j, :], ring[:, j % 2, g * CH:(g + 1) * CH], start=(j == 0), stop=False)
            last.then_inc(used, 1)

        def late_bias(bias, b, summed):
            for g in range(4):
                q = slice(32 * g, 32 * g + 1)
                last = mm(bank[32 * g:32 * g + 32, b, :], ONES[q, 0:32], bias[q, :], start=False)
            last.then_inc(summed, 1)

        def late_spread(row, banks, done):
            for g in range(4):
                q = slice(32 * g, 32 * g + 1)
                last = mm(bank[:, banks[g], :], ONES[q, :], row[q, :])
            last.then_inc(done, 1)

        pe.wait_ge(cc_done, 1)
        for k in range(NU + 2):
            if k < NU:
                scores(k)
            if 1 <= k <= NU:
                turn(k - 1)
            if k >= 2:
                values(k - 2)
            if 3 <= k < 3 + KC:
                late_rows(k - 3, CRING, crow_in, CC, late_used, 0)
            if k == 3 + KC:
                pe.wait_ge(cbias_in, 16)
                late_bias(CBIAS, 0, late_psum)
        pe.wait_ge(late_row, 1)
        pe.wait_ge(pt_copied, 16)
        late_spread(CROW, (0, 1, 2, 3), sc2_psum)
        for g in range(8):
            if g == 0:
                pe.wait_ge(mix_ret, 1)
                pe.wait_ge(o_scaled, 16)
                pe.wait_ge(pt_copied, 16)
            if g == 4:
                pe.wait_ge(mix_fox, 1)
                pe.wait_ge(sc2_copied, 1)
            for jj in range(2):
                for tt in range(TT):
                    last = pe.transpose(bank[:, (g + 4) % 8, (2 * jj + tt) * P:(2 * jj + tt + 1) * P],
                                        MIX[:, tt, (2 * g + jj) * P:(2 * g + jj + 1) * P], IDENT)
            last.then_inc(mt_psum, 1)
        pe.wait_ge(mt_copied, 8)
        pe.wait_ge(ml_done, 8)
        for cc in range(4):
            for gq in range(8):
                granule(8 * (14 + cc) + gq, gq, (MH, ML), 2 * cc, False)
        pe.wait_ge(yg_read, 2)
        pe.wait_ge(gc_done, 1)

        def g2_rows(j0, j1):
            for j in range(j0, j1):
                late_rows(j, GRING, grow_in, GC, g_used, 5)

        g2_rows(0, 4)
        for g in range(8):
            if g == 0:
                pe.wait_ge(h2_done, 2)
            if g >= 4:
                if g % 2 == 0:
                    pe.wait_ge(h2t_copied, (g - 4) // 2 + 1)
                else:
                    pe.wait_ge(h2t_dve, (g - 5) // 2 + 1)
            for jj in range(2):
                for tt in range(TT):
                    last = pe.transpose(bank[:, g % 4, (2 * jj + tt) * P:(2 * jj + tt + 1) * P], H2[:, tt, 2 * g + jj, :], IDENT)
            last.then_inc(h2t_psum, 1)
        g2_rows(4, 8)
        pe.wait_ge(h2t_copied, 4)
        pe.wait_ge(h2t_dve, 4)
        for tt in range(TT):
            for j in range(KC):
                last = mm(bank[:, 6 + tt, 0:36], H2T[:, j, tt * P:(tt + 1) * P], RWS[:, j, :], start=(j == 0), stop=(j == KC - 1))
            last.then_inc(lg_psum, 1)
        g2_rows(8, 14)
        pe.wait_ge(mk_done, 2)
        mm(bank[:, 4, 0:NE], TRI, MK[:, 0, :])
        mm(bank[:, 4, NE:2 * NE], TRI, MK[:, 1, :], stop=False)
        mm(bank[:, 4, NE:2 * NE], ONES, MK[:, 0, :], start=False)
        mm(bank[:, 4, 2 * NE:3 * NE], ONES, MK[:, 0, :], stop=False)
        mm(bank[:, 4, 2 * NE:3 * NE], ONES, MK[:, 1, :], start=False).then_inc(rank_psum, 1)

        def gather(n, first):
            pe.wait_ge(selg_done, n + 1)
            for g4 in range(4):
                if not first:
                    pe.wait_ge(xg_copied, 4 * n + (g4 - 1))
                elif g4 >= 2:
                    pe.wait_ge(xg_copied, g4 - 1)
                for j in range(4):
                    for tt in range(TT):
                        last = mm(bank[:, g4 % 2, j * P:(j + 1) * P], H2[:, tt, 4 * g4 + j, :], SELG[:, tt, :], start=(tt == 0), stop=(tt == 1))
                last.then_inc(xg_psum, 1)

        def weights_turned(g):
            pe.wait_ge(selc_done, g + 1)
            for tt in range(TT):
                last = pe.transpose(bank[:, 3, tt * P:(tt + 1) * P], SELC[:, tt, :], IDENT)
            last.then_inc(ct_psum, 1)

        def add_back(g):
            pe.wait_ge(ye_act, 2 * g + 1)
            pe.wait_ge(ye_dve, 2 * g + 1)
            pe.wait_ge(ct_copied, g + 1)
            for n in range(8):
                tt, cc = n // 4, n % 4
                pe.wait_ge(added, 8 * g + (n + 1))
                mm(bank[:, 6 + n % 2, :], SELT[:, tt * P:(tt + 1) * P], YS[:, cc * CH:(cc + 1) * CH]).then_inc(add_psum, 1)

        def expert(g, b):
            v = 2 * g + b
            for u in range(4):
                w13 = ER[:, u].rearrange("p (w j n) -> p w j n", w=2, j=4)
                if b == 0:
                    pe.wait_ge(xg_copied, 4 * g + (u + 1))
                pe.wait_ge(er_in[u], 32 * v + 32)
                for j in range(4):
                    for w in range(2):
                        k = 4 * u + j
                        last = mm(bank[SLOTS * w:SLOTS * w + SLOTS, 2, :], XT[:, k, SLOTS * b:SLOTS * b + SLOTS], w13[:, w, j, :],
                                  start=(k == 0), stop=(k == KC - 1))
                last.then_inc(er_used, 1)
            if b == 0:
                add_back(g)
            else:
                gather(g + 1, False)
                weights_turned(g)
                pe.wait_ge(ct_copied, g + 2)
            pe.wait_ge(hid_done, v + 1)
            pe.sem_inc(hid_seen, 1)
            for q in range(FQ):
                last = pe.transpose(bank[:, 3, q * SLOTS:(q + 1) * SLOTS],
                                    HID[SLOTS:P, :].rearrange("p (s q) -> p q s", q=FQ)[:, q, :], IDENT[SLOTS:P, SLOTS:P])
            last.then_inc(hidt_psum, 1)
            pe.wait_ge(hidt_copied, v + 1)
            pe.wait_ge(ye_act, v + 1)
            pe.wait_ge(ye_dve, v + 1)
            for q in range(FQ):
                u = 4 + q // 2
                w2t = ER[:, u].rearrange("p (q n) -> p q n", q=2)
                if q % 2 == 0:
                    pe.wait_ge(er_in[u], 16 * v + 16)
                for cc in range(2):
                    for w in range(2):
                        o = w * 2 * CH + cc * CH
                        last = mm(bank[SLOTS * w:SLOTS * w + SLOTS, 4 + cc, :], HIDT[:, q, :], w2t[:, q % 2, o:o + CH],
                                  start=(q == 0), stop=(q == FQ - 1))
                if q % 2 == 1:
                    last.then_inc(er_used, 1)

        g2_rows(14, KC)
        pe.wait_ge(gbias_in, 16)
        late_bias(GBIAS, 5, g_psum)
        pe.wait_ge(g_row, 1)
        late_spread(GROW, (2, 3, 6, 7), g2_psum)
        gather(0, True)
        with pe.Fori(0, NP) as g:
            for b in range(2):
                expert(g, b)
        pe.wait_ge(count_done, 1)
        most = pe.value_load(icount[0:1, 0:1], min_val=0, max_val=S)
        with pe.If(most > SLOTS):
            with pe.Fori(NP, ROUNDS * NP) as g:
                for b in range(2):
                    expert(g, b)
            add_back(ROUNDS * NP)
        with pe.Else():
            add_back(NP)

    @block.gpsimd
    def _(pool):
        def low(n, gq):
            pool.wait_ge(hi_done, n + 1)
            src = WR[:, gq // 2 % 2, 2 * (gq % 2):2 * (gq % 2) + 2, :]
            pool.tensor_tensor(WL[:, gq % 4], src, WH[:, gq % 4].bitcast(F32), ALU.subtract).then_inc(lo_done, 1)

        with pool.Fori(0, 18) as c:
            for gq in range(8):
                low(8 * c + gq, gq)

    @block.vector
    def _(dve):
        st = Steps(dve, v_step)
        tt_, ts_, stt = dve.tensor_tensor, dve.tensor_scalar, dve.scalar_tensor_tensor
        st.link(dve.memset(HACC, 0.0))
        dve.memset(ABIAS, 0.0).then_inc(zeroed, 1)
        dve.memset(EPSC, EPS).then_inc(zeroed, 1)
        dve.wait_ge(ce_done, 1)
        st.link(ts_(CE, CE, 1.0, None, ALU.add))
        st.link(dve.reciprocal(CE, CE))
        st.link(tt_(CA, CV, CE, ALU.mult))
        dve.wait_ge(hbias_in, 32)

        def head(v):
            with dve.Fori(0, 4) as i:
                for u in range(4):
                    dve.wait_ge(hring_in[u], 16 * i + (64 * v + 16))
                    stt(HACC[:, v, :], HRING[:, u, :], CA[:, bass.ds(4 * i + u, 1)], HACC[:, v, :], ALU.mult, ALU.add).then_inc(hrow_used, 1)
                    dve.wait_ge(hrow_used, 4 * i + (16 * v + u + 1))

        head(0)
        dve.sem_inc(hacc_done, 1)
        dve.wait_ge(xrt_done, 1)
        st.link(dve.reciprocal(RS[:, 0:2], RS[:, 0:2]))
        for tt in range(TT):
            ts_(XS[:, tt, :], X[:, tt, :], RS[:, tt:tt + 1], None, ALU.mult).then_inc(xs_done, 1)
        head(1)
        dve.sem_inc(hacc_done, 1)
        dve.wait_ge(hcol_psum, 2)
        dve.wait_ge(small_in, 16 * 9)
        st.link(stt(A1, bank[:, 7, 0:KC], 1.0, NPRE, ALU.add, ALU.mult))
        st.link(dve.tensor_copy(SH1, bank[:, 6, 0:KC]))
        dve.wait_ge(xt_copied, 8)
        for j in range(KC):
            ts_(HT[:, j, :], HT[:, j, :], A1[:, j:j + 1], SH1[:, j:j + 1], ALU.mult, ALU.add).then_inc(ht_done, 1)
        for j in range(KC):
            dve.wait_ge(hh_done, j + 1)
            dve.wait_ge(fg_psum, j + 1)
            tt_(HL[:, j, :], HT[:, j, :], HH[:, j, :].bitcast(F32), ALU.subtract).then_inc(hl_done, 1)

        def rows(ps, first=False):
            for k in range(4):
                dve.wait_ge(aring_in[k % 2], 32 * ps + (16 * (k // 2) + 16))
                for jj in range(4):
                    src = AACC
                    if k == 0 and jj == 0:
                        dve.wait_ge(abias_in, 16 * ps + 16)
                        if not first:
                            dve.wait_ge(mod_psum, ps)
                        src = ABIAS
                    ins = stt(AACC, ARING[:, k % 2, jj, :], CA[:, 4 * k + jj:4 * k + jj + 1], src, ALU.mult, ALU.add)
                    if jj < 3:
                        st.link(ins)
                        if k == 0 and jj == 0:
                            dve.sem_inc(abias_used, 1)
                    else:
                        ins.then_inc(arow_used, 1)
                        dve.wait_ge(arow_used, 4 * ps + (k + 1))
                        if k == 3:
                            dve.sem_inc(acc_done, 1)

        ROWS = 12

        def tensor_of(it, tt):
            return RAW[:, tt, bass.ds(it * HW, HW)].rearrange("p (h d) -> p h d", h=H)

        rows(0, True)
        z, az, lnv = SCR[0:16, 0, 3 * S:4 * S], SCR[0:16, 0, 0:S], SCR[0:16, 0, 2 * S:3 * S]
        one, mn = SCR[0:16, 1, 0:S], SCR[0:16, 1, S:2 * S]
        dve.wait_ge(fg_psum, KC)
        st.link(ts_(z, bank[0:16, 6, 0:S], FBIAS[0:16, :], None, ALU.add))
        st.link(ts_(mn, z, -1.0, None, ALU.mult))
        tt_(az, z, mn, ALU.max).then_inc(fg_abs, 1)
        dve.wait_ge(fg_abs, 1)
        st.link(ts_(mn, z, 0.0, None, ALU.min))
        st.link(dve.memset(one, 1.0))
        dve.wait_ge(fg_ln, 1)
        st.link(tt_(z, mn, lnv, ALU.subtract))
        dve.tensor_tensor_scan(FG[0:16, :], one, z, 0.0, ALU.mult, ALU.add).then_inc(fg_done, 1)
        dve.wait_ge(fg_done, 1)

        with dve.Fori(0, 2) as it, st.loop(it, ROWS + 12, 2):
            rows(it + 1)
            dve.wait_ge(ch_copied, 2 * it + 2)
            for tt in range(TT):
                x = tensor_of(it, tt)
                cos, sin = (TAB[:, o + tt * 64:o + tt * 64 + 64].unsqueeze(1).to_broadcast([P, H, 64]) for o in (T_COS, T_SIN))
                lo, hi = x[:, :, 0:64], x[:, :, 64:128]
                t1, t2 = (SCR[:, tt, i * CH:(i + 1) * CH].rearrange("p (h d) -> p h d", h=H) for i in range(2))
                st.link(tt_(t1, lo, sin, ALU.mult))
                st.link(tt_(t2, hi, sin, ALU.mult))
                st.link(tt_(lo, lo, cos, ALU.mult))
                st.link(tt_(hi, hi, cos, ALU.mult))
                st.link(tt_(lo, lo, t2, ALU.subtract))
                st.link(tt_(hi, hi, t1, ALU.add))
        dve.sem_inc(rope_done, 1)
        dve.sem_inc(rope_done, 1)
        with dve.Fori(2, 5) as it, st.loop(it - 2, ROWS, 3):
            rows(it + 1)
        dve.wait_ge(gate_exp, 1)
        dve.wait_ge(gnw_in, 16)
        st.link(ts_(SCR, SCR, 1.0, None, ALU.add))
        st.link(dve.reciprocal(SCR, SCR))
        st.link(tt_(GATE, GATE, SCR, ALU.mult))
        st.link(tt_(GATE, GATE, GNW.unsqueeze(1).to_broadcast([P, TT, HW]), ALU.mult))
        dve.sem_inc(gnw_used, 1)
        rows(6)
        rows(7)
        with dve.Fori(4, 6) as it, st.loop(it - 4, 4, 2):
            dve.wait_ge(ch_copied, 2 * it + 2)
            for tt in range(TT):
                x = tensor_of(it, tt)
                sq = SCR[:, tt, :].rearrange("p (h d) -> p h d", h=H)
                st.link(tt_(sq, x, x, ALU.mult))
                st.link(dve.tensor_reduce(SS[:, bass.ds((it - 4) * 16 + tt * H, H)], sq, AX_X, ALU.add))
        dve.sem_inc(qk_sq, 1)
        dve.wait_ge(qk_rt, 1)
        st.link(dve.reciprocal(RS, RS))
        for i in range(2):
            for tt in range(TT):
                x = RAW[:, tt, (4 + i) * HW:(5 + i) * HW].rearrange("p (h d) -> p h d", h=H)
                r = RS[:, i * 16 + tt * H:i * 16 + tt * H + H].unsqueeze(2).to_broadcast([P, H, DH])
                st.link(tt_(x, x, r, ALU.mult))
        st.link(ts_(QKN[:, 0:1], QKN[:, 0:1], QK_SCALE, None, ALU.mult))
        dve.sem_inc(qk_norm, 1)

        dve.wait_ge(mod_psum, 8)
        dve.tensor_copy(CC, CA.unsqueeze(2).to_broadcast([P, KC, 32])).then_inc(cc_done, 1)
        for g in range(1, 16, 2):
            dve.wait_ge(tq_psum, g + 1)
            t4, hp = g // 4, g % 4
            dst = QKT[:, t4, 2 * hp:2 * hp + 2, :].rearrange("p h s -> p (h s)")
            if t4 < 2:
                dve.tensor_copy(dst, bank[:, g % 4, :]).then_inc(tq_dve, 1)
            else:
                ts_(dst, bank[:, g % 4, :], QKN[:, t4 - 2:t4 - 1], None, ALU.mult).then_inc(tq_dve, 1)
        ts_(FQB, FG[0:16, :], TAB[0:16, T_QMUL:T_QMUL + 1], TAB[0:16, T_QADD:T_QADD + 1], ALU.mult, ALU.add).then_inc(fqb_done, 1)

        def key_bias(h):
            if h >= 2:
                dve.wait_ge(sc_psum, H + 2 * h - 2)
            ts_(FKB[0:16, h % 2, :], FG[0:16, :], TAB[0:16, T_SELA + h:T_SELA + h + 1], TAB[0:16, T_SELB + h:T_SELB + h + 1],
                ALU.mult, ALU.add).then_inc(fkb_done, 1)

        key_bias(0)
        key_bias(1)
        dve.wait_ge(dec_in, 16)

        def first(k):
            kind, h, t = units[k]
            sb = bank[:, 4 + k % 2, :]
            dve.wait_ge(sc_psum, k + 1)
            if kind == "ret":
                if k >= 2:
                    dve.wait_ge(o_psum, k - 1)
                st.link(tt_(ST[:, k % 2, 0:S], sb[:, 0:S], DEC[:, h, :], ALU.mult))
                tt_(ST[:, k % 2, S:S + P], sb[:, S:S + P], DEC[:, h, 0:P], ALU.mult).then_inc(st_done, 1)
            else:
                n = before("fox", k)
                w = P * (t + 1)
                if n >= 2:
                    dve.wait_ge(pt_psum, n - 1)
                mx = CST[:, t, h:h + 1]
                mask = TAB[:, T_MASK:T_MASK + S] if t else TAB[:, T_MASK + P:T_MASK + S]
                st.link(tt_(PR[:, k % 2, 0:w], sb[:, 0:w], mask, ALU.add))
                st.link(dve.tensor_reduce(mx, PR[:, k % 2, 0:w], AX_X, ALU.max))
                ts_(mx, mx, -1.0, None, ALU.mult).then_inc(lmax_done, 1)
                if t == 1 and h + 2 < H:
                    key_bias(h + 2)

        def second(k):
            kind, h, t = units[k]
            if kind == "fox":
                n = before("fox", k)
                w = P * (t + 1)
                dve.wait_ge(pt_psum, n + 1)
                if n >= 2:
                    dve.wait_ge(o_psum, k - 1)
                dve.tensor_copy(PRT[:, k % 2, 0:w], bank[:, 2 + k % 2, 0:w]).then_inc(pt_copied, 1)
                st.link(dve.reciprocal(CST[:, 10 + t, h:h + 1], CST[:, 2 + t, h:h + 1]))

        def third(k):
            kind, h, t = units[k]
            if kind == "fox":
                dve.wait_ge(o_psum, k + 1)
                ts_(MIX[:, t, HW + h * DH:HW + (h + 1) * DH], bank[:, 6 + k % 2, 0:P], CST[:, 10 + t, h:h + 1], None,
                    ALU.mult).then_inc(o_scaled, 1)

        def ret_stats():
            dve.wait_ge(o_copied, H)
            for t in range(TT):
                for h in range(H):
                    last = dve.bn_stats(BST[:, t * H + h, :], MIX[:, t, h * DH:(h + 1) * DH])
            st.link(last)
            for u in range(TT * H):
                last = dve.bn_aggr(BAG[:, u, :], BST[:, u, :])
            last.then_inc(bn_done, 1)
            dve.wait_ge(bn_done, 1)

        def ret_scale():
            dve.wait_ge(bn_rt, 1)
            st.link(dve.reciprocal(CST[:, 6:8, 0:8], CST[:, 6:8, 0:8]))
            for t in range(TT):
                for h in range(H):
                    y = MIX[:, t, h * DH:(h + 1) * DH]
                    last = ts_(y, y, BAG[:, t * H + h, 0:1], CST[:, 6 + t, h:h + 1], ALU.subtract, ALU.mult)
            st.link(last)
            tt_(MIX[:, :, 0:HW], MIX[:, :, 0:HW], GATE, ALU.mult).then_inc(mix_ret, 1)

        for k in range(NU + 2):
            if k < NU:
                first(k)
            if 1 <= k <= NU:
                second(k - 1)
            if k >= 2:
                third(k - 2)
            if k == NU - 8:
                ret_stats()
        ret_scale()
        dve.wait_ge(fo_rt, 1)
        dve.wait_ge(onw_in, 16)
        st.link(dve.reciprocal(CST[:, 8:10, 0:8], CST[:, 8:10, 0:8]))
        for t in range(TT):
            for h in range(H):
                y = MIX[:, t, HW + h * DH:HW + (h + 1) * DH]
                last = stt(y, y, CST[:, 8 + t, h:h + 1], ONW[:, h * DH:(h + 1) * DH], ALU.mult, ALU.mult)
        last.then_inc(mix_fox, 1)
        for g in range(8):
            dve.wait_ge(mt_copied, g + 1)
            tt_(ML[:, 2 * g:2 * g + 2, :].rearrange("p j s -> p (j s)"), bank[:, (g + 4) % 8, :],
                MH[:, 2 * g:2 * g + 2, :].bitcast(F32).rearrange("p j s -> p (j s)"), ALU.subtract).then_inc(ml_done, 1)

        dve.wait_ge(mod_copied, 8)
        dve.wait_ge(sc2_copied, 1)
        for n, (m, add) in enumerate(((G1B, 0.0), (SC2B, 1.0))):
            dve.wait_ge(nw_in, 16 * (n + 1))
            stt(m, m, add, NW, ALU.add, ALU.mult).then_inc(nw_used, 1)
        dve.wait_ge(nw_used, 2)
        for cc in range(4):
            for tt in range(TT):
                yb = bank[:, 2 * cc + tt, :]
                dve.wait_ge(y_sq, 2 * cc + tt + 1)
                st.link(tt_(yb, yb, G1B[:, cc * CH:(cc + 1) * CH], ALU.mult))
        dve.tensor_reduce(RS[:, 2:4], SS[:, 0:8].rearrange("p (t c) -> p t c", t=TT), AX_X, ALU.add).then_inc(yg_done, 1)
        dve.wait_ge(y_rt, 1)
        st.link(dve.reciprocal(RS[:, 0:2], RS[:, 0:2]))
        for tt in range(TT):
            yg = bank[:, :, :].rearrange("p (c t) n -> p t c n", t=TT)[:, tt]
            xv = X[:, tt, :].rearrange("p (c n) -> p c n", c=4)
            stt(xv, yg, RS[:, tt:tt + 1], xv, ALU.mult, ALU.add).then_inc(x1_done, 1)
        dve.wait_ge(x1_done, 2)
        dve.sem_inc(yg_read, 2)
        dve.tensor_copy(GC, CA.unsqueeze(2).to_broadcast([P, KC, 32])).then_inc(gc_done, 1)
        for tt in range(TT):
            dve.wait_ge(x1_rt, tt + 1)
            st.link(dve.reciprocal(RS[:, 6 + tt:7 + tt], RS[:, 6 + tt:7 + tt]))
            by_j = lambda r: r.rearrange("p (q j) -> p j q", j=KC)
            st.link(stt(H2[:, tt], by_j(X[:, tt, :]), RS[:, 6 + tt:7 + tt], by_j(SC2B), ALU.mult, ALU.mult))
            tt_(H2[:, tt], H2[:, tt], by_j(SH2B), ALU.add).then_inc(h2_done, 1)
        dve.wait_ge(h2_done, 2)
        dve.memset(YS, 0.0).then_inc(ye_dve, 1)
        for g in range(1, 8, 2):
            dve.wait_ge(h2t_psum, g + 1)
            dve.tensor_copy(H2T[:, 2 * g:2 * g + 2, :].rearrange("p j s -> p (j s)"), bank[:, g % 4, :]).then_inc(h2t_dve, 1)

        i32x = IOTA[:, 0:NE]
        st.link(dve.memset(CPAD, -BIG))
        for tt in range(TT):
            c = lambda n: RC[:, tt, n:n + 1]
            dve.wait_ge(lg_psum, tt + 1)
            st.link(tt_(LG[:, tt, :], bank[:, 6 + tt, 0:36], RBS, ALU.add))
            st.link(dve.tensor_copy(CPAD[:, tt, 0:NG], LG[:, tt, 0:NG]))
            st.link(dve.max(M8[:, tt, :], CPAD[:, tt, :]))
            ts_(c(0), M8[:, tt, 0:1], -1.0, None, ALU.mult).then_inc(cmax_done, 1)
            st.link(dve.max_index(etop[:, 0, :], M8[:, tt, :], CPAD[:, tt, :]))
            st.link(dve.tensor_copy(c(5), etop[:, 0, 0:1]))
            st.link(ts_(GE[:, tt, :], IOTA[:, 0:NG], c(5), None, ALU.is_equal))
            st.link(ts_(GE[:, tt, :], GE[:, tt, :], BIG, -BIG, ALU.mult, ALU.add))
            st.link(tt_(FM[:, tt, :].rearrange("p (g e) -> p g e", g=NG), LG[:, tt, NG:36].rearrange("p (g e) -> p g e", g=NG),
                        GE[:, tt, :].unsqueeze(2).to_broadcast([P, NG, EG]), ALU.add))
            st.link(dve.max(F8[:, tt, :], FM[:, tt, :]))
            tt_(c(3), F8[:, tt, 1:2], F8[:, tt, 0:1], ALU.subtract).then_inc(fdif_done, 1)
            st.link(dve.max_index(etop[:, 1, :], F8[:, tt, :], FM[:, tt, :]))
            st.link(dve.tensor_copy(RC[:, tt, 6:8], etop[:, 1, 0:2]))
            st.link(ts_(O1[:, tt, :], i32x, c(6), None, ALU.is_equal))
            st.link(ts_(O2[:, tt, :], i32x, c(7), None, ALU.is_equal))
            tt_(MK[:, tt, :], O1[:, tt, :], O2[:, tt, :], ALU.add).then_inc(mk_done, 1)
            dve.wait_ge(cexp_done, tt + 1)
            dve.wait_ge(fexp_done, tt + 1)
            st.link(stt(c(8), c(4), 1.0, c(1), ALU.add, ALU.mult))
            st.link(dve.reciprocal(c(9), c(8)))
            st.link(tt_(c(10), c(9), c(4), ALU.mult))
            st.link(ts_(CW[:, tt, :], O1[:, tt, :], c(9), None, ALU.mult))
            st.link(stt(CW[:, tt, :], O2[:, tt, :], c(10), CW[:, tt, :], ALU.mult, ALU.add))
        st.link(dve.memset(SLOT, -1.0))
        st.link(dve.memset(COEF, 0.0))
        dve.wait_ge(rank_psum, 1)
        dve.wait_ge(mk_done, 2)
        for tt in range(TT):
            s0 = SLOT[:, tt, 0:NE]
            st.link(stt(s0, bank[:, 4, tt * NE:(tt + 1) * NE], 1.0, MK[:, tt, :], ALU.add, ALU.mult))
            st.link(ts_(s0, s0, -1.0, None, ALU.add))
            for r in range(ROUNDS):
                if r:
                    st.link(ts_(SLOT[:, tt, r * NE:(r + 1) * NE], s0, -float(r * SLOTS), None, ALU.add))
                st.link(dve.tensor_copy(COEF[:, tt, r * NE:(r + 1) * NE], CW[:, tt, :]))
        st.link(dve.tensor_reduce(JUNK[:, 4:5], bank[:, 4, 2 * NE:3 * NE], AX_X, ALU.max))
        dve.tensor_copy(icount[:, 0:1], JUNK[:, 4:5]).then_inc(count_done, 1)
        dve.memset(SELT, 0.0).then_inc(ct_copied, 1)

        def gather_matrix(n):
            for tt in range(TT):
                for b in range(2):
                    last = ts_(SELG[:, tt, b * SLOTS:(b + 1) * SLOTS], IOTA, SLOT[:, tt, bass.ds(2 * n + b, 1)], None, ALU.is_equal)
            last.then_inc(selg_done, 1)

        def weight_matrix(n):
            for tt in range(TT):
                for b in range(2):
                    last = ts_(SELC[:, tt, b * SLOTS:(b + 1) * SLOTS], IOTA, SLOT[:, tt, bass.ds(2 * n + b, 1)],
                               COEF[:, tt, bass.ds(2 * n + b, 1)], ALU.is_equal, ALU.mult)
            last.then_inc(selc_done, 1)

        def add_back(g, last=False):
            for n in range(8):
                tt, cc = n // 4, n % 4
                y = YACC[:, tt, cc * CH:(cc + 1) * CH]
                dve.wait_ge(add_psum, 8 * g + (n + 1))
                tt_(y, bank[:, 6 + n % 2, :], y, ALU.add).then_inc(added, 1)
                if last and n % 4 == 3:
                    dve.wait_ge(added, 8 * g + (n + 3))
                    dve.sem_inc(sum_done, 1)

        def vector_expert(g, b, v):
            dve.wait_ge(silu_done, v + 1)
            tt_(HID[SLOTS:P, :], SG[SLOTS:P, :], bank[SLOTS:P, 2, :], ALU.mult).then_inc(hid_done, 1)
            if b == 0:
                weight_matrix(g)
                gather_matrix(g + 1)
                add_back(g)
            dve.wait_ge(er_used, 6 * v + 6)
            dve.tensor_copy(YS[SLOTS * b:SLOTS * b + SLOTS, 2 * CH:4 * CH], bank[SLOTS:P, 4:6, :].rearrange("p b n -> p (b n)")).then_inc(ye_dve, 1)

        gather_matrix(0)
        dve.wait_ge(g_used, KC)
        dve.memset(YACC[:, 0, :], 0.0).then_inc(added, 1)
        dve.memset(YACC[:, 1, :], 0.0).then_inc(added, 1)
        dve.wait_ge(g2_copied, 2)
        dve.wait_ge(nw2_in, 16)
        tt_(G2B, G2B, NW2, ALU.mult).then_inc(g2_done, 1)
        with dve.Fori(0, NP) as g:
            for b in range(2):
                vector_expert(g, b, 2 * g + b)
        most = dve.value_load(icount[0:1, 0:1], min_val=0, max_val=S)
        with dve.If(most > SLOTS):
            with dve.Fori(NP, ROUNDS * NP) as g:
                for b in range(2):
                    vector_expert(g, b, 2 * g + b)
            add_back(ROUNDS * NP, last=True)
        with dve.Else():
            add_back(NP, last=True)
        dve.wait_ge(g2_done, 1)
        for tt in range(TT):
            st.link(tt_(YG[:, tt, :], YACC[:, tt, :], G2B, ALU.mult))
        for tt in range(TT):
            dve.wait_ge(y2_rt, tt + 1)
            st.link(dve.reciprocal(RS[:, 10 + tt:11 + tt], RS[:, 10 + tt:11 + tt]))
            for half in range(2):
                c = slice(half * HW, (half + 1) * HW)
                stt(X[:, tt, c], YG[:, tt, c], RS[:, 10 + tt:11 + tt], X[:, tt, c], ALU.mult, ALU.add).then_inc(res_done, 1)


_INS = ["x", "c", "ada_w", "ada_b", "norm_pre_mix", "norm_post_mix", "w_in", "fox_f_bias", "ret_gn_w",
        "fox_qn_w", "fox_kn_w", "fox_on_w", "w_out", "norm_pre_ffn", "norm_post_ffn",
        "router_coarse_w", "router_coarse_b", "router_fine_w", "router_fine_b", "w1", "w3", "w2"]


def kernel(**inputs):
    import numpy as _np
    import concourse.bacc as _bacc
    from concourse import mybir as _mybir
    from concourse.bass_utils import run_bass_kernel_spmd as _run

    nc = _bacc.Bacc("TRN2", target_bir_lowering=False, num_devices=1)
    arrays = {f"in_{name}_dram": _np.ascontiguousarray(inputs[name]) for name in _INS}
    arrays["shape_table_dram"], arrays["decay_table_dram"] = shape_tables()
    args = {n: nc.dram_tensor(n, v.shape, _mybir.dt.from_np(v.dtype), kind="ExternalInput").ap() for n, v in arrays.items()}
    x = arrays["in_x_dram"]
    out = nc.dram_tensor("out_dram", x.shape, _mybir.dt.from_np(x.dtype), kind="ExternalOutput").ap()
    build(nc, {n: args[f"in_{n}_dram"] for n in _INS}, args["shape_table_dram"], args["decay_table_dram"], out)
    r = _run(nc, [arrays], core_ids=[0])
    return r.results[0]["out_dram"]
```

```python
from contextlib import ExitStack, contextmanager

import numpy as np

import concourse.bass as bass
from concourse import mybir

F32 = mybir.dt.float32
F32R = mybir.dt.float32r
I32 = mybir.dt.int32
U32 = mybir.dt.uint32
ALU = mybir.AluOpType
ACT = mybir.ActivationFunctionType
AX_X = mybir.AxisListType.X

P = 128
S, D = 256, 2048
TT = S // P
KC = D // P
DH = 128
H = 8
HW = H * DH
CH = 512
NT = 7
FE = 512
FQ = FE // P
NG, EG = 4, 8
NE = NG * EG
SLOTS = 64
WARM_H2 = 3
G2_EARLY = 12
ROUNDS = S // SLOTS
NP = NE // 2
NV = ROUNDS * NE
EPS = 1e-6
BIG = 1e30
ROPE_BASE = 10000.0
QK_SCALE = float(DH) ** -0.5

T_ID = 0
T_COS = T_ID + P
T_SIN = T_COS + TT * 64
T_MASK = T_SIN + TT * 64
T_TRI = T_MASK + 2 * P
T_IOTA = T_TRI + P
T_SELA = T_IOTA + SLOTS
T_SELB = T_SELA + H
T_QMUL = T_SELB + H
T_QADD = T_QMUL + 1
T_ONE = T_QADD + 1
TABLE = T_ONE + P


def shape_tables():
    t = np.zeros((P, TABLE), np.float32)
    t[:, T_ID:T_ID + P] = np.eye(P, dtype=np.float32)
    inv = np.float32(ROPE_BASE) ** (-np.arange(0, DH, 2, dtype=np.float32) / np.float32(DH))
    angle = np.arange(S, dtype=np.float32)[:, None] * inv[None, :].astype(np.float32)
    for tt in range(TT):
        t[:, T_COS + tt * 64:T_COS + tt * 64 + 64] = np.cos(angle[tt * P:(tt + 1) * P])
        t[:, T_SIN + tt * 64:T_SIN + tt * 64 + 64] = np.sin(angle[tt * P:(tt + 1) * P])
    r = np.arange(P)
    t[:, T_MASK + P:T_MASK + 2 * P] = np.where(r[None, :] <= r[:, None], 0.0, -BIG)
    t[:, T_TRI:T_TRI + P] = r[:, None] < r[None, :]
    t[:, T_IOTA:T_IOTA + SLOTS] = np.arange(SLOTS)
    for h in range(H):
        t[h, T_SELA + h] = 0.0
        t[h, T_SELB + h] = 1.0
        t[H + h, T_SELA + h] = -1.0
    t[0:H, T_QMUL] = 1.0
    t[H:2 * H, T_QADD] = 1.0
    t[:, T_ONE:T_ONE + P] = 1.0
    s = np.arange(P)[:, None]
    q = np.arange(S)[None, :]
    decay = np.zeros((P, H, S), np.float32)
    for h in range(H):
        lg = np.log1p(-np.exp2(-5.0 - h))
        decay[:, h, :] = np.where(q >= s, np.exp(lg * np.maximum(q - s, 0)), 0.0) * QK_SCALE
    return t, decay.reshape(P, H * S)


class Steps:

    def __init__(self, eng, sem):
        self.eng, self.sem, self.n, self.past = eng, sem, 0, 0

    def link(self, ins):
        ins.then_inc(self.sem, 1)
        self.n += 1
        self.eng.wait_ge(self.sem, self.past + self.n)

    @contextmanager
    def loop(self, i, per, count, first=0):
        n0 = self.n
        outer = self.past
        self.past = self.past + (i - first) * per if first else self.past + i * per
        yield
        assert self.n - n0 == per, (self.n - n0, per)
        self.n = n0 + per * count
        self.past = outer


def build(nc, a, table, decay_table, out):
    ctx = ExitStack()

    def sem(name):
        return ctx.enter_context(nc.semaphore(name))

    KB = 256
    base = 17376
    arena = nc.alloc_sbuf_tensor_at("arena", [P, 207 * KB], F32, offset=base)
    split_at = {"wh": (64, 4 * 2 * CH), "wl": (176, 4 * 2 * CH), "hh": (153, KC * S), "hl": (137, KC * S),
                "mh": (144, KC * S), "ml": (160, KC * S)}
    rounded = {n: nc.alloc_sbuf_tensor_at(f"rounded_{n}", [P, cols], F32R, offset=base + kb * 1024)
               for n, (kb, cols) in split_at.items()}
    plain_at = {"w_units": (48, 2 * 4 * CH), "h_columns": (137, KC * S)}
    plain = {n: nc.alloc_sbuf_tensor_at(n, [P, cols], F32, offset=base + kb * 1024) for n, (kb, cols) in plain_at.items()}
    icount = ctx.enter_context(nc.sbuf_tensor("icount", [P, 8], I32))
    etop = ctx.enter_context(nc.sbuf_tensor("etop", [P, 2, 8], U32))
    bank = ctx.enter_context(nc.psum_tensor("bank", [P, 8, CH], F32))

    def at(kb, cols):
        o = int(kb * KB)
        return arena[:, o:o + cols]

    WH, WL = (rounded[n][:, :].rearrange("p (s j n) -> p s j n", s=4, j=2) for n in ("wh", "wl"))
    HH, HL, MH, ML = (rounded[n][:, :].rearrange("p (j s) -> p j s", j=KC) for n in ("hh", "hl", "mh", "ml"))

    X = at(0, TT * D).rearrange("p (t d) -> p t d", t=TT)
    MOD = at(16, 4 * D)
    G1B, SH2B, SC2B, G2B = (MOD[:, i * D:(i + 1) * D] for i in range(4))
    WR = plain["w_units"][:, :].rearrange("p (u j n) -> p u j n", u=2, j=4)
    HRING = at(80, 4 * D).rearrange("p (u n) -> p u n", u=4)
    HACC = at(112, 2 * D).rearrange("p (v n) -> p v n", v=2)
    XS = at(176, TT * D).rearrange("p (t d) -> p t d", t=TT)
    HT = plain["h_columns"][:, :].rearrange("p (j s) -> p j s", j=KC)
    RAW = at(80, TT * NT * HW).rearrange("p (t n) -> p t n", t=TT)
    ARING = at(32, 2 * 4 * CH).rearrange("p (u j n) -> p u j n", u=2, j=4)
    ABIAS = at(171, CH)
    SCR = at(192, 2 * HW).rearrange("p (t n) -> p t n", t=TT)
    GNW = at(28, HW)
    AACC = at(169, CH)
    WF = at(174, KC * 16).rearrange("p (j n) -> p j n", j=KC)
    FG = at(175, S)
    QKT = at(137, 4 * H * S).rearrange("p (a h s) -> p a h s", a=4, h=H)
    MIX = RAW[:, :, 0:2 * HW]
    VRET, GATE, VFOX = (RAW[:, :, i * HW:(i + 1) * HW] for i in (2, 3, 6))
    ST = RAW[:, 0, 4 * HW:4 * HW + 768].rearrange("p (b n) -> p b n", b=2)
    PR = RAW[:, 0, 4 * HW + 768:5 * HW + 256].rearrange("p (b n) -> p b n", b=2)
    PRT = RAW[:, 0, 5 * HW + 256:5 * HW + 768].rearrange("p (b n) -> p b n", b=2)
    FQB = RAW[0:2 * H, 0, 5 * HW + 768:6 * HW]
    ONW = RAW[:, 1, 4 * HW:5 * HW]
    BST = RAW[:, 1, 5 * HW:5 * HW + 16 * 6].rearrange("p (u n) -> p u n", n=6)
    BAG = RAW[:, 1, 5 * HW + 128:5 * HW + 160].rearrange("p (u n) -> p u n", n=2)
    CST = RAW[:, 1, 5 * HW + 256:5 * HW + 512].rearrange("p (a u) -> p a u", a=16)
    CSQ = RAW[:, 1, 5 * HW + 512:5 * HW + 640]
    FKB = at(169, 2 * S).rearrange("p (b s) -> p b s", b=2)
    CRING = at(32, 2 * D).rearrange("p (u n) -> p u n", u=2)
    CC = at(171, KC * 32).rearrange("p (j m) -> p j m", m=32)
    CBIAS = at(173, CH)
    CROW = at(44, 2 * CH).rearrange("p (v n) -> p v n", v=2)
    DEC = at(192, H * S).rearrange("p (h s) -> p h s", h=H)
    NW = at(192, D)
    GRING = at(64, 2 * D).rearrange("p (u n) -> p u n", u=2)
    GC = at(16, KC * 32).rearrange("p (j m) -> p j m", m=32)
    GROW = at(20, CH)
    NW2 = at(32, D)
    ER = at(80, 6 * 8 * CH).rearrange("p (u n) -> p u n", u=6)
    H2 = at(176, TT * D).rearrange("p (t j q) -> p t j q", t=TT, j=KC)
    YG = at(176, TT * D).rearrange("p (t d) -> p t d", t=TT)
    H2T = at(48, KC * S).rearrange("p (j s) -> p j s", j=KC)
    YACC = at(64, TT * D).rearrange("p (t d) -> p t d", t=TT)
    XT = at(16, KC * P).rearrange("p (j s) -> p j s", j=KC)
    YS = at(24, D)
    SG = at(48, FE)
    HID = at(50, FE)
    HIDT = at(52, FQ * SLOTS).rearrange("p (q s) -> p q s", q=FQ)
    SELG = at(53, TT * P).rearrange("p (t s) -> p t s", t=TT)
    SELC = at(54, TT * P).rearrange("p (t s) -> p t s", t=TT)
    SELT = at(55, S)
    SLOT = at(192, TT * (NV + 2)).rearrange("p (t e) -> p t e", t=TT)
    COEF = at(194, TT * (NV + 2)).rearrange("p (t e) -> p t e", t=TT)
    used = [200 * KB]

    def small(cols):
        used[0] += cols
        assert used[0] <= 207 * KB, used
        return arena[:, used[0] - cols:used[0]]

    TAB = small(TABLE)
    IDENT = TAB[:, T_ID:T_ID + P]
    ONES = TAB[:, T_ONE:T_ONE + P]
    TRI = TAB[:, T_TRI:T_TRI + P]
    IOTA = TAB[:, T_IOTA:T_IOTA + SLOTS]
    CV, CE, CA, NPRE, SH1, A1 = (small(KC) for _ in range(6))
    SS, RS = small(32), small(32)
    QKN, FBIAS, EPSC = small(2), small(1), small(1)
    RWS = small(KC * 36).rearrange("p (j n) -> p j n", j=KC)
    RBS = small(36)
    W = [196 * KB]

    def work(cols):
        W[0] += cols
        return arena[:, W[0] - cols:W[0]]

    LG = work(TT * 36).rearrange("p (t n) -> p t n", t=TT)
    CPAD = work(TT * 8).rearrange("p (t n) -> p t n", t=TT)
    M8 = work(TT * 8).rearrange("p (t n) -> p t n", t=TT)
    F8 = work(TT * 8).rearrange("p (t n) -> p t n", t=TT)
    GE = work(TT * 4).rearrange("p (t n) -> p t n", t=TT)
    FM = work(TT * NE).rearrange("p (t n) -> p t n", t=TT)
    O1 = work(TT * NE).rearrange("p (t n) -> p t n", t=TT)
    O2 = work(TT * NE).rearrange("p (t n) -> p t n", t=TT)
    CW = work(TT * NE).rearrange("p (t n) -> p t n", t=TT)
    MK = work(TT * NE).rearrange("p (t n) -> p t n", t=TT)
    RC = work(TT * 16).rearrange("p (t n) -> p t n", t=TT)
    JUNK = work(8)

    x_v = a["x"][0].rearrange("(t p) d -> p t d", p=P)
    out_v = out[0].rearrange("(t p) d -> p t d", p=P)
    ada_v = a["ada_w"][0].rearrange("(p j) n -> p j n", j=KC)
    win_v = a["w_in"][0].rearrange("(p j) n -> p j n", j=KC)
    wout_v = a["w_out"][0].rearrange("(j p) n -> p j n", p=P)
    w1_v = a["w1"][0].rearrange("e (p j) n -> p e j n", j=KC)
    w3_v = a["w3"][0].rearrange("e (p j) n -> p e j n", j=KC)
    w2_v = a["w2"][0].rearrange("e (p q) n -> p e q n", q=FQ)

    def col(ap):
        return ap.rearrange("a (p n) -> (a p) n", n=1)

    def across(ap, n=P):
        return ap.broadcast_to([n, ap.shape[-1]])

    v_step, s_step = sem("vector_step"), sem("scalar_step")
    tab_in, c_in, x_in, small_in, fgate_in, gnw_in = (sem(n) for n in (
        "table_in", "c_in", "x_in", "small_in", "fgate_in", "gnw_in"))
    dec_in, onw_in, hbias_in, abias_in = sem("decay_in"), sem("onw_in"), sem("hbias_in"), sem("abias_in")
    nw_in = sem("normw_in")
    hring_in = [sem(f"head_rows_in{u}") for u in range(4)]
    aring_in = [sem(f"ada_rows_in{u}") for u in range(2)]
    wr_in = [sem(f"w_unit_in{u}") for u in range(2)]
    crow_in = [sem(f"late_rows_in{u}") for u in range(2)]
    cbias_in = sem("late_bias_in")
    nw2_in = sem("norm_post_ffn_in")
    er_in = [sem(f"expert_unit_in{u}") for u in range(6)]
    out_done = sem("out_done")
    zeroed, ce_done, ca_done, hrow_used = sem("zeroed"), sem("c_exp_done"), sem("c_act_done"), sem("head_rows_used")
    xsq_done, xrt_done, xs_done = sem("x_squares_done"), sem("x_root_done"), sem("x_scaled")
    xt_psum, xt_copied = sem("x_transposed"), sem("x_transposes_copied")
    hacc_done, hcol_psum, ht_done = sem("head_sum_done"), sem("head_columns_ready"), sem("h_ready")
    arow_used, abias_used, acc_done = sem("ada_rows_used"), sem("ada_bias_used"), sem("ada_sum_done")
    mod_psum, mod_copied = sem("mod_ready"), sem("mod_copied")
    hi_done, lo_done, part_used, ch_copied = (sem(n) for n in (
        "high_part_done", "low_part_done", "parts_used", "chunk_copied"))
    hh_done, hl_done, ml_done = sem("h_high_done"), sem("h_low_done"), sem("mix_low_done")
    cc_done, late_used, late_psum, late_row, late_spread, late_copied = (sem(n) for n in (
        "late_factors_done", "late_rows_used", "late_rows_summed", "late_sums_copied", "late_sums_spread", "late_vectors_copied"))
    grow_in = [sem(f"g2_rows_in{u}") for u in range(2)]
    gc_done, g_used, g_psum, g_row, g2_psum, g2_done = (sem(n) for n in (
        "g2_factors_done", "g2_rows_used", "g2_summed", "g2_row_copied", "g2_spread", "g2_done"))
    fg_psum, fg_abs, fg_exp, fg_ln, fg_done = (sem(n) for n in (
        "forget_ready", "forget_abs", "forget_exp", "forget_ln", "forget_done"))
    gate_exp, gnw_used = sem("gate_exp"), sem("gnw_used")
    qk_sq, qk_rt, rope_done, qk_norm = sem("qk_squares"), sem("qk_root"), sem("rope_done"), sem("qk_normed")
    tq_psum, tq_act, tq_dve = sem("qk_transposed"), sem("qk_copied_scalar"), sem("qk_copied_vector")
    fqb_done, fkb_done = sem("query_bias_done"), sem("key_bias_done")
    sc_psum, st_done, lmax_done, exp_done = (sem(n) for n in (
        "scores_ready", "decayed", "max_done", "exp_done"))
    pt_psum, pt_copied, o_psum, o_copied, o_scaled = (sem(n) for n in (
        "probs_transposed", "probs_copied", "heads_out_ready", "ret_out_copied", "fox_out_scaled"))
    bn_done, bn_rt, fsq_done, fo_rt, mix_ret, mix_fox = (sem(n) for n in (
        "bn_done", "bn_root", "fox_squares_done", "fox_root", "ret_mixed", "fox_mixed"))
    bn_inv, ret_scaled = sem("bn_reciprocal_done"), sem("ret_heads_scaled")
    mt_psum, mt_copied = sem("mix_transposed"), sem("mix_high_done")
    y_sq, y_rt, nw_used, yg_done, yg_read = (sem(n) for n in ("y_squares", "y_root", "normw_used", "yg_done", "yg_read"))
    x1_done, x1_sq, x1_rt, h2_done = sem("x1_done"), sem("x1_squares"), sem("x1_root"), sem("h2_done")
    h2t_psum, h2t_copied, h2t_dve, lg_psum = sem("h2_transposed"), sem("h2t_copied_scalar"), sem("h2t_copied_vector"), sem("logits_ready")
    cmax_done, cexp_done, fdif_done, fexp_done, mk_done, rank_psum, count_done = (sem(n) for n in (
        "coarse_max", "coarse_exp", "fine_difference", "fine_exp", "mask_done", "ranks_ready", "count_done"))
    selg_done, selc_done = sem("gather_matrix_done"), sem("weight_matrix_done")
    xg_psum, xg_copied, ct_psum, ct_copied = (sem(n) for n in (
        "gathered", "gathered_copied", "weights_transposed", "weights_copied"))
    silu_done, hid_done, hid_seen, hidt_psum, hidt_copied = (sem(n) for n in (
        "silu_done", "hidden_done", "hidden_seen", "hidden_transposed", "hidden_copied"))
    ye_act, ye_dve, er_used = (sem(n) for n in (
        "result_copied_scalar", "result_copied_vector", "expert_unit_used"))
    add_psum, added = sem("addend_ready"), sem("added")
    sum_done, y2_sq, y2_rt, res_done = sem("sum_done"), sem("y2_squares"), sem("y2_root"), sem("out_ready")

    units = [("ret", h, 0) for h in range(H)] + [("fox", h, t) for h in range(H) for t in range(TT)]
    NU = len(units)

    tq_bank = (5, 1, 6, 7)
    mt_bank = (4, 5, 6, 7, 2, 3, 4, 5)
    late_granules = range(5, 13, 2)

    def before(kind, k):
        return sum(u[0] == kind for u in units[:max(k, 0)])

    block = ctx.enter_context(nc.Block())

    @block.sync
    def _(sp):
        sp.dma_start(CV, a["c"].rearrange("b (p j) -> (b p) j", j=KC)).then_inc(c_in, 16)
        sp.dma_start(TAB, table).then_inc(tab_in, 16)

        for v in range(2):
            for u in range(4 if v == 0 else 0):
                sp.dma_start(HRING[:, u, :], ada_v[:, u, 0:D]).then_inc(hring_in[u], 16)
            with sp.Fori(1 - v, 4) as i:
                for u in range(4):
                    sp.wait_ge(hrow_used, 4 * i + (16 * v - 3) + u)
                    sp.dma_start(HRING[:, u, :], ada_v[:, bass.ds(4 * i + u, 1), v * D:(v + 1) * D]).then_inc(hring_in[u], 16)

        def win(chunk, u, first=False):
            if not first:
                sp.wait_ge(lo_done, 8 * chunk + (2 * u - 2))
            sp.dma_start(WR[:, u % 2], win_v[:, 4 * u:4 * u + 4, bass.ds(chunk * CH, CH)]).then_inc(wr_in[u % 2], 16)

        def ada(ps, k, first=False):
            if not first:
                sp.wait_ge(arow_used, 4 * ps + (k - 1))
            sp.dma_start(ARING[:, k % 2], ada_v[:, 4 * k:4 * k + 4, bass.ds(ps * CH + 2 * D, CH)]).then_inc(aring_in[k % 2], 16)

        def abias(ps):
            sp.wait_ge(abias_used, ps)
            sp.dma_start(ABIAS[0:1, :], a["ada_b"][:, bass.ds(ps * CH + 2 * D, CH)]).then_inc(abias_in, 16)

        def iteration(it):
            for k in range(8):
                win(2 * it + k // 4, k % 4)
                if k == 0:
                    abias(it + 1)
                if k % 2 == 1:
                    ada(it + 1, k // 2)

        for u in range(2):
            win(0, u, first=True)
        for k in range(2):
            ada(0, k, first=True)
        win(0, 2)
        win(0, 3)
        ada(0, 2)
        win(1, 0)
        ada(0, 3)
        win(1, 1)
        abias(1)
        for k in range(4):
            ada(1, k)
            if k < 2:
                win(1, 2 + k)
        with sp.Fori(1, 7) as it:
            iteration(it)

        def wout(n):
            sp.wait_ge(lo_done, 2 * (56 + n) - 2)
            sp.dma_start(WR[:, n % 2], wout_v[:, 4 * (n % 4):4 * (n % 4) + 4, (n // 4) * CH:(n // 4 + 1) * CH]).then_inc(wr_in[n % 2], 16)

        sp.wait_ge(arow_used, 32)
        for n in range(KC + G2_EARLY):
            v, j = n // KC, n % KC
            if n == 6:
                wout(0)
                wout(1)
            if n in (2, 19):
                if n == 2:
                    sp.wait_ge(fg_psum, KC)
                else:
                    sp.wait_ge(late_psum, 1)
                sp.dma_start(CBIAS[0:P:32, :], a["ada_b"][:, (4 + v) * D:(5 + v) * D].rearrange("a (g n) -> (a g) n", g=4)).then_inc(cbias_in, 16)
            if n >= 2:
                sp.wait_ge(late_used, n - 1)
            sp.dma_start(CRING[:, n % 2, :], ada_v[:, j, (4 + v) * D:(5 + v) * D]).then_inc(crow_in[n % 2], 16)

        def expert(e, u, halves=(0, 1)):
            if u < 4:
                w13 = ER[:, u].rearrange("p (w j n) -> p w j n", w=2, j=4)
                for w in halves:
                    src = (w1_v, w3_v)[w]
                    sp.dma_start(w13[:, w], src[:, bass.ds(e, 1), 4 * u:4 * u + 4, :].rearrange("p e j n -> p (e j) n")).then_inc(er_in[u], 16)
            else:
                sp.dma_start(ER[:, u].rearrange("p (q n) -> p q n", q=2),
                             w2_v[:, bass.ds(e, 1), 2 * u - 8:2 * u - 6, :].rearrange("p e q n -> p (e q) n")).then_inc(er_in[u], 16)

        for n in range(2, 16):
            if n == 4:
                sp.wait_ge(mt_psum, 8)
            if 4 <= n < 12:
                expert(0, (n - 4) // 2, (n % 2,))
            wout(n)
        sp.wait_ge(part_used, 8 * 18)
        for j in range(G2_EARLY, KC):
            n = j - G2_EARLY
            if n >= 2:
                sp.wait_ge(g_used, n - 1)
            sp.dma_start(GRING[:, n % 2, :], ada_v[:, j, 5 * D:6 * D]).then_inc(grow_in[n % 2], 16)
            if n == 1:
                expert(0, 4)
                expert(0, 5)
        sp.wait_ge(h2_done, 2)
        sp.dma_start(NW2, across(a["norm_post_ffn"])).then_inc(nw2_in, 16)

        def expert_loop(e, v):
            for u in range(6):
                sp.wait_ge(er_used, 6 * v + (u - 5))
                expert(e, u)

        with sp.Fori(1, NE) as e:
            expert_loop(e, e)
        sp.wait_ge(count_done, 1)
        most = sp.value_load(icount[0:1, 0:1], min_val=0, max_val=S)
        with sp.If(most > SLOTS):
            with sp.Fori(1, ROUNDS) as r:
                with sp.Fori(0, NE) as e:
                    expert_loop(e, NE * r + e)
        for tt in range(TT):
            for half in range(2):
                c = slice(half * HW, (half + 1) * HW)
                sp.wait_ge(res_done, 2 * tt + half + 1)
                sp.dma_start(out_v[:, tt, c], X[:, tt, c]).then_inc(out_done, 16)
        sp.wait_ge(out_done, 64)

    @block.scalar
    def _(act):
        st = Steps(act, s_step)
        for tt in range(TT):
            act.dma_start(X[:, tt, :], x_v[:, tt, :]).then_inc(x_in, 16)
        act.dma_start(NPRE, a["norm_pre_mix"].rearrange("l (p j) -> (l p) j", j=KC)).then_inc(small_in, 16)
        act.dma_start(QKN[:, 0:1], col(a["fox_qn_w"])).then_inc(small_in, 16)
        act.dma_start(QKN[:, 1:2], col(a["fox_kn_w"])).then_inc(small_in, 16)
        for r in range(2):
            act.dma_start(FBIAS[r * H:(r + 1) * H, :], col(a["fox_f_bias"])).then_inc(small_in, 16)
        act.dma_start(RWS[:, :, 0:NG], a["router_coarse_w"][0].rearrange("(p j) n -> p j n", j=KC)).then_inc(small_in, 16)
        act.dma_start(RWS[:, :, NG:36], a["router_fine_w"][0].rearrange("(p j) n -> p j n", j=KC)).then_inc(small_in, 16)
        act.dma_start(RBS[:, 0:NG], across(a["router_coarse_b"])).then_inc(small_in, 16)
        act.dma_start(RBS[:, NG:36], across(a["router_fine_b"])).then_inc(small_in, 16)
        for r in range(2):
            act.dma_start(WF[:, :, r * H:(r + 1) * H], win_v[:, :, NT * HW:NT * HW + H]).then_inc(fgate_in, 16)
        act.dma_start(GNW, across(a["ret_gn_w"])).then_inc(gnw_in, 16)
        act.wait_ge(zeroed, 1)
        act.dma_start(HACC[0:1, 0, :], a["ada_b"][:, 0:D]).then_inc(hbias_in, 16)
        act.dma_start(HACC[0:1, 1, :], a["ada_b"][:, D:2 * D]).then_inc(hbias_in, 16)
        act.dma_start(ABIAS[0:1, :], a["ada_b"][:, 2 * D:2 * D + CH]).then_inc(abias_in, 16)
        act.wait_ge(c_in, 16)
        act.activation(CE, CV, ACT.Exp, scale=-1.0).then_inc(ce_done, 1)
        act.wait_ge(x_in, 32)
        for tt in range(TT):
            act.activation(XS[:, tt, :], X[:, tt, :], ACT.Square, accum_out=SS[:, tt:tt + 1]).then_inc(xsq_done, 1)
        act.wait_ge(zeroed, 2)
        act.wait_ge(xsq_done, 2)
        act.activation(RS[:, 0:2], SS[:, 0:2], ACT.Sqrt, scale=1.0 / D, bias=EPSC).then_inc(xrt_done, 1)
        for g in range(8):
            act.wait_ge(xt_psum, g + 1)
            act.activation(HT[:, 2 * g:2 * g + 2, :], bank[:, g % 4, :], ACT.Copy).then_inc(xt_copied, 1)

        def high(n, gq):
            if not (isinstance(n, int) and n < 4):
                act.wait_ge(part_used, n - 3)
            if gq % 2 == 0:
                act.wait_ge(wr_in[gq // 2 % 2], (2 * n - 2 * gq) * 2 + (16 * (gq // 4) + 16))
            src = WR[:, gq // 2 % 2, 2 * (gq % 2):2 * (gq % 2) + 2, :]
            act.activation(WH[:, gq % 4], src, ACT.Copy).then_inc(hi_done, 1)

        for gq in range(4):
            high(gq, gq)
        for j in range(KC):
            act.wait_ge(ht_done, j + 1)
            act.activation(HH[:, j, :], HT[:, j, :], ACT.Copy).then_inc(hh_done, 1)

        def chunk_copy(c):
            b = c[1]
            act.wait_ge(part_used, 8 * c[0] + 8)
            act.activation(RAW[:, :, bass.ds(c[0] * CH, CH)], bank[:, 2 * b:2 * b + 2, :], ACT.Copy).then_inc(ch_copied, 1)

        def forget():
            act.wait_ge(fg_abs, 1)
            act.activation(SCR[0:16, 0, S:2 * S], SCR[0:16, 0, 0:S], ACT.Exp, scale=-1.0).then_inc(fg_exp, 1)
            act.wait_ge(fg_exp, 1)
            act.activation(SCR[0:16, 0, 2 * S:3 * S], SCR[0:16, 0, S:2 * S], ACT.Ln, bias=1.0).then_inc(fg_ln, 1)

        def iteration(it, last_gates=False):
            for b in range(2):
                for gq in range(8):
                    high(16 * it + (8 * b + gq), gq)
                    if last_gates and b == 1 and gq == 5:
                        act.wait_ge(fg_done, 1)
                        act.wait_ge(rope_done, 2)
                        act.wait_ge(ch_copied, 8)
                        act.activation(SCR, GATE, ACT.Exp, scale=-1.0).then_inc(gate_exp, 1)
                    if gq == 3:
                        chunk_copy((2 * it + (b - 1), 1 - b))
                    if gq == 1 and b == 1:
                        if isinstance(it, int) and it == 6:
                            act.wait_ge(gnw_used, 1)
                        act.wait_ge(mod_psum, it + 1)
                        act.activation(MOD[:, bass.ds(it * CH, CH)], bank[:, 4, :], ACT.Copy).then_inc(mod_copied, 1)

        for b, gq in [(b, gq) for b in range(2) for gq in range(8)][4:]:
            high(8 * b + gq, gq)
            if b == 1 and gq == 2:
                forget()
            if b == 1 and gq == 3:
                chunk_copy((0, 0))
                act.wait_ge(mod_psum, 1)
                act.activation(MOD[:, 0:CH], bank[:, 4, :], ACT.Copy).then_inc(mod_copied, 1)
        with act.Fori(1, 4) as it:
            iteration(it)
        iteration(4, last_gates=True)
        iteration(5)
        iteration(6)
        act.wait_ge(qk_sq, 1)
        act.activation(RS[:, 0:32], SS[:, 0:32], ACT.Sqrt, scale=1.0 / DH, bias=EPSC).then_inc(qk_rt, 1)
        act.wait_ge(qk_rt, 1)
        act.dma_start(DEC, decay_table.rearrange("p (h s) -> p h s", h=H)).then_inc(dec_in, 16)
        act.wait_ge(mod_psum, 8)
        act.activation(MOD[:, 7 * CH:8 * CH], bank[:, 4, :], ACT.Copy).then_inc(mod_copied, 1)
        chunk_copy((13, 1))
        for g in range(0, 16, 2):
            act.wait_ge(tq_psum, g + 1)
            t4, hp = g // 4, g % 4
            dst = QKT[:, t4, 2 * hp:2 * hp + 2, :]
            if t4 < 2:
                act.activation(dst, bank[:, tq_bank[g % 4], :], ACT.Copy).then_inc(tq_act, 1)
            else:
                act.activation(dst, bank[:, tq_bank[g % 4], :], ACT.Copy, scale=QKN[:, t4 - 2:t4 - 1]).then_inc(tq_act, 1)
        for gq in range(4):
            high(112 + gq, gq)
        act.wait_ge(tq_psum, 16)
        act.dma_start(ONW, across(a["fox_on_w"])).then_inc(onw_in, 16)

        def out_copy(k):
            kind, h, t = units[k]
            if kind == "ret":
                act.wait_ge(o_psum, k + 1)
                act.activation(MIX[:, :, h * DH:(h + 1) * DH], bank[:, 6 + k % 2, 0:2 * P], ACT.Copy).then_inc(o_copied, 1)
            else:
                act.wait_ge(o_scaled, before("fox", k) + 1)
                n = before("fox", k)
                if n:
                    act.wait_ge(fsq_done, n)
                act.activation(CSQ, MIX[:, t, HW + h * DH:HW + (h + 1) * DH], ACT.Square,
                               accum_out=CST[:, 4 + t, h:h + 1]).then_inc(fsq_done, 1)

        for k in range(NU + 2):
            if k < NU and units[k][0] == "fox":
                n = before("fox", k)
                act.wait_ge(lmax_done, n + 1)
                w = P * (units[k][2] + 1)
                act.activation(PR[:, k % 2, 0:w], PR[:, k % 2, 0:w], ACT.Exp, bias=CST[:, 0 + units[k][2], units[k][1]:units[k][1] + 1],
                               accum_out=CST[:, 2 + units[k][2], units[k][1]:units[k][1] + 1]).then_inc(exp_done, 1)
            if k == 12:
                act.wait_ge(st_done, 8)
                act.dma_start(NW, across(a["norm_post_mix"])).then_inc(nw_in, 16)
            if k == 13:
                act.wait_ge(bn_done, 1)
                act.activation(CST[:, 6:8, 0:8], BAG[:, :, 1].rearrange("p (t h) -> p t h", t=TT), ACT.Sqrt, bias=EPSC).then_inc(bn_rt, 1)
            if 1 <= k <= NU and units[k - 1][0] == "fox":
                n = before("fox", k - 1)
                w = P * (units[k - 1][2] + 1)
                act.wait_ge(pt_psum, n + 1)
                if n >= 2:
                    act.wait_ge(o_psum, k - 2)
                act.activation(PRT[:, (k - 1) % 2, 0:w], bank[:, 2 + (k - 1) % 2, 0:w], ACT.Copy).then_inc(pt_copied, 1)
            if k >= 3:
                out_copy(k - 3)
        act.activation(SS[:, 31:32], EPSC, ACT.Sqrt)
        out_copy(NU - 1)
        act.wait_ge(fsq_done, 16)
        act.activation(CST[:, 8:10, 0:8], CST[:, 4:6, 0:8], ACT.Sqrt, scale=1.0 / DH, bias=EPSC).then_inc(fo_rt, 1)
        act.wait_ge(late_psum, 2)
        for v in range(2):
            act.activation(CROW[:, v, :], bank[:, v, :], ACT.Copy).then_inc(late_row, 1)
        for g in range(8):
            act.wait_ge(mt_psum, g + 1)
            act.activation(MH[:, 2 * g:2 * g + 2, :], bank[:, mt_bank[g], :], ACT.Copy).then_inc(mt_copied, 1)

        act.wait_ge(nw_used, 1)
        act.dma_start(NW, across(a["norm_pre_ffn"])).then_inc(nw_in, 16)

        def squares(cc):
            act.wait_ge(part_used, 8 * (14 + cc) + 8)
            for tt in range(TT):
                act.wait_ge(nw_used, 2)
                if 2 * cc + tt:
                    act.wait_ge(y_sq, 2 * cc + tt)
                act.activation(NW[:, 0:CH], bank[:, 2 * cc + tt, :], ACT.Square,
                               accum_out=SS[:, 4 * tt + cc:4 * tt + cc + 1]).then_inc(y_sq, 1)

        for n in range(4, 32):
            high(112 + n, n % 8)
            if n - 5 in late_granules:
                i = late_granules.index(n - 5)
                act.wait_ge(late_spread, i + 1)
                act.activation(MOD[:, (8 + i) * CH:(9 + i) * CH], bank[:, 6 + i % 2, :], ACT.Copy).then_inc(late_copied, 1)
            if n == 19:
                squares(0)
                squares(1)
            if n == 27:
                squares(2)
        squares(3)
        act.wait_ge(yg_done, 1)
        act.activation(RS[:, 0:2], RS[:, 2:4], ACT.Sqrt, scale=1.0 / D, bias=EPSC).then_inc(y_rt, 1)
        for tt in range(TT):
            act.wait_ge(x1_done, tt + 1)
            if tt:
                act.wait_ge(x1_sq, tt)
            act.activation(NW, X[:, tt, :], ACT.Square, accum_out=RS[:, 4 + tt:5 + tt]).then_inc(x1_sq, 1)
            act.wait_ge(x1_sq, tt + 1)
            act.activation(RS[:, 6 + tt:7 + tt], RS[:, 4 + tt:5 + tt], ACT.Sqrt, scale=1.0 / D, bias=EPSC).then_inc(x1_rt, 1)
        def h2_turned(tt, j4):
            act.wait_ge(h2t_psum, 4 * tt + j4 + 1)
            act.activation(H2T[:, 4 * j4:4 * j4 + 4, tt * P:(tt + 1) * P], bank[:, j4, :].rearrange("p (j s) -> p j s", j=4),
                           ACT.Copy).then_inc(h2t_copied, 1)

        for tt in range(TT):
            for j4 in (0, 2):
                h2_turned(tt, j4)
        for tt in range(TT):
            act.wait_ge(cmax_done, tt + 1)
            act.activation(JUNK[:, 0:4], LG[:, tt, 0:NG], ACT.Exp, bias=RC[:, tt, 0:1], accum_out=RC[:, tt, 1:2]).then_inc(cexp_done, 1)
            act.wait_ge(cexp_done, tt + 1)
            act.wait_ge(fdif_done, tt + 1)
            act.activation(RC[:, tt, 4:5], RC[:, tt, 3:4], ACT.Exp).then_inc(fexp_done, 1)

        def gathered(n, g4):
            act.wait_ge(xg_psum, n)
            act.activation(XT[:, 4 * g4:4 * g4 + 4, :], bank[:, g4 % 2, :], ACT.Copy).then_inc(xg_copied, 1)

        def scalar_expert(g, b, v):
            act.wait_ge(er_used, 6 * v + 4)
            act.activation(SG[SLOTS:P, :], bank[0:SLOTS, 2, :], ACT.Silu).then_inc(silu_done, 1)
            if b == 1:
                for g4 in range(4):
                    gathered(4 * g + (5 + g4), g4)
                act.wait_ge(ct_psum, g + 1)
                act.activation(SELT, bank[:, 3, 0:S], ACT.Copy).then_inc(ct_copied, 1)
            act.wait_ge(hidt_psum, v + 1)
            act.activation(HIDT, bank[:, 3, 0:FQ * SLOTS], ACT.Copy).then_inc(hidt_copied, 1)
            act.wait_ge(er_used, 6 * v + 6)
            if b == 0:
                act.wait_ge(add_psum, 8 * g + 8)
            act.activation(YS[SLOTS * b:SLOTS * b + SLOTS, 0:2 * CH], bank[0:SLOTS, 4:6, :], ACT.Copy).then_inc(ye_act, 1)

        def scalar_pair(g):
            for b in range(2):
                scalar_expert(g, b, 2 * g + b)

        def scalar_end():
            act.activation(JUNK[:, 7:8], EPSC, ACT.Sqrt)
            for tt in range(TT):
                act.wait_ge(sum_done, tt + 1)
                act.activation(XT.rearrange("p j s -> p (j s)"), YACC[:, tt, :], ACT.Square, accum_out=RS[:, 8 + tt:9 + tt]).then_inc(y2_sq, 1)
                act.wait_ge(y2_sq, 1 + tt)
                act.activation(RS[:, 10 + tt:11 + tt], RS[:, 8 + tt:9 + tt], ACT.Sqrt, scale=1.0 / D, bias=EPSC).then_inc(y2_rt, 1)

        act.wait_ge(g_psum, 1)
        act.activation(GROW, bank[:, 5, :], ACT.Copy).then_inc(g_row, 1)
        act.activation(JUNK[:, 6:7], EPSC, ACT.Copy).then_inc(ye_act, 1)
        for g4 in range(4):
            gathered(g4 + 1, g4)
        with act.Fori(0, NP) as g:
            scalar_pair(g)
        act.wait_ge(count_done, 1)
        most = act.value_load(icount[0:1, 0:1], min_val=0, max_val=S)
        with act.If(most > SLOTS):
            with act.Fori(NP, ROUNDS * NP) as g:
                scalar_pair(g)
        scalar_end()

    @block.tensor
    def _(pe):
        def mm(o, l, r, start=True, stop=True):
            return pe.matmul(o, l, r, start=start, stop=stop, skip_group_check=True)

        def warm_up(n):
            for _ in range(n):
                mm(bank[:, 4, :], IDENT, TAB[:, 0:CH])

        pe.wait_ge(tab_in, 16)
        pe.wait_ge(xs_done, 2)
        for g in range(8):
            if g >= 4:
                pe.wait_ge(xt_copied, g - 3)
            for jj in range(2):
                for tt in range(TT):
                    j = 2 * g + jj
                    last = pe.transpose(bank[:, g % 4, (2 * jj + tt) * P:(2 * jj + tt + 1) * P],
                                        XS[:, tt, :].rearrange("p (q j) -> p j q", j=KC)[:, j, :], IDENT)
            last.then_inc(xt_psum, 1)
        for v in range(2):
            if v:
                pe.wait_ge(hrow_used, 2 * KC - 2)
                warm_up(3)
            pe.wait_ge(hacc_done, v + 1)
            for j in range(KC):
                last = mm(bank[:, 6 + v, j:j + 1], HACC[:, v, :].rearrange("p (q j) -> p j q", j=KC)[:, j, :], ONES[:, 0:1])
            last.then_inc(hcol_psum, 1)
        pe.wait_ge(fgate_in, 32)
        for j in range(KC):
            pe.wait_ge(ht_done, j + 1)
            mm(bank[0:16, 6, 0:S], WF[:, j, :], HT[:, j, :], start=(j == 0), stop=(j == KC - 1)).then_inc(fg_psum, 1)

        def granule(n, gq, left, b0, first):
            pe.wait_ge(lo_done, n + 1)
            lh, ll = left
            for jj in range(2):
                k = 2 * gq + jj
                if first:
                    pe.wait_ge(hl_done, k + 1)
                for tt in range(TT):
                    o, tok = bank[:, b0 + tt, :], slice(tt * P, (tt + 1) * P)
                    mm(o, lh[:, k, tok], WH[:, gq % 4, jj, :], start=(k == 0), stop=False)
                    mm(o, lh[:, k, tok], WL[:, gq % 4, jj, :], start=False, stop=False)
                    last = mm(o, ll[:, k, tok], WH[:, gq % 4, jj, :], start=False, stop=(k == KC - 1))
            last.then_inc(part_used, 1)

        def project(it, b, first=False):
            if not first:
                pe.wait_ge(ch_copied, 2 * it + (b - 1))
            for gq in range(8):
                granule(16 * it + (8 * b + gq), gq, (HH, HL), 2 * b, first and b == 0)
                if b == 0 and gq == (7 if first else 3):
                    spread(it, first)
                if isinstance(it, int) and it == 6 and b == 1 and gq == 5:
                    spread(7)

        def spread(ps, first=False):
            pe.wait_ge(acc_done, ps + 1)
            if not first:
                pe.wait_ge(mod_copied, ps)
            mm(bank[:, 4, :], ONES, AACC).then_inc(mod_psum, 1)

        for b in range(2):
            project(0, b, True)
        with pe.Fori(1, 6) as it:
            for b in range(2):
                project(it, b)
        for b in range(2):
            project(6, b)

        def late_row_added(n):
            v, j = n // KC, n % KC
            pe.wait_ge(crow_in[n % 2], 16 * (n // 2) + 16)
            for g in range(4):
                last = mm(bank[32 * g:32 * g + 32, v, :], CC[:, j, :], CRING[:, n % 2, g * CH:(g + 1) * CH], start=(j == 0), stop=False)
            last.then_inc(late_used, 1)
            if n in (KC - 1, KC + G2_EARLY - 1):
                pe.wait_ge(cbias_in, 16 * (v + 1))
                for g in range(4):
                    q = slice(32 * g, 32 * g + 1)
                    last = mm(bank[32 * g:32 * g + 32, v, :], ONES[q, 0:32], CBIAS[q, :], start=False)
                last.then_inc(late_psum, 1)

        pe.wait_ge(rope_done, 2)
        pe.wait_ge(ch_copied, 13)
        pe.wait_ge(cc_done, 1)
        late_row_added(0)
        late_row_added(1)
        for g in range(16):
            t4, hp = g // 4, g % 4
            if g >= 4:
                if g % 2 == 0:
                    pe.wait_ge(tq_act, (g - 4) // 2 + 1)
                else:
                    pe.wait_ge(tq_dve, (g - 5) // 2 + 1)
            if g == 8:
                pe.wait_ge(qk_norm, 1)
            for hh in range(2):
                for tt in range(TT):
                    o = (0, 1, 4, 5)[t4] * HW + (2 * hp + hh) * DH
                    last = pe.transpose(bank[:, tq_bank[g % 4], (2 * hh + tt) * P:(2 * hh + tt + 1) * P], RAW[:, tt, o:o + DH], IDENT)
            last.then_inc(tq_psum, 1)
            if g % 3 == 2:
                late_row_added(2 + g // 3)
        pe.wait_ge(ch_copied, 14)
        pe.wait_ge(tq_act, 8)
        pe.wait_ge(tq_dve, 8)
        pe.wait_ge(mod_copied, 8)

        def scores(k):
            kind, h, t = units[k]
            sb = bank[:, 4 + k % 2, :]
            if k >= 2:
                pe.wait_ge(st_done if units[k - 2][0] == "ret" else lmax_done, before(units[k - 2][0], k - 1))
            if kind == "ret":
                mm(sb[:, 0:S], QKT[:, 1, h, 0:P], QKT[:, 0, h, :])
                mm(sb[:, S:S + P], QKT[:, 1, h, P:S], QKT[:, 0, h, P:S]).then_inc(sc_psum, 1)
            else:
                w = P * (t + 1)
                pe.wait_ge(fkb_done, h + 1)
                if h == 0:
                    pe.wait_ge(fqb_done, 1)
                mm(sb[:, 0:w], QKT[:, 2, h, t * P:(t + 1) * P], QKT[:, 3, h, 0:w], stop=False)
                mm(sb[:, 0:w], FQB[:, t * P:(t + 1) * P], FKB[0:2 * H, h % 2, 0:w], start=False).then_inc(sc_psum, 1)

        def turn(k):
            kind, h, t = units[k]
            if kind == "fox":
                n = before("fox", k)
                pe.wait_ge(exp_done, n + 1)
                if n >= 2:
                    pe.wait_ge(pt_copied, n - 1)
                for sblk in range(t + 1):
                    last = pe.transpose(bank[:, 2 + k % 2, sblk * P:(sblk + 1) * P], PR[:, k % 2, sblk * P:(sblk + 1) * P], IDENT)
                last.then_inc(pt_psum, 1)

        def values(k):
            kind, h, t = units[k]
            ob = bank[:, 6 + k % 2, :]
            if k >= 2:
                pe.wait_ge(o_copied if units[k - 2][0] == "ret" else o_scaled, before(units[k - 2][0], k - 1))
            if kind == "ret":
                pe.wait_ge(st_done, before("ret", k) + 1)
                v = VRET[:, :, h * DH:(h + 1) * DH]
                mm(ob[:, 0:P], ST[:, k % 2, 0:P], v[:, 0, :])
                mm(ob[:, P:S], ST[:, k % 2, P:S], v[:, 0, :], stop=False)
                mm(ob[:, P:S], ST[:, k % 2, S:S + P], v[:, 1, :], start=False).then_inc(o_psum, 1)
            else:
                n = before("fox", k)
                pe.wait_ge(pt_copied, n + 1)
                for sblk in range(t + 1):
                    last = mm(ob[:, 0:P], PRT[:, k % 2, sblk * P:(sblk + 1) * P], VFOX[:, sblk, h * DH:(h + 1) * DH],
                              start=(sblk == 0), stop=(sblk == t))
                last.then_inc(o_psum, 1)

        for k in range(NU + 2):
            if k < NU:
                scores(k)
            if 1 <= k <= NU:
                turn(k - 1)
            if k >= 2:
                values(k - 2)
            if k < KC + G2_EARLY - 7:
                late_row_added(7 + k)
        for g in range(8):
            if g == 0:
                pe.wait_ge(mix_ret, 2)
                pe.wait_ge(o_scaled, 16)
                pe.wait_ge(pt_copied, 16)
            if g == 4:
                pe.wait_ge(mix_fox, 1)
            if g >= 6:
                pe.wait_ge(ml_done, g - 5)
            for jj in range(2):
                for tt in range(TT):
                    last = pe.transpose(bank[:, mt_bank[g], (2 * jj + tt) * P:(2 * jj + tt + 1) * P],
                                        MIX[:, tt, (2 * g + jj) * P:(2 * g + jj + 1) * P], IDENT)
            last.then_inc(mt_psum, 1)
        pe.wait_ge(late_row, 2)
        for cc in range(4):
            for gq in range(8):
                if cc == 0:
                    pe.wait_ge(ml_done, gq + 1)
                if cc == 3 and gq == 0:
                    pe.wait_ge(late_copied, 4)
                granule(8 * (14 + cc) + gq, gq, (MH, ML), 2 * cc, False)
                if 8 * cc + gq in late_granules:
                    i = late_granules.index(8 * cc + gq)
                    if i >= 2:
                        pe.wait_ge(late_copied, i - 1)
                    q = slice(32 * i, 32 * i + 1)
                    mm(bank[:, 6 + i % 2, :], ONES[q, :], CROW[q, 0, :]).then_inc(late_spread, 1)
        pe.wait_ge(yg_read, 2)
        pe.wait_ge(gc_done, 1)

        def g2_rows(n0, n1):
            for n in range(n0, n1):
                pe.wait_ge(grow_in[n % 2], 16 * (n // 2) + 16)
                for g in range(4):
                    last = mm(bank[32 * g:32 * g + 32, 5, :], GC[:, G2_EARLY + n, :], GRING[:, n % 2, g * CH:(g + 1) * CH], start=(n == 0), stop=False)
                last.then_inc(g_used, 1)

        g2_rows(0, 2)
        pe.wait_ge(x1_done, 2)
        warm_up(WARM_H2)
        for tt in range(TT):
            pe.wait_ge(h2_done, tt + 1)
            for j4 in range(4):
                g = 4 * tt + j4
                if tt:
                    pe.wait_ge((h2t_copied, h2t_dve)[j4 % 2], j4 // 2 + 1)
                for j in range(4 * j4, 4 * j4 + 4):
                    last = pe.transpose(bank[:, j4, (j % 4) * P:(j % 4 + 1) * P], H2[:, tt, j, :], IDENT)
                last.then_inc(h2t_psum, 1)
        for tt in range(TT):
            pe.wait_ge(h2t_copied, 2 * tt + 2)
            pe.wait_ge(h2t_dve, 2 * tt + 2)
            for j in range(KC):
                last = mm(bank[:, 6 + tt, 0:36], H2T[:, j, tt * P:(tt + 1) * P], RWS[:, j, :], start=(j == 0), stop=(j == KC - 1))
            last.then_inc(lg_psum, 1)
        g2_rows(2, KC - G2_EARLY)
        for g in range(4):
            q = slice(32 * g, 32 * g + 1)
            last = mm(bank[32 * g:32 * g + 32, 5, :], ONES[q, 0:32], CROW[q, 1, :], start=False)
        last.then_inc(g_psum, 1)
        pe.wait_ge(mk_done, 2)
        mm(bank[:, 4, 0:NE], TRI, MK[:, 0, :])
        mm(bank[:, 4, NE:2 * NE], TRI, MK[:, 1, :], stop=False)
        mm(bank[:, 4, NE:2 * NE], ONES, MK[:, 0, :], start=False)
        mm(bank[:, 4, 2 * NE:3 * NE], ONES, MK[:, 0, :], stop=False)
        mm(bank[:, 4, 2 * NE:3 * NE], ONES, MK[:, 1, :], start=False).then_inc(rank_psum, 1)

        def gather(n, first):
            pe.wait_ge(selg_done, n + 1)
            for g4 in range(4):
                if not first:
                    pe.wait_ge(xg_copied, 4 * n + (g4 - 1))
                elif g4 >= 2:
                    pe.wait_ge(xg_copied, g4 - 1)
                for j in range(4):
                    for tt in range(TT):
                        last = mm(bank[:, g4 % 2, j * P:(j + 1) * P], H2[:, tt, 4 * g4 + j, :], SELG[:, tt, :], start=(tt == 0), stop=(tt == 1))
                last.then_inc(xg_psum, 1)

        def weights_turned(g):
            pe.wait_ge(selc_done, g + 1)
            for tt in range(TT):
                last = pe.transpose(bank[:, 3, tt * P:(tt + 1) * P], SELC[:, tt, :], IDENT)
            last.then_inc(ct_psum, 1)

        def add_back(g):
            pe.wait_ge(ye_act, 2 * g + 1)
            pe.wait_ge(ye_dve, 2 * g + 1)
            pe.wait_ge(ct_copied, g + 1)
            for n in range(8):
                tt, cc = n // 4, n % 4
                pe.wait_ge(added, 8 * g + (n + 1))
                mm(bank[:, 6 + n % 2, :], SELT[:, tt * P:(tt + 1) * P], YS[:, cc * CH:(cc + 1) * CH]).then_inc(add_psum, 1)

        def expert(g, b):
            v = 2 * g + b
            for u in range(4):
                w13 = ER[:, u].rearrange("p (w j n) -> p w j n", w=2, j=4)
                if b == 0:
                    pe.wait_ge(xg_copied, 4 * g + (u + 1))
                pe.wait_ge(er_in[u], 32 * v + 32)
                for j in range(4):
                    for w in range(2):
                        k = 4 * u + j
                        last = mm(bank[SLOTS * w:SLOTS * w + SLOTS, 2, :], XT[:, k, SLOTS * b:SLOTS * b + SLOTS], w13[:, w, j, :],
                                  start=(k == 0), stop=(k == KC - 1))
                last.then_inc(er_used, 1)
            if b == 0:
                add_back(g)
            else:
                gather(g + 1, False)
                weights_turned(g)
                pe.wait_ge(ct_copied, g + 2)
            pe.wait_ge(hid_done, v + 1)
            pe.sem_inc(hid_seen, 1)
            for q in range(FQ):
                last = pe.transpose(bank[:, 3, q * SLOTS:(q + 1) * SLOTS],
                                    HID[SLOTS:P, :].rearrange("p (s q) -> p q s", q=FQ)[:, q, :], IDENT[SLOTS:P, SLOTS:P])
            last.then_inc(hidt_psum, 1)
            pe.wait_ge(hidt_copied, v + 1)
            pe.wait_ge(ye_act, v + 1)
            pe.wait_ge(ye_dve, v + 1)
            for q in range(FQ):
                u = 4 + q // 2
                w2t = ER[:, u].rearrange("p (q n) -> p q n", q=2)
                if q % 2 == 0:
                    pe.wait_ge(er_in[u], 16 * v + 16)
                for cc in range(2):
                    for w in range(2):
                        o = w * 2 * CH + cc * CH
                        last = mm(bank[SLOTS * w:SLOTS * w + SLOTS, 4 + cc, :], HIDT[:, q, :], w2t[:, q % 2, o:o + CH],
                                  start=(q == 0), stop=(q == FQ - 1))
                if q % 2 == 1:
                    last.then_inc(er_used, 1)

        pe.wait_ge(g_row, 1)
        for g, b in enumerate((2, 3, 6, 7)):
            q = slice(32 * g, 32 * g + 1)
            last = mm(bank[:, b, :], ONES[q, :], GROW[q, :])
        last.then_inc(g2_psum, 1)
        gather(0, True)
        pe.wait_ge(g2_done, 2)
        with pe.Fori(0, NP) as g:
            for b in range(2):
                expert(g, b)
        pe.wait_ge(count_done, 1)
        most = pe.value_load(icount[0:1, 0:1], min_val=0, max_val=S)
        with pe.If(most > SLOTS):
            with pe.Fori(NP, ROUNDS * NP) as g:
                for b in range(2):
                    expert(g, b)
            add_back(ROUNDS * NP)
        with pe.Else():
            add_back(NP)

    @block.gpsimd
    def _(pool):
        def low(n, gq):
            pool.wait_ge(hi_done, n + 1)
            src = WR[:, gq // 2 % 2, 2 * (gq % 2):2 * (gq % 2) + 2, :]
            pool.tensor_tensor(WL[:, gq % 4], src, WH[:, gq % 4].bitcast(F32), ALU.subtract).then_inc(lo_done, 1)

        with pool.Fori(0, 14) as c:
            for gq in range(8):
                low(8 * c + gq, gq)
        def key_bias(h):
            if h >= 2:
                pool.wait_ge(sc_psum, H + 2 * h - 2)
            pool.tensor_scalar(FKB[0:16, h % 2, :], FG[0:16, :], TAB[0:16, T_SELA + h:T_SELA + h + 1],
                               TAB[0:16, T_SELB + h:T_SELB + h + 1], ALU.mult, ALU.add).then_inc(fkb_done, 1)

        def ret_scale(t, heads):
            for h in heads:
                y = MIX[:, t, h * DH:(h + 1) * DH]
                pool.tensor_scalar(y, y, BAG[:, t * H + h, 0:1], CST[:, 6 + t, h:h + 1], ALU.subtract, ALU.mult).then_inc(ret_scaled, 1)

        def ret_gate(t):
            pool.wait_ge(ret_scaled, H * (t + 1))
            pool.tensor_tensor(MIX[:, t, 0:HW], MIX[:, t, 0:HW], GATE[:, t], ALU.mult).then_inc(mix_ret, 1)

        pool.wait_ge(mod_psum, 8)
        pool.wait_ge(fg_done, 1)
        key_bias(0)
        key_bias(1)
        for gq in range(4):
            low(8 * 14 + gq, gq)
        key_bias(2)
        key_bias(3)
        pool.wait_ge(bn_inv, 1)
        for h in range(4, H):
            key_bias(h)
            ret_scale((h - 4) // 2, range(4 * (h % 2), 4 * (h % 2) + 4))
            if h % 2 == 1:
                ret_gate((h - 4) // 2)
        for gq in range(4, 8):
            low(8 * 14 + gq, gq)
        with pool.Fori(15, 18) as c:
            for gq in range(8):
                low(8 * c + gq, gq)

    @block.vector
    def _(dve):
        st = Steps(dve, v_step)
        tt_, ts_, stt = dve.tensor_tensor, dve.tensor_scalar, dve.scalar_tensor_tensor
        st.link(dve.memset(HACC, 0.0))
        dve.memset(ABIAS, 0.0).then_inc(zeroed, 1)
        dve.memset(EPSC, EPS).then_inc(zeroed, 1)
        dve.wait_ge(ce_done, 1)
        st.link(ts_(CE, CE, 1.0, None, ALU.add))
        st.link(dve.reciprocal(CE, CE))
        st.link(tt_(CA, CV, CE, ALU.mult))
        dve.wait_ge(hbias_in, 32)

        def head(v):
            with dve.Fori(0, 4) as i:
                for u in range(4):
                    dve.wait_ge(hring_in[u], 16 * i + (64 * v + 16))
                    stt(HACC[:, v, :], HRING[:, u, :], CA[:, bass.ds(4 * i + u, 1)], HACC[:, v, :], ALU.mult, ALU.add).then_inc(hrow_used, 1)
                    dve.wait_ge(hrow_used, 4 * i + (16 * v + u + 1))

        head(0)
        dve.sem_inc(hacc_done, 1)
        dve.wait_ge(xrt_done, 1)
        st.link(dve.reciprocal(RS[:, 0:2], RS[:, 0:2]))
        for tt in range(TT):
            ts_(XS[:, tt, :], X[:, tt, :], RS[:, tt:tt + 1], None, ALU.mult).then_inc(xs_done, 1)
        head(1)
        dve.sem_inc(hacc_done, 1)
        dve.wait_ge(hcol_psum, 2)
        dve.wait_ge(small_in, 16 * 9)
        st.link(stt(A1, bank[:, 7, 0:KC], 1.0, NPRE, ALU.add, ALU.mult))
        st.link(dve.tensor_copy(SH1, bank[:, 6, 0:KC]))
        dve.wait_ge(xt_copied, 8)
        for j in range(KC):
            ts_(HT[:, j, :], HT[:, j, :], A1[:, j:j + 1], SH1[:, j:j + 1], ALU.mult, ALU.add).then_inc(ht_done, 1)
        for j in range(KC):
            dve.wait_ge(hh_done, j + 1)
            dve.wait_ge(fg_psum, j + 1)
            tt_(HL[:, j, :], HT[:, j, :], HH[:, j, :].bitcast(F32), ALU.subtract).then_inc(hl_done, 1)

        def rows(ps, first=False):
            for k in range(4):
                dve.wait_ge(aring_in[k % 2], 32 * ps + (16 * (k // 2) + 16))
                for jj in range(4):
                    src = AACC
                    if k == 0 and jj == 0:
                        dve.wait_ge(abias_in, 16 * ps + 16)
                        if not first:
                            dve.wait_ge(mod_psum, ps)
                        src = ABIAS
                    ins = stt(AACC, ARING[:, k % 2, jj, :], CA[:, 4 * k + jj:4 * k + jj + 1], src, ALU.mult, ALU.add)
                    if jj < 3:
                        st.link(ins)
                        if k == 0 and jj == 0:
                            dve.sem_inc(abias_used, 1)
                    else:
                        ins.then_inc(arow_used, 1)
                        dve.wait_ge(arow_used, 4 * ps + (k + 1))
                        if k == 3:
                            dve.sem_inc(acc_done, 1)

        ROWS = 12

        def tensor_of(it, tt):
            return RAW[:, tt, bass.ds(it * HW, HW)].rearrange("p (h d) -> p h d", h=H)

        rows(0, True)
        z, az, lnv = SCR[0:16, 0, 3 * S:4 * S], SCR[0:16, 0, 0:S], SCR[0:16, 0, 2 * S:3 * S]
        one, mn = SCR[0:16, 1, 0:S], SCR[0:16, 1, S:2 * S]
        dve.wait_ge(fg_psum, KC)
        st.link(ts_(z, bank[0:16, 6, 0:S], FBIAS[0:16, :], None, ALU.add))
        st.link(ts_(mn, z, -1.0, None, ALU.mult))
        tt_(az, z, mn, ALU.max).then_inc(fg_abs, 1)
        dve.wait_ge(fg_abs, 1)
        st.link(ts_(mn, z, 0.0, None, ALU.min))
        st.link(dve.memset(one, 1.0))
        dve.wait_ge(fg_ln, 1)
        st.link(tt_(z, mn, lnv, ALU.subtract))
        dve.tensor_tensor_scan(FG[0:16, :], one, z, 0.0, ALU.mult, ALU.add).then_inc(fg_done, 1)
        dve.wait_ge(fg_done, 1)

        with dve.Fori(0, 2) as it, st.loop(it, ROWS + 12, 2):
            rows(it + 1)
            dve.wait_ge(ch_copied, 2 * it + 2)
            for tt in range(TT):
                x = tensor_of(it, tt)
                cos, sin = (TAB[:, o + tt * 64:o + tt * 64 + 64].unsqueeze(1).to_broadcast([P, H, 64]) for o in (T_COS, T_SIN))
                lo, hi = x[:, :, 0:64], x[:, :, 64:128]
                t1, t2 = (SCR[:, tt, i * CH:(i + 1) * CH].rearrange("p (h d) -> p h d", h=H) for i in range(2))
                st.link(tt_(t1, lo, sin, ALU.mult))
                st.link(tt_(t2, hi, sin, ALU.mult))
                st.link(tt_(lo, lo, cos, ALU.mult))
                st.link(tt_(hi, hi, cos, ALU.mult))
                st.link(tt_(lo, lo, t2, ALU.subtract))
                st.link(tt_(hi, hi, t1, ALU.add))
        dve.sem_inc(rope_done, 1)
        dve.sem_inc(rope_done, 1)
        with dve.Fori(2, 5) as it, st.loop(it - 2, ROWS, 3):
            rows(it + 1)
        dve.wait_ge(gate_exp, 1)
        dve.wait_ge(gnw_in, 16)
        st.link(ts_(SCR, SCR, 1.0, None, ALU.add))
        st.link(dve.reciprocal(SCR, SCR))
        st.link(tt_(GATE, GATE, SCR, ALU.mult))
        st.link(tt_(GATE, GATE, GNW.unsqueeze(1).to_broadcast([P, TT, HW]), ALU.mult))
        dve.sem_inc(gnw_used, 1)
        rows(6)
        with dve.Fori(4, 6) as it, st.loop(it - 4, 4, 2):
            dve.wait_ge(ch_copied, 2 * it + 2)
            for tt in range(TT):
                x = tensor_of(it, tt)
                sq = SCR[:, tt, :].rearrange("p (h d) -> p h d", h=H)
                st.link(tt_(sq, x, x, ALU.mult))
                st.link(dve.tensor_reduce(SS[:, bass.ds((it - 4) * 16 + tt * H, H)], sq, AX_X, ALU.add))
        dve.sem_inc(qk_sq, 1)
        rows(7)
        dve.wait_ge(qk_rt, 1)
        st.link(dve.reciprocal(RS, RS))
        for i in range(2):
            for tt in range(TT):
                x = RAW[:, tt, (4 + i) * HW:(5 + i) * HW].rearrange("p (h d) -> p h d", h=H)
                r = RS[:, i * 16 + tt * H:i * 16 + tt * H + H].unsqueeze(2).to_broadcast([P, H, DH])
                st.link(tt_(x, x, r, ALU.mult))
        st.link(ts_(QKN[:, 0:1], QKN[:, 0:1], QK_SCALE, None, ALU.mult))
        dve.sem_inc(qk_norm, 1)

        dve.tensor_copy(CC, CA.unsqueeze(2).to_broadcast([P, KC, 32])).then_inc(cc_done, 1)
        for g in range(1, 16, 2):
            dve.wait_ge(tq_psum, g + 1)
            t4, hp = g // 4, g % 4
            dst = QKT[:, t4, 2 * hp:2 * hp + 2, :].rearrange("p h s -> p (h s)")
            if t4 < 2:
                dve.tensor_copy(dst, bank[:, tq_bank[g % 4], :]).then_inc(tq_dve, 1)
            else:
                ts_(dst, bank[:, tq_bank[g % 4], :], QKN[:, t4 - 2:t4 - 1], None, ALU.mult).then_inc(tq_dve, 1)
        ts_(FQB, FG[0:16, :], TAB[0:16, T_QMUL:T_QMUL + 1], TAB[0:16, T_QADD:T_QADD + 1], ALU.mult, ALU.add).then_inc(fqb_done, 1)

        dve.wait_ge(dec_in, 16)

        def first(k):
            kind, h, t = units[k]
            sb = bank[:, 4 + k % 2, :]
            dve.wait_ge(sc_psum, k + 1)
            if kind == "ret":
                if k >= 2:
                    dve.wait_ge(o_psum, k - 1)
                st.link(tt_(ST[:, k % 2, 0:S], sb[:, 0:S], DEC[:, h, :], ALU.mult))
                tt_(ST[:, k % 2, S:S + P], sb[:, S:S + P], DEC[:, h, 0:P], ALU.mult).then_inc(st_done, 1)
            else:
                n = before("fox", k)
                w = P * (t + 1)
                if n >= 2:
                    dve.wait_ge(pt_psum, n - 1)
                mx = CST[:, t, h:h + 1]
                mask = TAB[:, T_MASK:T_MASK + S] if t else TAB[:, T_MASK + P:T_MASK + S]
                st.link(tt_(PR[:, k % 2, 0:w], sb[:, 0:w], mask, ALU.add))
                st.link(dve.tensor_reduce(mx, PR[:, k % 2, 0:w], AX_X, ALU.max))
                ts_(mx, mx, -1.0, None, ALU.mult).then_inc(lmax_done, 1)

        def second(k):
            kind, h, t = units[k]
            if kind == "fox":
                dve.wait_ge(exp_done, before("fox", k) + 1)
                st.link(dve.reciprocal(CST[:, 10 + t, h:h + 1], CST[:, 2 + t, h:h + 1]))

        def third(k):
            kind, h, t = units[k]
            if kind == "fox":
                dve.wait_ge(o_psum, k + 1)
                ts_(MIX[:, t, HW + h * DH:HW + (h + 1) * DH], bank[:, 6 + k % 2, 0:P], CST[:, 10 + t, h:h + 1], None,
                    ALU.mult).then_inc(o_scaled, 1)

        def ret_stats(h):
            dve.wait_ge(o_copied, h + 1)
            for t in range(TT):
                last = dve.bn_stats(BST[:, t * H + h, :], MIX[:, t, h * DH:(h + 1) * DH])
            st.link(last)
            for t in range(TT):
                last = dve.bn_aggr(BAG[:, t * H + h, :], BST[:, t * H + h, :])
            st.link(last)

        for k in range(NU + 2):
            if k < NU:
                first(k)
            if 1 <= k <= NU:
                second(k - 1)
            if k >= 2:
                third(k - 2)
            if 4 <= k < 4 + H:
                ret_stats(k - 4)
            if k == 4 + H:
                dve.sem_inc(bn_done, 1)
            if k == 6 + H:
                dve.wait_ge(bn_rt, 1)
                dve.reciprocal(CST[:, 6:8, 0:8], CST[:, 6:8, 0:8]).then_inc(bn_inv, 1)
        dve.wait_ge(fo_rt, 1)
        dve.wait_ge(onw_in, 16)
        st.link(dve.reciprocal(CST[:, 8:10, 0:8], CST[:, 8:10, 0:8]))
        for t in range(TT):
            for h in range(H):
                y = MIX[:, t, HW + h * DH:HW + (h + 1) * DH]
                last = stt(y, y, CST[:, 8 + t, h:h + 1], ONW[:, h * DH:(h + 1) * DH], ALU.mult, ALU.mult)
        last.then_inc(mix_fox, 1)
        for g in range(8):
            dve.wait_ge(mt_copied, g + 1)
            tt_(ML[:, 2 * g:2 * g + 2, :].rearrange("p j s -> p (j s)"), bank[:, mt_bank[g], :],
                MH[:, 2 * g:2 * g + 2, :].bitcast(F32).rearrange("p j s -> p (j s)"), ALU.subtract).then_inc(ml_done, 1)

        dve.wait_ge(mod_copied, 8)
        dve.wait_ge(nw_in, 16)
        stt(G1B, G1B, 0.0, NW, ALU.add, ALU.mult).then_inc(nw_used, 1)
        dve.wait_ge(late_copied, 4)
        dve.wait_ge(nw_in, 32)
        stt(SC2B, SC2B, 1.0, NW, ALU.add, ALU.mult).then_inc(nw_used, 1)
        dve.wait_ge(nw_used, 2)
        for cc in range(4):
            for tt in range(TT):
                yb = bank[:, 2 * cc + tt, :]
                dve.wait_ge(y_sq, 2 * cc + tt + 1)
                st.link(tt_(yb, yb, G1B[:, cc * CH:(cc + 1) * CH], ALU.mult))
        dve.tensor_reduce(RS[:, 2:4], SS[:, 0:8].rearrange("p (t c) -> p t c", t=TT), AX_X, ALU.add).then_inc(yg_done, 1)
        dve.wait_ge(yg_done, 1)
        dve.wait_ge(yg_done, 1)
        dve.tensor_copy(GC, CA.unsqueeze(2).to_broadcast([P, KC, 32])).then_inc(gc_done, 1)
        dve.wait_ge(y_rt, 1)
        st.link(dve.reciprocal(RS[:, 0:2], RS[:, 0:2]))
        by_j = lambda row: row.rearrange("p (q j) -> p j q", j=KC)

        def x1(tt):
            yg = bank[:, :, :].rearrange("p (c t) n -> p t c n", t=TT)[:, tt]
            xv = X[:, tt, :].rearrange("p (c n) -> p c n", c=4)
            stt(xv, yg, RS[:, tt:tt + 1], xv, ALU.mult, ALU.add).then_inc(x1_done, 1)
            dve.wait_ge(x1_done, tt + 1)

        def h2_product(tt):
            st.link(tt_(H2[:, tt], by_j(X[:, tt, :]), by_j(SC2B), ALU.mult))

        def h2(tt):
            dve.wait_ge(x1_rt, tt + 1)
            st.link(dve.reciprocal(RS[:, 6 + tt:7 + tt], RS[:, 6 + tt:7 + tt]))
            stt(H2[:, tt], H2[:, tt], RS[:, 6 + tt:7 + tt], by_j(SH2B), ALU.mult, ALU.add).then_inc(h2_done, 1)

        x1(0)
        h2_product(0)
        x1(1)
        dve.sem_inc(yg_read, 2)
        h2(0)
        h2_product(1)
        h2(1)

        def h2_turned(tt, j4):
            dve.wait_ge(h2t_psum, 4 * tt + j4 + 1)
            dve.tensor_copy(H2T[:, 4 * j4:4 * j4 + 4, tt * P:(tt + 1) * P],
                            bank[:, j4, :].rearrange("p (j s) -> p j s", j=4)).then_inc(h2t_dve, 1)

        for tt in range(TT):
            for j4 in (1, 3):
                h2_turned(tt, j4)

        i32x = IOTA[:, 0:NE]
        st.link(dve.memset(CPAD, -BIG))
        for tt in range(TT):
            c = lambda n: RC[:, tt, n:n + 1]
            dve.wait_ge(lg_psum, tt + 1)
            st.link(tt_(LG[:, tt, :], bank[:, 6 + tt, 0:36], RBS, ALU.add))
            st.link(dve.tensor_copy(CPAD[:, tt, 0:NG], LG[:, tt, 0:NG]))
            st.link(dve.max(M8[:, tt, :], CPAD[:, tt, :]))
            ts_(c(0), M8[:, tt, 0:1], -1.0, None, ALU.mult).then_inc(cmax_done, 1)
            st.link(dve.max_index(etop[:, 0, :], M8[:, tt, :], CPAD[:, tt, :]))
            st.link(dve.tensor_copy(c(5), etop[:, 0, 0:1]))
            st.link(ts_(GE[:, tt, :], IOTA[:, 0:NG], c(5), None, ALU.is_equal))
            st.link(ts_(GE[:, tt, :], GE[:, tt, :], BIG, -BIG, ALU.mult, ALU.add))
            st.link(tt_(FM[:, tt, :].rearrange("p (g e) -> p g e", g=NG), LG[:, tt, NG:36].rearrange("p (g e) -> p g e", g=NG),
                        GE[:, tt, :].unsqueeze(2).to_broadcast([P, NG, EG]), ALU.add))
            st.link(dve.max(F8[:, tt, :], FM[:, tt, :]))
            tt_(c(3), F8[:, tt, 1:2], F8[:, tt, 0:1], ALU.subtract).then_inc(fdif_done, 1)
            st.link(dve.max_index(etop[:, 1, :], F8[:, tt, :], FM[:, tt, :]))
            st.link(dve.tensor_copy(RC[:, tt, 6:8], etop[:, 1, 0:2]))
            st.link(ts_(O1[:, tt, :], i32x, c(6), None, ALU.is_equal))
            st.link(ts_(O2[:, tt, :], i32x, c(7), None, ALU.is_equal))
            tt_(MK[:, tt, :], O1[:, tt, :], O2[:, tt, :], ALU.add).then_inc(mk_done, 1)
            dve.wait_ge(cexp_done, tt + 1)
            dve.wait_ge(fexp_done, tt + 1)
            st.link(stt(c(8), c(4), 1.0, c(1), ALU.add, ALU.mult))
            st.link(dve.reciprocal(c(9), c(8)))
            st.link(tt_(c(10), c(9), c(4), ALU.mult))
            st.link(ts_(CW[:, tt, :], O1[:, tt, :], c(9), None, ALU.mult))
            st.link(stt(CW[:, tt, :], O2[:, tt, :], c(10), CW[:, tt, :], ALU.mult, ALU.add))
        st.link(dve.memset(SLOT, -1.0))
        st.link(dve.memset(COEF, 0.0))
        for tt in range(TT):
            for r in range(ROUNDS):
                last = dve.tensor_copy(COEF[:, tt, r * NE:(r + 1) * NE], CW[:, tt, :])
        st.link(last)
        dve.wait_ge(h2_done, 2)
        dve.memset(YS, 0.0).then_inc(ye_dve, 1)
        dve.wait_ge(rank_psum, 1)
        dve.wait_ge(mk_done, 2)
        for tt in range(TT):
            last = stt(SLOT[:, tt, 0:NE], bank[:, 4, tt * NE:(tt + 1) * NE], 1.0, MK[:, tt, :], ALU.add, ALU.mult)
        st.link(last)
        st.link(ts_(SLOT[:, :, 0:NE], SLOT[:, :, 0:NE], -1.0, None, ALU.add))

        def gather_matrix(n):
            for tt in range(TT):
                for b in range(2):
                    last = ts_(SELG[:, tt, b * SLOTS:(b + 1) * SLOTS], IOTA, SLOT[:, tt, bass.ds(2 * n + b, 1)], None, ALU.is_equal)
            last.then_inc(selg_done, 1)

        def weight_matrix(n):
            for tt in range(TT):
                for b in range(2):
                    last = ts_(SELC[:, tt, b * SLOTS:(b + 1) * SLOTS], IOTA, SLOT[:, tt, bass.ds(2 * n + b, 1)],
                               COEF[:, tt, bass.ds(2 * n + b, 1)], ALU.is_equal, ALU.mult)
            last.then_inc(selc_done, 1)

        def add_back(g, last=False):
            for n in range(8):
                tt, cc = n // 4, n % 4
                y = YACC[:, tt, cc * CH:(cc + 1) * CH]
                dve.wait_ge(add_psum, 8 * g + (n + 1))
                tt_(y, bank[:, 6 + n % 2, :], y, ALU.add).then_inc(added, 1)
                if last and n % 4 == 3:
                    dve.wait_ge(added, 8 * g + (n + 3))
                    dve.sem_inc(sum_done, 1)

        def vector_expert(g, b, v):
            dve.wait_ge(silu_done, v + 1)
            tt_(HID[SLOTS:P, :], SG[SLOTS:P, :], bank[SLOTS:P, 2, :], ALU.mult).then_inc(hid_done, 1)
            if b == 0:
                weight_matrix(g)
                gather_matrix(g + 1)
                add_back(g)
            dve.wait_ge(er_used, 6 * v + 6)
            dve.tensor_copy(YS[SLOTS * b:SLOTS * b + SLOTS, 2 * CH:4 * CH], bank[SLOTS:P, 4:6, :].rearrange("p b n -> p (b n)")).then_inc(ye_dve, 1)

        gather_matrix(0)
        dve.wait_ge(g2_psum, 1)
        dve.wait_ge(nw2_in, 16)
        for n, b in enumerate((2, 6)):
            c = slice(n * HW, (n + 1) * HW)
            tt_(G2B[:, c], bank[:, b:b + 2, :].rearrange("p b n -> p (b n)"), NW2[:, c], ALU.mult).then_inc(g2_done, 1)
        for r in range(1, ROUNDS):
            last = ts_(SLOT[:, :, r * NE:(r + 1) * NE], SLOT[:, :, 0:NE], -float(r * SLOTS), None, ALU.add)
        st.link(last)
        st.link(dve.tensor_reduce(JUNK[:, 4:5], bank[:, 4, 2 * NE:3 * NE], AX_X, ALU.max))
        dve.tensor_copy(icount[:, 0:1], JUNK[:, 4:5]).then_inc(count_done, 1)
        dve.memset(SELT, 0.0).then_inc(ct_copied, 1)
        dve.memset(YACC[:, 0, :], 0.0).then_inc(added, 1)
        dve.memset(YACC[:, 1, :], 0.0).then_inc(added, 1)
        with dve.Fori(0, NP) as g:
            for b in range(2):
                vector_expert(g, b, 2 * g + b)
        most = dve.value_load(icount[0:1, 0:1], min_val=0, max_val=S)
        with dve.If(most > SLOTS):
            with dve.Fori(NP, ROUNDS * NP) as g:
                for b in range(2):
                    vector_expert(g, b, 2 * g + b)
            add_back(ROUNDS * NP, last=True)
        with dve.Else():
            add_back(NP, last=True)
        dve.wait_ge(g2_done, 2)
        for tt in range(TT):
            st.link(tt_(YG[:, tt, :], YACC[:, tt, :], G2B, ALU.mult))
        for tt in range(TT):
            dve.wait_ge(y2_rt, tt + 1)
            st.link(dve.reciprocal(RS[:, 10 + tt:11 + tt], RS[:, 10 + tt:11 + tt]))
            for half in range(2):
                c = slice(half * HW, (half + 1) * HW)
                stt(X[:, tt, c], YG[:, tt, c], RS[:, 10 + tt:11 + tt], X[:, tt, c], ALU.mult, ALU.add).then_inc(res_done, 1)


_INS = ["x", "c", "ada_w", "ada_b", "norm_pre_mix", "norm_post_mix", "w_in", "fox_f_bias", "ret_gn_w",
        "fox_qn_w", "fox_kn_w", "fox_on_w", "w_out", "norm_pre_ffn", "norm_post_ffn",
        "router_coarse_w", "router_coarse_b", "router_fine_w", "router_fine_b", "w1", "w3", "w2"]


def kernel(**inputs):
    import numpy as _np
    import concourse.bacc as _bacc
    from concourse import mybir as _mybir
    from concourse.bass_utils import run_bass_kernel_spmd as _run

    nc = _bacc.Bacc("TRN2", target_bir_lowering=False, num_devices=1)
    arrays = {f"in_{name}_dram": _np.ascontiguousarray(inputs[name]) for name in _INS}
    arrays["shape_table_dram"], arrays["decay_table_dram"] = shape_tables()
    args = {n: nc.dram_tensor(n, v.shape, _mybir.dt.from_np(v.dtype), kind="ExternalInput").ap() for n, v in arrays.items()}
    x = arrays["in_x_dram"]
    out = nc.dram_tensor("out_dram", x.shape, _mybir.dt.from_np(x.dtype), kind="ExternalOutput").ap()
    build(nc, {n: args[f"in_{n}_dram"] for n in _INS}, args["shape_table_dram"], args["decay_table_dram"], out)
    r = _run(nc, [arrays], core_ids=[0])
    return r.results[0]["out_dram"]
```

```python
from contextlib import ExitStack, contextmanager

import numpy as np

import concourse.bass as bass
from concourse import mybir

F32 = mybir.dt.float32
F32R = mybir.dt.float32r
I32 = mybir.dt.int32
U32 = mybir.dt.uint32
ALU = mybir.AluOpType
ACT = mybir.ActivationFunctionType
AX_X = mybir.AxisListType.X

P = 128
S, D = 256, 2048
TT = S // P
KC = D // P
DH = 128
H = 8
HW = H * DH
CH = 512
NT = 7
FE = 512
FQ = FE // P
NG, EG = 4, 8
NE = NG * EG
SLOTS = 64
WARM_H2, WARM_RANK, WARM_GATHER = 4, 1, 4
PW = 736
PASSES = 7
ROUNDS = S // SLOTS
NP = NE // 2
NV = ROUNDS * NE
EPS = 1e-6
BIG = 1e30
ROPE_BASE = 10000.0
QK_SCALE = float(DH) ** -0.5

T_ID = 0
T_COS = T_ID + P
T_SIN = T_COS + TT * 64
T_MASK = T_SIN + TT * 64
T_TRI = T_MASK + 2 * P
T_IOTA = T_TRI + P
T_SELA = T_IOTA + SLOTS
T_SELB = T_SELA + H
T_QMUL = T_SELB + H
T_QADD = T_QMUL + 1
T_ONE = T_QADD + 1
TABLE = T_ONE + P


def shape_tables():
    t = np.zeros((P, TABLE), np.float32)
    t[:, T_ID:T_ID + P] = np.eye(P, dtype=np.float32)
    inv = np.float32(ROPE_BASE) ** (-np.arange(0, DH, 2, dtype=np.float32) / np.float32(DH))
    angle = np.arange(S, dtype=np.float32)[:, None] * inv[None, :].astype(np.float32)
    for tt in range(TT):
        t[:, T_COS + tt * 64:T_COS + tt * 64 + 64] = np.cos(angle[tt * P:(tt + 1) * P])
        t[:, T_SIN + tt * 64:T_SIN + tt * 64 + 64] = np.sin(angle[tt * P:(tt + 1) * P])
    r = np.arange(P)
    t[:, T_MASK + P:T_MASK + 2 * P] = np.where(r[None, :] <= r[:, None], 0.0, -BIG)
    t[:, T_TRI:T_TRI + P] = r[:, None] < r[None, :]
    t[:, T_IOTA:T_IOTA + SLOTS] = np.arange(SLOTS)
    for h in range(H):
        t[h, T_SELA + h] = 0.0
        t[h, T_SELB + h] = 1.0
        t[H + h, T_SELA + h] = -1.0
    t[0:H, T_QMUL] = 1.0
    t[H:2 * H, T_QADD] = 1.0
    t[:, T_ONE:T_ONE + P] = 1.0
    s = np.arange(P)[:, None]
    q = np.arange(S)[None, :]
    decay = np.zeros((P, H, S), np.float32)
    for h in range(H):
        lg = np.log1p(-np.exp2(-5.0 - h))
        decay[:, h, :] = np.where(q >= s, np.exp(lg * np.maximum(q - s, 0)), 0.0) * QK_SCALE
    return t, decay.reshape(P, H * S)


class Steps:

    def __init__(self, eng, sem):
        self.eng, self.sem, self.n, self.past = eng, sem, 0, 0

    def link(self, ins):
        ins.then_inc(self.sem, 1)
        self.n += 1
        self.eng.wait_ge(self.sem, self.past + self.n)

    @contextmanager
    def loop(self, i, per, count, first=0):
        n0 = self.n
        outer = self.past
        self.past = self.past + (i - first) * per if first else self.past + i * per
        yield
        assert self.n - n0 == per, (self.n - n0, per)
        self.n = n0 + per * count
        self.past = outer


def build(nc, a, table, decay_table, out):
    ctx = ExitStack()

    def sem(name):
        return ctx.enter_context(nc.semaphore(name))

    KB = 256
    base = 17376
    arena = nc.alloc_sbuf_tensor_at("arena", [P, 207 * KB], F32, offset=base)
    split_at = {"wh": (64, 4 * 2 * CH), "wl": (176, 4 * 2 * CH), "hh": (153, KC * S), "hl": (137, KC * S),
                "mh": (144, KC * S), "ml": (160, KC * S)}
    rounded = {n: nc.alloc_sbuf_tensor_at(f"rounded_{n}", [P, cols], F32R, offset=base + kb * 1024)
               for n, (kb, cols) in split_at.items()}
    plain_at = {"w_units": (48, 2 * 4 * CH), "h_columns": (137, KC * S)}
    plain = {n: nc.alloc_sbuf_tensor_at(n, [P, cols], F32, offset=base + kb * 1024) for n, (kb, cols) in plain_at.items()}
    icount = ctx.enter_context(nc.sbuf_tensor("icount", [P, 8], I32))
    etop = ctx.enter_context(nc.sbuf_tensor("etop", [P, 2, 8], U32))
    bank = ctx.enter_context(nc.psum_tensor("bank", [P, 8, CH], F32))

    def at(kb, cols):
        o = int(kb * KB)
        return arena[:, o:o + cols]

    WH, WL = (rounded[n][:, :].rearrange("p (s j n) -> p s j n", s=4, j=2) for n in ("wh", "wl"))
    HH, HL, MH, ML = (rounded[n][:, :].rearrange("p (j s) -> p j s", j=KC) for n in ("hh", "hl", "mh", "ml"))

    X = at(0, TT * D).rearrange("p (t d) -> p t d", t=TT)
    MOD = at(16, 4 * D)
    MOD_EARLY = PASSES * PW
    G1B, SH2B, SC2B, G2B = (MOD[:, i * D:(i + 1) * D] for i in range(4))
    WR = plain["w_units"][:, :].rearrange("p (u j n) -> p u j n", u=2, j=4)
    HRING = at(80, 4 * D).rearrange("p (u n) -> p u n", u=4)
    HACC = at(112, 2 * D).rearrange("p (v n) -> p v n", v=2)
    XS = at(176, TT * D).rearrange("p (t d) -> p t d", t=TT)
    HT = plain["h_columns"][:, :].rearrange("p (j s) -> p j s", j=KC)
    RAW = at(80, TT * NT * HW).rearrange("p (t n) -> p t n", t=TT)
    ARING = at(36, 2 * 2 * PW).rearrange("p (u j n) -> p u j n", u=2, j=2)
    ABIAS = at(172, PW)
    SCR = at(192, 2 * HW).rearrange("p (t n) -> p t n", t=TT)
    GNW = at(32, HW)
    AACC = at(169, PW)
    WF = at(136, KC * 16).rearrange("p (j n) -> p j n", j=KC)
    FG = at(175, S)
    QKT = at(137, 4 * H * S).rearrange("p (a h s) -> p a h s", a=4, h=H)
    MIX = RAW[:, :, 0:2 * HW]
    VRET, GATE, VFOX = (RAW[:, :, i * HW:(i + 1) * HW] for i in (2, 3, 6))
    ST = RAW[:, 0, 4 * HW:4 * HW + 768].rearrange("p (b n) -> p b n", b=2)
    PR = RAW[:, 0, 4 * HW + 768:5 * HW + 256].rearrange("p (b n) -> p b n", b=2)
    PRT = RAW[:, 0, 5 * HW + 256:5 * HW + 768].rearrange("p (b n) -> p b n", b=2)
    FQB = RAW[0:2 * H, 0, 5 * HW + 768:6 * HW]
    ONW = RAW[:, 1, 4 * HW:5 * HW]
    BST = RAW[:, 1, 5 * HW:5 * HW + 16 * 6].rearrange("p (u n) -> p u n", n=6)
    BAG = RAW[:, 1, 5 * HW + 128:5 * HW + 160].rearrange("p (u n) -> p u n", n=2)
    CST = RAW[:, 1, 5 * HW + 256:5 * HW + 512].rearrange("p (a u) -> p a u", a=16)
    CSQ = RAW[:, 1, 5 * HW + 512:5 * HW + 640]
    FKB = at(169, 2 * S).rearrange("p (b s) -> p b s", b=2)
    HALF = (4 * D - MOD_EARLY) // 2
    late_groups = ((0, HALF - 2 * CH), (HALF - 2 * CH, CH), (HALF - CH, CH))
    CRING = at(48 - 8 * HALF / 1024, 2 * HALF).rearrange("p (u n) -> p u n", u=2)
    CC = at(171, KC * 32).rearrange("p (j m) -> p j m", m=32)
    CBIAS = at(173, CH)
    CROW = at(44, 2 * CH).rearrange("p (v n) -> p v n", v=2)
    DEC = at(192, H * S).rearrange("p (h s) -> p h s", h=H)
    NW = at(192, D)
    NW2 = at(32, D)
    ER = at(80, 6 * 8 * CH).rearrange("p (u n) -> p u n", u=6)
    H2 = at(176, TT * D).rearrange("p (t j q) -> p t j q", t=TT, j=KC)
    YG = at(176, TT * D).rearrange("p (t d) -> p t d", t=TT)
    H2T = at(48, KC * S).rearrange("p (j s) -> p j s", j=KC)
    YACC = at(64, TT * D).rearrange("p (t d) -> p t d", t=TT)
    XT = at(16, KC * P).rearrange("p (j s) -> p j s", j=KC)
    YS = at(24, D)
    SG = at(48, FE)
    HID = at(50, FE)
    HIDT = at(52, FQ * SLOTS).rearrange("p (q s) -> p q s", q=FQ)
    SELG = at(53, TT * P).rearrange("p (t s) -> p t s", t=TT)
    SELC = at(54, TT * P).rearrange("p (t s) -> p t s", t=TT)
    SELT = at(55, S)
    SLOT = at(192, TT * (NV + 2)).rearrange("p (t e) -> p t e", t=TT)
    COEF = at(194, TT * (NV + 2)).rearrange("p (t e) -> p t e", t=TT)
    used = [200 * KB]

    def small(cols):
        used[0] += cols
        assert used[0] <= 207 * KB, used
        return arena[:, used[0] - cols:used[0]]

    TAB = small(TABLE)
    IDENT = TAB[:, T_ID:T_ID + P]
    ONES = TAB[:, T_ONE:T_ONE + P]
    TRI = TAB[:, T_TRI:T_TRI + P]
    IOTA = TAB[:, T_IOTA:T_IOTA + SLOTS]
    CV, CE, CA, NPRE, SH1, A1 = (small(KC) for _ in range(6))
    SS, RS = small(32), small(32)
    QKN, FBIAS, EPSC = small(2), small(1), small(1)
    RWS = small(KC * 36).rearrange("p (j n) -> p j n", j=KC)
    RBS = small(36)
    W = [196 * KB]

    def work(cols):
        W[0] += cols
        return arena[:, W[0] - cols:W[0]]

    LG = work(TT * 36).rearrange("p (t n) -> p t n", t=TT)
    CPAD = work(TT * 8).rearrange("p (t n) -> p t n", t=TT)
    M8 = work(TT * 8).rearrange("p (t n) -> p t n", t=TT)
    F8 = work(TT * 8).rearrange("p (t n) -> p t n", t=TT)
    GE = work(TT * 4).rearrange("p (t n) -> p t n", t=TT)
    FM = work(TT * NE).rearrange("p (t n) -> p t n", t=TT)
    O1 = work(TT * NE).rearrange("p (t n) -> p t n", t=TT)
    O2 = work(TT * NE).rearrange("p (t n) -> p t n", t=TT)
    CW = work(TT * NE).rearrange("p (t n) -> p t n", t=TT)
    MK = work(TT * NE).rearrange("p (t n) -> p t n", t=TT)
    RC = work(TT * 16).rearrange("p (t n) -> p t n", t=TT)
    JUNK = work(8)

    mod_sum = bank[:, 4:6, :].rearrange("p b n -> p (b n)")[:, 0:PW]

    x_v = a["x"][0].rearrange("(t p) d -> p t d", p=P)
    out_v = out[0].rearrange("(t p) d -> p t d", p=P)
    ada_v = a["ada_w"][0].rearrange("(p j) n -> p j n", j=KC)
    win_v = a["w_in"][0].rearrange("(p j) n -> p j n", j=KC)
    wout_v = a["w_out"][0].rearrange("(j p) n -> p j n", p=P)
    w1_v = a["w1"][0].rearrange("e (p j) n -> p e j n", j=KC)
    w3_v = a["w3"][0].rearrange("e (p j) n -> p e j n", j=KC)
    w2_v = a["w2"][0].rearrange("e (p q) n -> p e q n", q=FQ)

    def col(ap):
        return ap.rearrange("a (p n) -> (a p) n", n=1)

    def across(ap, n=P):
        return ap.broadcast_to([n, ap.shape[-1]])

    v_step, s_step = sem("vector_step"), sem("scalar_step")
    tab_in, c_in, x_in, small_in, fgate_in, gnw_in = (sem(n) for n in (
        "table_in", "c_in", "x_in", "small_in", "fgate_in", "gnw_in"))
    dec_in, onw_in, hbias_in, abias_in = sem("decay_in"), sem("onw_in"), sem("hbias_in"), sem("abias_in")
    nw_in = sem("normw_in")
    hring_in = [sem(f"head_rows_in{u}") for u in range(4)]
    aring_in = [sem(f"ada_rows_in{u}") for u in range(2)]
    wr_in = [sem(f"w_unit_in{u}") for u in range(2)]
    crow_in = [sem(f"late_rows_in{u}") for u in range(2)]
    cbias_in = sem("late_bias_in")
    nw2_in = sem("norm_post_ffn_in")
    er_in = [sem(f"expert_unit_in{u}") for u in range(6)]
    out_done = sem("out_done")
    zeroed, ce_done, ca_done, hrow_used = sem("zeroed"), sem("c_exp_done"), sem("c_act_done"), sem("head_rows_used")
    xsq_done, xrt_done, xs_done = sem("x_squares_done"), sem("x_root_done"), sem("x_scaled")
    xt_psum, xt_copied = sem("x_transposed"), sem("x_transposes_copied")
    hacc_done, hcol_psum, ht_done = sem("head_sum_done"), sem("head_columns_ready"), sem("h_ready")
    arow_used, abias_used, acc_done = sem("ada_rows_used"), sem("ada_bias_used"), sem("ada_sum_done")
    mod_psum, mod_copied = sem("mod_ready"), sem("mod_copied")
    hi_done, lo_done, part_used, ch_copied = (sem(n) for n in (
        "high_part_done", "low_part_done", "parts_used", "chunk_copied"))
    hh_done, hl_done, ml_done = sem("h_high_done"), sem("h_low_done"), sem("mix_low_done")
    cc_done, late_used, late_row, late_spread, late_copied = (sem(n) for n in (
        "late_factors_done", "late_rows_used", "late_sums_copied", "late_sums_spread", "late_vectors_copied"))
    yg_pool = sem("first_tile_multiplied")
    late_bias, g2_done = sem("late_bias_used"), sem("g2_done")
    fg_psum, fg_abs, fg_exp, fg_ln, fg_done = (sem(n) for n in (
        "forget_ready", "forget_abs", "forget_exp", "forget_ln", "forget_done"))
    gate_exp, gnw_used = sem("gate_exp"), sem("gnw_used")
    qk_sq, qk_rt, rope_done, qk_norm = sem("qk_squares"), sem("qk_root"), sem("rope_done"), sem("qk_normed")
    tq_psum, tq_act, tq_dve = sem("qk_transposed"), sem("qk_copied_scalar"), sem("qk_copied_vector")
    fqb_done, fkb_done = sem("query_bias_done"), sem("key_bias_done")
    sc_psum, st_done, lmax_done, exp_done = (sem(n) for n in (
        "scores_ready", "decayed", "max_done", "exp_done"))
    pt_psum, pt_copied, o_psum, o_copied, o_scaled = (sem(n) for n in (
        "probs_transposed", "probs_copied", "heads_out_ready", "ret_out_copied", "fox_out_scaled"))
    bn_done, bn_rt, fsq_done, fo_rt, mix_ret, mix_fox = (sem(n) for n in (
        "bn_done", "bn_root", "fox_squares_done", "fox_root", "ret_mixed", "fox_mixed"))
    bn_inv, ret_scaled = sem("bn_reciprocal_done"), sem("ret_heads_scaled")
    mt_psum, mt_copied = sem("mix_transposed"), sem("mix_high_done")
    y_sq, y_rt, nw_used, yg_done, yg_read = (sem(n) for n in ("y_squares", "y_root", "normw_used", "yg_done", "yg_read"))
    x1_done, x1_sq, x1_rt, h2_done = sem("x1_done"), sem("x1_squares"), sem("x1_root"), sem("h2_done")
    h2t_psum, h2t_copied, h2t_dve, lg_psum = sem("h2_transposed"), sem("h2t_copied_scalar"), sem("h2t_copied_vector"), sem("logits_ready")
    cmax_done, cexp_done, fdif_done, fexp_done, mk_done, rank_psum, count_done = (sem(n) for n in (
        "coarse_max", "coarse_exp", "fine_difference", "fine_exp", "mask_done", "ranks_ready", "count_done"))
    selg_done, selc_done = sem("gather_matrix_done"), sem("weight_matrix_done")
    xg_psum, xg_copied, ct_psum, ct_copied = (sem(n) for n in (
        "gathered", "gathered_copied", "weights_transposed", "weights_copied"))
    silu_done, hid_done, hid_seen, hidt_psum, hidt_copied = (sem(n) for n in (
        "silu_done", "hidden_done", "hidden_seen", "hidden_transposed", "hidden_copied"))
    ye_act, ye_dve, er_used = (sem(n) for n in (
        "result_copied_scalar", "result_copied_vector", "expert_unit_used"))
    add_psum, added = sem("addend_ready"), sem("added")
    sum_done, y2_sq, y2_rt, res_done = sem("sum_done"), sem("y2_squares"), sem("y2_root"), sem("out_ready")

    units = [("ret", h, 0) for h in range(H)] + [("fox", h, t) for h in range(H) for t in range(TT)]
    NU = len(units)
    ADA_AT = ((0,), (1,), (), (2,), (3, 4), (5,), (6,), (7,))
    SPREAD_AT = 1
    LATE_TWICE = (10, 13, 16)
    LATE_AT = (5, 9, 13)

    tq_bank = (6, 7, 2, 3)
    mt_bank = (4, 5, 6, 7, 2, 3, 4, 5)
    late_granules = range(5, 17, 2)

    late_at_step, n = [], len(LATE_AT)
    for k in range(NU + 2):
        late_at_step.append(range(n, min(n + 1 + (k in LATE_TWICE), 2 * KC)))
        n = late_at_step[-1].stop

    def before(kind, k):
        return sum(u[0] == kind for u in units[:max(k, 0)])

    block = ctx.enter_context(nc.Block())

    @block.sync
    def _(sp):
        sp.dma_start(CV, a["c"].rearrange("b (p j) -> (b p) j", j=KC)).then_inc(c_in, 16)
        sp.dma_start(TAB, table).then_inc(tab_in, 16)

        for v in range(2):
            for u in range(4 if v == 0 else 0):
                sp.dma_start(HRING[:, u, :], ada_v[:, u, 0:D]).then_inc(hring_in[u], 16)
            with sp.Fori(1 - v, 4) as i:
                for u in range(4):
                    sp.wait_ge(hrow_used, 4 * i + (16 * v - 3) + u)
                    sp.dma_start(HRING[:, u, :], ada_v[:, bass.ds(4 * i + u, 1), v * D:(v + 1) * D]).then_inc(hring_in[u], 16)

        def win(chunk, u, first=False):
            if not first:
                sp.wait_ge(lo_done, 8 * chunk + (2 * u - 2))
            sp.dma_start(WR[:, u % 2], win_v[:, 4 * u:4 * u + 4, bass.ds(chunk * CH, CH)]).then_inc(wr_in[u % 2], 16)

        def ada(ps, k, first=False):
            if not first:
                sp.wait_ge(arow_used, 8 * ps + (k - 1))
            sp.dma_start(ARING[:, k % 2], ada_v[:, 2 * k:2 * k + 2, bass.ds(ps * PW + 2 * D, PW)]).then_inc(aring_in[k % 2], 16)

        def abias(ps):
            sp.wait_ge(abias_used, ps)
            sp.dma_start(ABIAS[0:1, :], a["ada_b"][:, bass.ds(ps * PW + 2 * D, PW)]).then_inc(abias_in, 16)

        def iteration(it):
            for k in range(8):
                win(2 * it + k // 4, k % 4)
                if k == 0:
                    abias(it)
                for u in ADA_AT[k]:
                    ada(it, u)

        for u in range(2):
            win(0, u, first=True)
        for k in range(2):
            ada(0, k, first=True)
        win(0, 2)
        win(0, 3)
        ada(0, 2)
        win(1, 0)
        ada(0, 3)
        ada(0, 4)
        win(1, 1)
        ada(0, 5)
        win(1, 2)
        ada(0, 6)
        win(1, 3)
        ada(0, 7)
        with sp.Fori(1, 7) as it:
            iteration(it)

        def wout(n):
            sp.wait_ge(lo_done, 2 * (56 + n) - 2)
            sp.dma_start(WR[:, n % 2], wout_v[:, 4 * (n % 4):4 * (n % 4) + 4, (n // 4) * CH:(n // 4 + 1) * CH]).then_inc(wr_in[n % 2], 16)

        late_col = 2 * D + MOD_EARLY
        sp.wait_ge(arow_used, 8 * PASSES)
        for n in range(2 * KC):
            j, v = n // 2, n % 2
            c = late_col + v * HALF
            if n in (2, 16):
                cb = late_col + (n // 16) * HALF
                if n == 16:
                    sp.wait_ge(late_bias, 1)
                sp.dma_start(CBIAS[0:1, 0:HALF - 2 * CH], a["ada_b"][:, cb:cb + HALF - 2 * CH]).then_inc(cbias_in, 16)
                sp.dma_start(CBIAS[32:96:32, :], a["ada_b"][:, cb + HALF - 2 * CH:cb + HALF].rearrange(
                    "a (g n) -> (a g) n", g=2)).then_inc(cbias_in, 16)
            if n in (18, 20):
                wout((n - 18) // 2)
            if n >= 2:
                sp.wait_ge(late_used, n - 1)
            sp.dma_start(CRING[:, v, :], ada_v[:, j, c:c + HALF]).then_inc(crow_in[v], 16)

        def expert(e, u, halves=(0, 1)):
            if u < 4:
                w13 = ER[:, u].rearrange("p (w j n) -> p w j n", w=2, j=4)
                for w in halves:
                    src = (w1_v, w3_v)[w]
                    sp.dma_start(w13[:, w], src[:, bass.ds(e, 1), 4 * u:4 * u + 4, :].rearrange("p e j n -> p (e j) n")).then_inc(er_in[u], 16)
            else:
                sp.dma_start(ER[:, u].rearrange("p (q n) -> p q n", q=2),
                             w2_v[:, bass.ds(e, 1), 2 * u - 8:2 * u - 6, :].rearrange("p e q n -> p (e q) n")).then_inc(er_in[u], 16)

        for n in range(2, 16):
            if n == 4:
                sp.wait_ge(mt_psum, 8)
            if 4 <= n < 12:
                expert(0, (n - 4) // 2, (n % 2,))
            wout(n)
        sp.wait_ge(part_used, 8 * 18)
        expert(0, 4)
        expert(0, 5)
        sp.wait_ge(h2_done, 2)
        sp.dma_start(NW2, across(a["norm_post_ffn"])).then_inc(nw2_in, 16)

        def expert_loop(e, v):
            for u in range(6):
                sp.wait_ge(er_used, 6 * v + (u - 5))
                expert(e, u)

        with sp.Fori(1, NE) as e:
            expert_loop(e, e)
        sp.wait_ge(count_done, 1)
        most = sp.value_load(icount[0:1, 0:1], min_val=0, max_val=S)
        with sp.If(most > SLOTS):
            with sp.Fori(1, ROUNDS) as r:
                with sp.Fori(0, NE) as e:
                    expert_loop(e, NE * r + e)
        for tt in range(TT):
            for half in range(2):
                c = slice(half * HW, (half + 1) * HW)
                sp.wait_ge(res_done, 2 * tt + half + 1)
                sp.dma_start(out_v[:, tt, c], X[:, tt, c]).then_inc(out_done, 16)
        sp.wait_ge(out_done, 64)

    @block.scalar
    def _(act):
        st = Steps(act, s_step)
        for tt in range(TT):
            act.dma_start(X[:, tt, :], x_v[:, tt, :]).then_inc(x_in, 16)
        act.dma_start(NPRE, a["norm_pre_mix"].rearrange("l (p j) -> (l p) j", j=KC)).then_inc(small_in, 16)
        act.dma_start(QKN[:, 0:1], col(a["fox_qn_w"])).then_inc(small_in, 16)
        act.dma_start(QKN[:, 1:2], col(a["fox_kn_w"])).then_inc(small_in, 16)
        for r in range(2):
            act.dma_start(FBIAS[r * H:(r + 1) * H, :], col(a["fox_f_bias"])).then_inc(small_in, 16)
        act.dma_start(RWS[:, :, 0:NG], a["router_coarse_w"][0].rearrange("(p j) n -> p j n", j=KC)).then_inc(small_in, 16)
        act.dma_start(RWS[:, :, NG:36], a["router_fine_w"][0].rearrange("(p j) n -> p j n", j=KC)).then_inc(small_in, 16)
        act.dma_start(RBS[:, 0:NG], across(a["router_coarse_b"])).then_inc(small_in, 16)
        act.dma_start(RBS[:, NG:36], across(a["router_fine_b"])).then_inc(small_in, 16)
        for r in range(2):
            act.dma_start(WF[:, :, r * H:(r + 1) * H], win_v[:, :, NT * HW:NT * HW + H]).then_inc(fgate_in, 16)
        act.dma_start(GNW, across(a["ret_gn_w"])).then_inc(gnw_in, 16)
        act.wait_ge(zeroed, 1)
        act.dma_start(HACC[0:1, 0, :], a["ada_b"][:, 0:D]).then_inc(hbias_in, 16)
        act.dma_start(HACC[0:1, 1, :], a["ada_b"][:, D:2 * D]).then_inc(hbias_in, 16)
        act.dma_start(ABIAS[0:1, :], a["ada_b"][:, 2 * D:2 * D + PW]).then_inc(abias_in, 16)
        act.wait_ge(c_in, 16)
        act.activation(CE, CV, ACT.Exp, scale=-1.0).then_inc(ce_done, 1)
        act.wait_ge(x_in, 32)
        for tt in range(TT):
            act.activation(XS[:, tt, :], X[:, tt, :], ACT.Square, accum_out=SS[:, tt:tt + 1]).then_inc(xsq_done, 1)
        act.wait_ge(zeroed, 2)
        act.wait_ge(xsq_done, 2)
        act.activation(RS[:, 0:2], SS[:, 0:2], ACT.Sqrt, scale=1.0 / D, bias=EPSC).then_inc(xrt_done, 1)
        for g in range(8):
            act.wait_ge(xt_psum, g + 1)
            act.activation(HT[:, 2 * g:2 * g + 2, :], bank[:, g % 4, :], ACT.Copy).then_inc(xt_copied, 1)

        def high(n, gq):
            if not (isinstance(n, int) and n < 4):
                act.wait_ge(part_used, n - 3)
            if gq % 2 == 0:
                act.wait_ge(wr_in[gq // 2 % 2], (2 * n - 2 * gq) * 2 + (16 * (gq // 4) + 16))
            src = WR[:, gq // 2 % 2, 2 * (gq % 2):2 * (gq % 2) + 2, :]
            act.activation(WH[:, gq % 4], src, ACT.Copy).then_inc(hi_done, 1)

        for gq in range(4):
            high(gq, gq)
        for j in range(KC):
            act.wait_ge(ht_done, j + 1)
            act.activation(HH[:, j, :], HT[:, j, :], ACT.Copy).then_inc(hh_done, 1)

        def chunk_copy(c):
            b = c[1]
            act.wait_ge(part_used, 8 * c[0] + 8)
            act.activation(RAW[:, :, bass.ds(c[0] * CH, CH)], bank[:, 2 * b:2 * b + 2, :], ACT.Copy).then_inc(ch_copied, 1)

        def forget():
            act.wait_ge(fg_abs, 1)
            act.activation(SCR[0:16, 0, S:2 * S], SCR[0:16, 0, 0:S], ACT.Exp, scale=-1.0).then_inc(fg_exp, 1)
            act.wait_ge(fg_exp, 1)
            act.activation(SCR[0:16, 0, 2 * S:3 * S], SCR[0:16, 0, S:2 * S], ACT.Ln, bias=1.0).then_inc(fg_ln, 1)

        def iteration(it, last_gates=False):
            for b in range(2):
                for gq in range(8):
                    high(16 * it + (8 * b + gq), gq)
                    if last_gates and b == 1 and gq == 5:
                        act.wait_ge(fg_done, 1)
                        act.wait_ge(rope_done, 2)
                        act.wait_ge(ch_copied, 8)
                        act.activation(SCR, GATE, ACT.Exp, scale=-1.0).then_inc(gate_exp, 1)
                    if gq == 3:
                        chunk_copy((2 * it + (b - 1), 1 - b))
                    if gq == 4 and b == 1:
                        if isinstance(it, int) and it == PASSES - 1:
                            act.wait_ge(gnw_used, 1)
                        mod_copy(it - 1)

        def mod_copy(ps):
            act.wait_ge(mod_psum, ps + 1)
            act.activation(MOD[:, bass.ds(ps * PW, PW)], mod_sum, ACT.Copy).then_inc(mod_copied, 1)

        for b, gq in [(b, gq) for b in range(2) for gq in range(8)][4:]:
            high(8 * b + gq, gq)
            if b == 0 and gq == 5:
                forget()
            if b == 1 and gq == 3:
                chunk_copy((0, 0))
        with act.Fori(1, 4) as it:
            iteration(it)
        iteration(4, last_gates=True)
        iteration(5)
        iteration(6)
        act.wait_ge(qk_sq, 1)
        act.activation(RS[:, 0:32], SS[:, 0:32], ACT.Sqrt, scale=1.0 / DH, bias=EPSC).then_inc(qk_rt, 1)
        act.wait_ge(qk_rt, 1)
        act.dma_start(DEC, decay_table.rearrange("p (h s) -> p h s", h=H)).then_inc(dec_in, 16)
        chunk_copy((13, 1))
        for g in range(0, 16, 2):
            act.wait_ge(tq_psum, g + 1)
            t4, hp = g // 4, g % 4
            dst = QKT[:, t4, 2 * hp:2 * hp + 2, :]
            if t4 < 2:
                act.activation(dst, bank[:, tq_bank[g % 4], :], ACT.Copy).then_inc(tq_act, 1)
            else:
                act.activation(dst, bank[:, tq_bank[g % 4], :], ACT.Copy, scale=QKN[:, t4 - 2:t4 - 1]).then_inc(tq_act, 1)
            if g == 2:
                mod_copy(PASSES - 1)
        act.wait_ge(tq_psum, 16)
        act.dma_start(ONW, across(a["fox_on_w"])).then_inc(onw_in, 16)

        def out_copy(k):
            kind, h, t = units[k]
            if kind == "ret":
                act.wait_ge(o_psum, k + 1)
                act.activation(MIX[:, :, h * DH:(h + 1) * DH], bank[:, 6 + k % 2, 0:2 * P], ACT.Copy).then_inc(o_copied, 1)
            else:
                act.wait_ge(o_scaled, before("fox", k) + 1)
                n = before("fox", k)
                if n:
                    act.wait_ge(fsq_done, n)
                act.activation(CSQ, MIX[:, t, HW + h * DH:HW + (h + 1) * DH], ACT.Square,
                               accum_out=CST[:, 4 + t, h:h + 1]).then_inc(fsq_done, 1)

        for k in range(NU + 2):
            if k < NU and units[k][0] == "fox":
                n = before("fox", k)
                act.wait_ge(lmax_done, n + 1)
                w = P * (units[k][2] + 1)
                act.activation(PR[:, k % 2, 0:w], PR[:, k % 2, 0:w], ACT.Exp, bias=CST[:, 0 + units[k][2], units[k][1]:units[k][1] + 1],
                               accum_out=CST[:, 2 + units[k][2], units[k][1]:units[k][1] + 1]).then_inc(exp_done, 1)
            if 18 <= k < 22:
                high(112 + k - 18, k - 18)
            if k == 12:
                act.wait_ge(st_done, 8)
                act.dma_start(NW, across(a["norm_post_mix"])).then_inc(nw_in, 16)
            if k == 13:
                act.wait_ge(bn_done, 1)
                act.activation(CST[:, 6:8, 0:8], BAG[:, :, 1].rearrange("p (t h) -> p t h", t=TT), ACT.Sqrt, bias=EPSC).then_inc(bn_rt, 1)
            if 1 <= k <= NU and units[k - 1][0] == "fox":
                n = before("fox", k - 1)
                w = P * (units[k - 1][2] + 1)
                act.wait_ge(pt_psum, n + 1)
                if n >= 2:
                    act.wait_ge(o_psum, k - 2)
                act.activation(PRT[:, (k - 1) % 2, 0:w], bank[:, 2 + (k - 1) % 2, 0:w], ACT.Copy).then_inc(pt_copied, 1)
            if k >= 3:
                out_copy(k - 3)
        act.activation(SS[:, 31:32], EPSC, ACT.Sqrt)
        out_copy(NU - 1)
        act.wait_ge(fsq_done, 16)
        act.activation(CST[:, 8:10, 0:8], CST[:, 4:6, 0:8], ACT.Sqrt, scale=1.0 / DH, bias=EPSC).then_inc(fo_rt, 1)
        act.wait_ge(late_bias, 2)
        act.wait_ge(late_used, 2 * KC)
        for v in range(2):
            act.activation(CROW[:, v, :], bank[:, v, :], ACT.Copy).then_inc(late_row, 1)
        for g in range(8):
            act.wait_ge(mt_psum, g + 1)
            act.activation(MH[:, 2 * g:2 * g + 2, :], bank[:, mt_bank[g], :], ACT.Copy).then_inc(mt_copied, 1)

        act.wait_ge(nw_used, 1)
        act.dma_start(NW, across(a["norm_pre_ffn"])).then_inc(nw_in, 16)

        def squares(cc):
            act.wait_ge(part_used, 8 * (14 + cc) + 8)
            for tt in range(TT):
                act.wait_ge(nw_used, 2)
                if 2 * cc + tt:
                    act.wait_ge(y_sq, 2 * cc + tt)
                act.activation(NW[:, 0:CH], bank[:, 2 * cc + tt, :], ACT.Square,
                               accum_out=SS[:, 4 * tt + cc:4 * tt + cc + 1]).then_inc(y_sq, 1)

        for n in range(4, 32):
            high(112 + n, n % 8)
            if n - 5 in late_granules:
                i = late_granules.index(n - 5)
                act.wait_ge(late_spread, i + 1)
                off, w = late_groups[i % 3]
                c = MOD_EARLY + i // 3 * HALF + off
                act.activation(MOD[:, c:c + w], bank[:, 6 + i % 2, 0:w], ACT.Copy).then_inc(late_copied, 1)
            if n == 19:
                squares(0)
                squares(1)
            if n == 27:
                squares(2)
        squares(3)
        act.wait_ge(yg_done, 1)
        act.activation(RS[:, 0:2], RS[:, 2:4], ACT.Sqrt, scale=1.0 / D, bias=EPSC).then_inc(y_rt, 1)
        for tt in range(TT):
            act.wait_ge(x1_done, tt + 1)
            if tt:
                act.wait_ge(x1_sq, tt)
            act.activation(NW, X[:, tt, :], ACT.Square, accum_out=RS[:, 4 + tt:5 + tt]).then_inc(x1_sq, 1)
            act.wait_ge(x1_sq, tt + 1)
            act.activation(RS[:, 6 + tt:7 + tt], RS[:, 4 + tt:5 + tt], ACT.Sqrt, scale=1.0 / D, bias=EPSC).then_inc(x1_rt, 1)
        def h2_turned(tt, j4):
            act.wait_ge(h2t_psum, 4 * tt + j4 + 1)
            act.activation(H2T[:, 4 * j4:4 * j4 + 4, tt * P:(tt + 1) * P], bank[:, j4, :].rearrange("p (j s) -> p j s", j=4),
                           ACT.Copy).then_inc(h2t_copied, 1)

        for tt in range(TT):
            for j4 in (0, 2):
                h2_turned(tt, j4)
        for tt in range(TT):
            act.wait_ge(cmax_done, tt + 1)
            act.activation(JUNK[:, 0:4], LG[:, tt, 0:NG], ACT.Exp, bias=RC[:, tt, 0:1], accum_out=RC[:, tt, 1:2]).then_inc(cexp_done, 1)
            act.wait_ge(cexp_done, tt + 1)
            act.wait_ge(fdif_done, tt + 1)
            act.activation(RC[:, tt, 4:5], RC[:, tt, 3:4], ACT.Exp).then_inc(fexp_done, 1)

        def gathered(n, g4):
            act.wait_ge(xg_psum, n)
            act.activation(XT[:, 4 * g4:4 * g4 + 4, :], bank[:, g4 % 2, :], ACT.Copy).then_inc(xg_copied, 1)

        def scalar_expert(g, b, v):
            act.wait_ge(er_used, 6 * v + 4)
            act.activation(SG[SLOTS:P, :], bank[0:SLOTS, 2, :], ACT.Silu).then_inc(silu_done, 1)
            if b == 1:
                for g4 in range(4):
                    gathered(4 * g + (5 + g4), g4)
                act.wait_ge(ct_psum, g + 1)
                act.activation(SELT, bank[:, 3, 0:S], ACT.Copy).then_inc(ct_copied, 1)
            act.wait_ge(hidt_psum, v + 1)
            act.activation(HIDT, bank[:, 3, 0:FQ * SLOTS], ACT.Copy).then_inc(hidt_copied, 1)
            act.wait_ge(er_used, 6 * v + 6)
            if b == 0:
                act.wait_ge(add_psum, 8 * g + 8)
            act.activation(YS[SLOTS * b:SLOTS * b + SLOTS, 0:2 * CH], bank[0:SLOTS, 4:6, :], ACT.Copy).then_inc(ye_act, 1)

        def scalar_pair(g):
            for b in range(2):
                scalar_expert(g, b, 2 * g + b)

        def scalar_end():
            act.activation(JUNK[:, 7:8], EPSC, ACT.Sqrt)
            for tt in range(TT):
                act.wait_ge(sum_done, tt + 1)
                act.activation(XT.rearrange("p j s -> p (j s)"), YACC[:, tt, :], ACT.Square, accum_out=RS[:, 8 + tt:9 + tt]).then_inc(y2_sq, 1)
                act.wait_ge(y2_sq, 1 + tt)
                act.activation(RS[:, 10 + tt:11 + tt], RS[:, 8 + tt:9 + tt], ACT.Sqrt, scale=1.0 / D, bias=EPSC).then_inc(y2_rt, 1)

        act.activation(JUNK[:, 6:7], EPSC, ACT.Copy).then_inc(ye_act, 1)
        for g4 in range(4):
            gathered(g4 + 1, g4)
        with act.Fori(0, NP) as g:
            scalar_pair(g)
        act.wait_ge(count_done, 1)
        most = act.value_load(icount[0:1, 0:1], min_val=0, max_val=S)
        with act.If(most > SLOTS):
            with act.Fori(NP, ROUNDS * NP) as g:
                scalar_pair(g)
        scalar_end()

    @block.tensor
    def _(pe):
        def mm(o, l, r, start=True, stop=True):
            return pe.matmul(o, l, r, start=start, stop=stop, skip_group_check=True)

        def warm_up(n, b=4):
            for _ in range(n):
                mm(bank[:, b, :], IDENT, TAB[:, 0:CH])

        pe.wait_ge(tab_in, 16)
        pe.wait_ge(xs_done, 2)
        for g in range(8):
            if g >= 4:
                pe.wait_ge(xt_copied, g - 3)
            for jj in range(2):
                for tt in range(TT):
                    j = 2 * g + jj
                    last = pe.transpose(bank[:, g % 4, (2 * jj + tt) * P:(2 * jj + tt + 1) * P],
                                        XS[:, tt, :].rearrange("p (q j) -> p j q", j=KC)[:, j, :], IDENT)
            last.then_inc(xt_psum, 1)
        for v in range(2):
            if v:
                pe.wait_ge(hrow_used, 2 * KC - 2)
                warm_up(3)
            pe.wait_ge(hacc_done, v + 1)
            for j in range(KC):
                last = mm(bank[:, 6 + v, j:j + 1], HACC[:, v, :].rearrange("p (q j) -> p j q", j=KC)[:, j, :], ONES[:, 0:1])
            last.then_inc(hcol_psum, 1)
        pe.wait_ge(fgate_in, 32)
        for j in range(KC):
            pe.wait_ge(ht_done, j + 1)
            mm(bank[0:16, 6, 0:S], WF[:, j, :], HT[:, j, :], start=(j == 0), stop=(j == KC - 1)).then_inc(fg_psum, 1)

        def granule(n, gq, left, b0, first):
            pe.wait_ge(lo_done, n + 1)
            lh, ll = left
            for jj in range(2):
                k = 2 * gq + jj
                if first:
                    pe.wait_ge(hl_done, k + 1)
                for tt in range(TT):
                    o, tok = bank[:, b0 + tt, :], slice(tt * P, (tt + 1) * P)
                    mm(o, lh[:, k, tok], WH[:, gq % 4, jj, :], start=(k == 0), stop=False)
                    mm(o, lh[:, k, tok], WL[:, gq % 4, jj, :], start=False, stop=False)
                    last = mm(o, ll[:, k, tok], WH[:, gq % 4, jj, :], start=False, stop=(k == KC - 1))
            last.then_inc(part_used, 1)

        def project(it, b, first=False):
            if not first:
                pe.wait_ge(ch_copied, 2 * it + (b - 1))
            for gq in range(8):
                granule(16 * it + (8 * b + gq), gq, (HH, HL), 2 * b, first and b == 0)
                if b == 0 and gq == SPREAD_AT and not first:
                    spread(it - 1)

        def spread(ps):
            pe.wait_ge(acc_done, ps + 1)
            if not (isinstance(ps, int) and ps == 0):
                pe.wait_ge(mod_copied, ps)
            mm(bank[:, 4, :], ONES, AACC[:, 0:CH])
            mm(bank[:, 5, 0:PW - CH], ONES, AACC[:, CH:PW]).then_inc(mod_psum, 1)

        for b in range(2):
            project(0, b, True)
        for b in range(2):
            project(1, b)
        with pe.Fori(2, 7) as it:
            for b in range(2):
                project(it, b)

        def late_row_added(n):
            j, v = n // 2, n % 2
            pe.wait_ge(crow_in[v], 16 * j + 16)
            for g, (off, w) in enumerate(late_groups):
                last = mm(bank[32 * g:32 * g + 32, v, 0:w], CC[:, j, :], CRING[:, v, off:off + w], start=(j == 0), stop=False)
            last.then_inc(late_used, 1)
            if n in (14, 2 * KC - 1):
                pe.wait_ge(cbias_in, 32 * (v + 1))
                for g, (off, w) in enumerate(late_groups):
                    q = slice(32 * g, 32 * g + 1)
                    last = mm(bank[32 * g:32 * g + 32, v, 0:w], ONES[q, 0:32], CBIAS[q, 0:w], start=False, stop=False)
                last.then_inc(late_bias, 1)

        pe.wait_ge(rope_done, 2)
        for g in range(16):
            t4, hp = g // 4, g % 4
            if g >= 4:
                if g % 2 == 0:
                    pe.wait_ge(tq_act, (g - 4) // 2 + 1)
                else:
                    pe.wait_ge(tq_dve, (g - 5) // 2 + 1)
            if g == 8:
                pe.wait_ge(qk_norm, 1)
            for hh in range(2):
                for tt in range(TT):
                    o = (0, 1, 4, 5)[t4] * HW + (2 * hp + hh) * DH
                    last = pe.transpose(bank[:, tq_bank[g % 4], (2 * hh + tt) * P:(2 * hh + tt + 1) * P], RAW[:, tt, o:o + DH], IDENT)
            last.then_inc(tq_psum, 1)
            if g == 1:
                pe.wait_ge(ch_copied, 14)
            if g == 3:
                spread(PASSES - 1)
            if g in LATE_AT:
                pe.wait_ge(cc_done, 1)
                late_row_added(LATE_AT.index(g))
        pe.wait_ge(tq_act, 8)
        pe.wait_ge(tq_dve, 8)
        pe.wait_ge(mod_copied, PASSES)

        def scores(k):
            kind, h, t = units[k]
            sb = bank[:, 4 + k % 2, :]
            if k >= 2:
                pe.wait_ge(st_done if units[k - 2][0] == "ret" else lmax_done, before(units[k - 2][0], k - 1))
            if kind == "ret":
                mm(sb[:, 0:S], QKT[:, 1, h, 0:P], QKT[:, 0, h, :])
                mm(sb[:, S:S + P], QKT[:, 1, h, P:S], QKT[:, 0, h, P:S]).then_inc(sc_psum, 1)
            else:
                w = P * (t + 1)
                pe.wait_ge(fkb_done, h + 1)
                if h == 0:
                    pe.wait_ge(fqb_done, 1)
                mm(sb[:, 0:w], QKT[:, 2, h, t * P:(t + 1) * P], QKT[:, 3, h, 0:w], stop=False)
                mm(sb[:, 0:w], FQB[:, t * P:(t + 1) * P], FKB[0:2 * H, h % 2, 0:w], start=False).then_inc(sc_psum, 1)

        def turn(k):
            kind, h, t = units[k]
            if kind == "fox":
                n = before("fox", k)
                pe.wait_ge(exp_done, n + 1)
                if n >= 2:
                    pe.wait_ge(pt_copied, n - 1)
                for sblk in range(t + 1):
                    last = pe.transpose(bank[:, 2 + k % 2, sblk * P:(sblk + 1) * P], PR[:, k % 2, sblk * P:(sblk + 1) * P], IDENT)
                last.then_inc(pt_psum, 1)

        def values(k):
            kind, h, t = units[k]
            ob = bank[:, 6 + k % 2, :]
            if k >= 2:
                pe.wait_ge(o_copied if units[k - 2][0] == "ret" else o_scaled, before(units[k - 2][0], k - 1))
            if kind == "ret":
                pe.wait_ge(st_done, before("ret", k) + 1)
                v = VRET[:, :, h * DH:(h + 1) * DH]
                mm(ob[:, 0:P], ST[:, k % 2, 0:P], v[:, 0, :])
                mm(ob[:, P:S], ST[:, k % 2, P:S], v[:, 0, :], stop=False)
                mm(ob[:, P:S], ST[:, k % 2, S:S + P], v[:, 1, :], start=False).then_inc(o_psum, 1)
            else:
                n = before("fox", k)
                pe.wait_ge(pt_copied, n + 1)
                for sblk in range(t + 1):
                    last = mm(ob[:, 0:P], PRT[:, k % 2, sblk * P:(sblk + 1) * P], VFOX[:, sblk, h * DH:(h + 1) * DH],
                              start=(sblk == 0), stop=(sblk == t))
                last.then_inc(o_psum, 1)

        for k in range(NU + 2):
            if k < NU:
                scores(k)
            if 1 <= k <= NU:
                turn(k - 1)
            if k >= 2:
                values(k - 2)
            for n in late_at_step[k]:
                late_row_added(n)
        for g in range(8):
            if g == 0:
                pe.wait_ge(mix_ret, 2)
                pe.wait_ge(o_scaled, 16)
                pe.wait_ge(pt_copied, 16)
            if g == 4:
                pe.wait_ge(mix_fox, 1)
            if g >= 6:
                pe.wait_ge(ml_done, g - 5)
            for jj in range(2):
                for tt in range(TT):
                    last = pe.transpose(bank[:, mt_bank[g], (2 * jj + tt) * P:(2 * jj + tt + 1) * P],
                                        MIX[:, tt, (2 * g + jj) * P:(2 * g + jj + 1) * P], IDENT)
            last.then_inc(mt_psum, 1)
        pe.wait_ge(late_row, 2)
        for cc in range(4):
            for gq in range(8):
                if cc == 0:
                    pe.wait_ge(ml_done, gq + 1)
                if cc == 3 and gq == 0:
                    pe.wait_ge(late_copied, 6)
                granule(8 * (14 + cc) + gq, gq, (MH, ML), 2 * cc, False)
                if 8 * cc + gq in late_granules:
                    i = late_granules.index(8 * cc + gq)
                    if i >= 2:
                        pe.wait_ge(late_copied, i - 1)
                    q = slice(32 * (i % 3), 32 * (i % 3) + 1)
                    w = late_groups[i % 3][1]
                    mm(bank[:, 6 + i % 2, 0:w], ONES[q, :], CROW[q, i // 3, 0:w]).then_inc(late_spread, 1)
        pe.wait_ge(yg_read, 2)
        pe.wait_ge(x1_done, 2)
        warm_up(WARM_H2)
        for tt in range(TT):
            pe.wait_ge(h2_done, tt + 1)
            for j4 in range(4):
                g = 4 * tt + j4
                if tt:
                    pe.wait_ge((h2t_copied, h2t_dve)[j4 % 2], j4 // 2 + 1)
                for j in range(4 * j4, 4 * j4 + 4):
                    last = pe.transpose(bank[:, j4, (j % 4) * P:(j % 4 + 1) * P], H2[:, tt, j, :], IDENT)
                last.then_inc(h2t_psum, 1)
        for tt in range(TT):
            pe.wait_ge(h2t_copied, 2 * tt + 2)
            pe.wait_ge(h2t_dve, 2 * tt + 2)
            for j in range(KC):
                last = mm(bank[:, 6 + tt, 0:36], H2T[:, j, tt * P:(tt + 1) * P], RWS[:, j, :], start=(j == 0), stop=(j == KC - 1))
            last.then_inc(lg_psum, 1)
        pe.wait_ge(mk_done, 1)
        warm_up(WARM_RANK)
        pe.wait_ge(mk_done, 2)
        mm(bank[:, 4, 0:NE], TRI, MK[:, 0, :])
        mm(bank[:, 4, NE:2 * NE], TRI, MK[:, 1, :], stop=False)
        mm(bank[:, 4, NE:2 * NE], ONES, MK[:, 0, :], start=False)
        mm(bank[:, 4, 2 * NE:3 * NE], ONES, MK[:, 0, :], stop=False)
        mm(bank[:, 4, 2 * NE:3 * NE], ONES, MK[:, 1, :], start=False).then_inc(rank_psum, 1)

        def gather(n, first):
            pe.wait_ge(selg_done, n + 1)
            for g4 in range(4):
                if not first:
                    pe.wait_ge(xg_copied, 4 * n + (g4 - 1))
                elif g4 >= 2:
                    pe.wait_ge(xg_copied, g4 - 1)
                for j in range(4):
                    for tt in range(TT):
                        last = mm(bank[:, g4 % 2, j * P:(j + 1) * P], H2[:, tt, 4 * g4 + j, :], SELG[:, tt, :], start=(tt == 0), stop=(tt == 1))
                last.then_inc(xg_psum, 1)

        def weights_turned(g):
            pe.wait_ge(selc_done, g + 1)
            for tt in range(TT):
                last = pe.transpose(bank[:, 3, tt * P:(tt + 1) * P], SELC[:, tt, :], IDENT)
            last.then_inc(ct_psum, 1)

        def add_back(g):
            pe.wait_ge(ye_act, 2 * g + 1)
            pe.wait_ge(ye_dve, 2 * g + 1)
            pe.wait_ge(ct_copied, g + 1)
            for n in range(8):
                tt, cc = n // 4, n % 4
                pe.wait_ge(added, 8 * g + (n + 1))
                mm(bank[:, 6 + n % 2, :], SELT[:, tt * P:(tt + 1) * P], YS[:, cc * CH:(cc + 1) * CH]).then_inc(add_psum, 1)

        def expert(g, b):
            v = 2 * g + b
            for u in range(4):
                w13 = ER[:, u].rearrange("p (w j n) -> p w j n", w=2, j=4)
                if b == 0:
                    pe.wait_ge(xg_copied, 4 * g + (u + 1))
                pe.wait_ge(er_in[u], 32 * v + 32)
                for j in range(4):
                    for w in range(2):
                        k = 4 * u + j
                        last = mm(bank[SLOTS * w:SLOTS * w + SLOTS, 2, :], XT[:, k, SLOTS * b:SLOTS * b + SLOTS], w13[:, w, j, :],
                                  start=(k == 0), stop=(k == KC - 1))
                last.then_inc(er_used, 1)
            if b == 0:
                add_back(g)
            else:
                gather(g + 1, False)
                weights_turned(g)
                pe.wait_ge(ct_copied, g + 2)
            pe.wait_ge(hid_done, v + 1)
            pe.sem_inc(hid_seen, 1)
            for q in range(FQ):
                last = pe.transpose(bank[:, 3, q * SLOTS:(q + 1) * SLOTS],
                                    HID[SLOTS:P, :].rearrange("p (s q) -> p q s", q=FQ)[:, q, :], IDENT[SLOTS:P, SLOTS:P])
            last.then_inc(hidt_psum, 1)
            pe.wait_ge(hidt_copied, v + 1)
            pe.wait_ge(ye_act, v + 1)
            pe.wait_ge(ye_dve, v + 1)
            for q in range(FQ):
                u = 4 + q // 2
                w2t = ER[:, u].rearrange("p (q n) -> p q n", q=2)
                if q % 2 == 0:
                    pe.wait_ge(er_in[u], 16 * v + 16)
                for cc in range(2):
                    for w in range(2):
                        o = w * 2 * CH + cc * CH
                        last = mm(bank[SLOTS * w:SLOTS * w + SLOTS, 4 + cc, :], HIDT[:, q, :], w2t[:, q % 2, o:o + CH],
                                  start=(q == 0), stop=(q == FQ - 1))
                if q % 2 == 1:
                    last.then_inc(er_used, 1)

        warm_up(WARM_GATHER, 5)
        gather(0, True)
        with pe.Fori(0, NP) as g:
            for b in range(2):
                expert(g, b)
        pe.wait_ge(count_done, 1)
        most = pe.value_load(icount[0:1, 0:1], min_val=0, max_val=S)
        with pe.If(most > SLOTS):
            with pe.Fori(NP, ROUNDS * NP) as g:
                for b in range(2):
                    expert(g, b)
            add_back(ROUNDS * NP)
        with pe.Else():
            add_back(NP)

    @block.gpsimd
    def _(pool):
        def low(n, gq):
            pool.wait_ge(hi_done, n + 1)
            src = WR[:, gq // 2 % 2, 2 * (gq % 2):2 * (gq % 2) + 2, :]
            pool.tensor_tensor(WL[:, gq % 4], src, WH[:, gq % 4].bitcast(F32), ALU.subtract).then_inc(lo_done, 1)

        with pool.Fori(0, 14) as c:
            for gq in range(8):
                low(8 * c + gq, gq)
        def key_bias(h):
            if h >= 2:
                pool.wait_ge(sc_psum, H + 2 * h - 2)
            pool.tensor_scalar(FKB[0:16, h % 2, :], FG[0:16, :], TAB[0:16, T_SELA + h:T_SELA + h + 1],
                               TAB[0:16, T_SELB + h:T_SELB + h + 1], ALU.mult, ALU.add).then_inc(fkb_done, 1)

        def ret_scale(t, heads):
            for h in heads:
                y = MIX[:, t, h * DH:(h + 1) * DH]
                pool.tensor_scalar(y, y, BAG[:, t * H + h, 0:1], CST[:, 6 + t, h:h + 1], ALU.subtract, ALU.mult).then_inc(ret_scaled, 1)

        def ret_gate(t):
            pool.wait_ge(ret_scaled, H * (t + 1))
            pool.tensor_tensor(MIX[:, t, 0:HW], MIX[:, t, 0:HW], GATE[:, t], ALU.mult).then_inc(mix_ret, 1)

        pool.wait_ge(mod_psum, PASSES)
        pool.wait_ge(fg_done, 1)
        key_bias(0)
        key_bias(1)
        key_bias(2)
        key_bias(3)
        pool.wait_ge(bn_inv, 1)
        for h in range(4, H):
            key_bias(h)
            ret_scale((h - 4) // 2, range(4 * (h % 2), 4 * (h % 2) + 4))
            if h % 2 == 1:
                ret_gate((h - 4) // 2)
            if h >= 6:
                for gq in range(2 * h - 12, 2 * h - 10):
                    low(8 * 14 + gq, gq)
        for gq in range(4, 8):
            low(8 * 14 + gq, gq)
        with pool.Fori(15, 18) as c:
            for gq in range(8):
                low(8 * c + gq, gq)
        pool.wait_ge(g2_done, 1)
        pool.wait_ge(sum_done, 1)
        pool.tensor_tensor(YG[:, 0, :], YACC[:, 0, :], G2B, ALU.mult).then_inc(yg_pool, 1)

    @block.vector
    def _(dve):
        st = Steps(dve, v_step)
        tt_, ts_, stt = dve.tensor_tensor, dve.tensor_scalar, dve.scalar_tensor_tensor
        st.link(dve.memset(HACC, 0.0))
        dve.memset(ABIAS, 0.0).then_inc(zeroed, 1)
        dve.memset(EPSC, EPS).then_inc(zeroed, 1)
        dve.wait_ge(ce_done, 1)
        st.link(ts_(CE, CE, 1.0, None, ALU.add))
        st.link(dve.reciprocal(CE, CE))
        st.link(tt_(CA, CV, CE, ALU.mult))
        dve.wait_ge(hbias_in, 32)

        def head(v):
            with dve.Fori(0, 4) as i:
                for u in range(4):
                    dve.wait_ge(hring_in[u], 16 * i + (64 * v + 16))
                    stt(HACC[:, v, :], HRING[:, u, :], CA[:, bass.ds(4 * i + u, 1)], HACC[:, v, :], ALU.mult, ALU.add).then_inc(hrow_used, 1)
                    dve.wait_ge(hrow_used, 4 * i + (16 * v + u + 1))

        head(0)
        dve.sem_inc(hacc_done, 1)
        dve.wait_ge(xrt_done, 1)
        st.link(dve.reciprocal(RS[:, 0:2], RS[:, 0:2]))
        for tt in range(TT):
            ts_(XS[:, tt, :], X[:, tt, :], RS[:, tt:tt + 1], None, ALU.mult).then_inc(xs_done, 1)
        head(1)
        dve.sem_inc(hacc_done, 1)
        dve.wait_ge(hcol_psum, 2)
        dve.wait_ge(small_in, 16 * 9)
        st.link(stt(A1, bank[:, 7, 0:KC], 1.0, NPRE, ALU.add, ALU.mult))
        st.link(dve.tensor_copy(SH1, bank[:, 6, 0:KC]))
        dve.wait_ge(xt_copied, 8)
        for j in range(KC):
            ts_(HT[:, j, :], HT[:, j, :], A1[:, j:j + 1], SH1[:, j:j + 1], ALU.mult, ALU.add).then_inc(ht_done, 1)
        for j in range(KC):
            dve.wait_ge(hh_done, j + 1)
            dve.wait_ge(fg_psum, j + 1)
            tt_(HL[:, j, :], HT[:, j, :], HH[:, j, :].bitcast(F32), ALU.subtract).then_inc(hl_done, 1)

        def rows(ps, first=False, between=None):
            for k in range(8):
                dve.wait_ge(aring_in[k % 2], 64 * ps + (16 * (k // 2) + 16))
                src = AACC
                if k == 0:
                    dve.wait_ge(abias_in, 16 * ps + 16)
                    if not first:
                        dve.wait_ge(mod_psum, ps)
                    src = ABIAS
                st.link(stt(AACC, ARING[:, k % 2, 0, :], CA[:, 2 * k:2 * k + 1], src, ALU.mult, ALU.add))
                if k == 0:
                    dve.sem_inc(abias_used, 1)
                stt(AACC, ARING[:, k % 2, 1, :], CA[:, 2 * k + 1:2 * k + 2], AACC, ALU.mult, ALU.add).then_inc(arow_used, 1)
                dve.wait_ge(arow_used, 8 * ps + (k + 1))
                if between:
                    between(k)
            dve.sem_inc(acc_done, 1)

        ROWS = 8

        def tensor_of(it, tt):
            return RAW[:, tt, bass.ds(it * HW, HW)].rearrange("p (h d) -> p h d", h=H)

        z, az, lnv = SCR[0:16, 0, 3 * S:4 * S], SCR[0:16, 0, 0:S], SCR[0:16, 0, 2 * S:3 * S]
        one, mn = SCR[0:16, 1, 0:S], SCR[0:16, 1, S:2 * S]
        dve.wait_ge(fg_psum, KC)
        st.link(ts_(z, bank[0:16, 6, 0:S], FBIAS[0:16, :], None, ALU.add))
        st.link(ts_(mn, z, -1.0, None, ALU.mult))
        tt_(az, z, mn, ALU.max).then_inc(fg_abs, 1)
        dve.wait_ge(fg_abs, 1)
        st.link(ts_(mn, z, 0.0, None, ALU.min))
        st.link(dve.memset(one, 1.0))
        rows(0, True)
        dve.wait_ge(fg_ln, 1)
        st.link(tt_(z, mn, lnv, ALU.subtract))
        dve.tensor_tensor_scan(FG[0:16, :], one, z, 0.0, ALU.mult, ALU.add).then_inc(fg_done, 1)
        dve.wait_ge(fg_done, 1)

        with dve.Fori(0, 2) as it, st.loop(it, ROWS + 12, 2):
            rows(it + 1)
            dve.wait_ge(ch_copied, 2 * it + 2)
            for tt in range(TT):
                x = tensor_of(it, tt)
                cos, sin = (TAB[:, o + tt * 64:o + tt * 64 + 64].unsqueeze(1).to_broadcast([P, H, 64]) for o in (T_COS, T_SIN))
                lo, hi = x[:, :, 0:64], x[:, :, 64:128]
                t1, t2 = (SCR[:, tt, i * CH:(i + 1) * CH].rearrange("p (h d) -> p h d", h=H) for i in range(2))
                st.link(tt_(t1, lo, sin, ALU.mult))
                st.link(tt_(t2, hi, sin, ALU.mult))
                st.link(tt_(lo, lo, cos, ALU.mult))
                st.link(tt_(hi, hi, cos, ALU.mult))
                st.link(tt_(lo, lo, t2, ALU.subtract))
                st.link(tt_(hi, hi, t1, ALU.add))
        dve.sem_inc(rope_done, 1)
        dve.sem_inc(rope_done, 1)
        with dve.Fori(2, 4) as it, st.loop(it - 2, ROWS, 2):
            rows(it + 1)
        def gate(k):
            t, c = k // 4, k % 4
            c = slice(c * 256, (c + 1) * 256)
            st.link(ts_(SCR[:, t, c], SCR[:, t, c], 1.0, None, ALU.add))
            st.link(dve.reciprocal(SCR[:, t, c], SCR[:, t, c]))
            st.link(tt_(GATE[:, t, c], GATE[:, t, c], SCR[:, t, c], ALU.mult))
            st.link(tt_(GATE[:, t, c], GATE[:, t, c], GNW[:, c], ALU.mult))

        def squares(k):
            if k >= 4:
                return
            i, tt = k // 2, k % 2
            if tt == 0:
                dve.wait_ge(ch_copied, 10 + 2 * i)
            x = RAW[:, tt, (4 + i) * HW:(5 + i) * HW].rearrange("p (h d) -> p h d", h=H)
            sq = SCR[:, tt, :].rearrange("p (h d) -> p h d", h=H)
            st.link(tt_(sq, x, x, ALU.mult))
            st.link(dve.tensor_reduce(SS[:, i * 16 + tt * H:i * 16 + tt * H + H], sq, AX_X, ALU.add))

        dve.wait_ge(gate_exp, 1)
        dve.wait_ge(gnw_in, 16)
        rows(5, between=gate)
        dve.sem_inc(gnw_used, 1)
        rows(6, between=squares)
        dve.sem_inc(qk_sq, 1)
        dve.wait_ge(qk_rt, 1)
        st.link(dve.reciprocal(RS, RS))
        for i in range(2):
            for tt in range(TT):
                x = RAW[:, tt, (4 + i) * HW:(5 + i) * HW].rearrange("p (h d) -> p h d", h=H)
                r = RS[:, i * 16 + tt * H:i * 16 + tt * H + H].unsqueeze(2).to_broadcast([P, H, DH])
                st.link(tt_(x, x, r, ALU.mult))
        st.link(ts_(QKN[:, 0:1], QKN[:, 0:1], QK_SCALE, None, ALU.mult))
        dve.sem_inc(qk_norm, 1)

        for g in range(1, 16, 2):
            dve.wait_ge(tq_psum, g + 1)
            t4, hp = g // 4, g % 4
            dst = QKT[:, t4, 2 * hp:2 * hp + 2, :].rearrange("p h s -> p (h s)")
            if t4 < 2:
                dve.tensor_copy(dst, bank[:, tq_bank[g % 4], :]).then_inc(tq_dve, 1)
            else:
                ts_(dst, bank[:, tq_bank[g % 4], :], QKN[:, t4 - 2:t4 - 1], None, ALU.mult).then_inc(tq_dve, 1)
            if g == 3:
                dve.wait_ge(mod_psum, PASSES)
                dve.tensor_copy(CC, CA.unsqueeze(2).to_broadcast([P, KC, 32])).then_inc(cc_done, 1)
        ts_(FQB, FG[0:16, :], TAB[0:16, T_QMUL:T_QMUL + 1], TAB[0:16, T_QADD:T_QADD + 1], ALU.mult, ALU.add).then_inc(fqb_done, 1)

        dve.wait_ge(dec_in, 16)

        def first(k):
            kind, h, t = units[k]
            sb = bank[:, 4 + k % 2, :]
            dve.wait_ge(sc_psum, k + 1)
            if kind == "ret":
                if k >= 2:
                    dve.wait_ge(o_psum, k - 1)
                st.link(tt_(ST[:, k % 2, 0:S], sb[:, 0:S], DEC[:, h, :], ALU.mult))
                tt_(ST[:, k % 2, S:S + P], sb[:, S:S + P], DEC[:, h, 0:P], ALU.mult).then_inc(st_done, 1)
            else:
                n = before("fox", k)
                w = P * (t + 1)
                if n >= 2:
                    dve.wait_ge(pt_psum, n - 1)
                mx = CST[:, t, h:h + 1]
                mask = TAB[:, T_MASK:T_MASK + S] if t else TAB[:, T_MASK + P:T_MASK + S]
                st.link(tt_(PR[:, k % 2, 0:w], sb[:, 0:w], mask, ALU.add))
                st.link(dve.tensor_reduce(mx, PR[:, k % 2, 0:w], AX_X, ALU.max))
                ts_(mx, mx, -1.0, None, ALU.mult).then_inc(lmax_done, 1)

        def second(k):
            kind, h, t = units[k]
            if kind == "fox":
                dve.wait_ge(exp_done, before("fox", k) + 1)
                st.link(dve.reciprocal(CST[:, 10 + t, h:h + 1], CST[:, 2 + t, h:h + 1]))

        def third(k):
            kind, h, t = units[k]
            if kind == "fox":
                dve.wait_ge(o_psum, k + 1)
                ts_(MIX[:, t, HW + h * DH:HW + (h + 1) * DH], bank[:, 6 + k % 2, 0:P], CST[:, 10 + t, h:h + 1], None,
                    ALU.mult).then_inc(o_scaled, 1)

        def ret_stats(h):
            dve.wait_ge(o_copied, h + 1)
            for t in range(TT):
                last = dve.bn_stats(BST[:, t * H + h, :], MIX[:, t, h * DH:(h + 1) * DH])
            st.link(last)
            for t in range(TT):
                last = dve.bn_aggr(BAG[:, t * H + h, :], BST[:, t * H + h, :])
            st.link(last)

        for k in range(NU + 2):
            if k < NU:
                first(k)
            if 1 <= k <= NU:
                second(k - 1)
            if k >= 2:
                third(k - 2)
            if 4 <= k < 4 + H:
                ret_stats(k - 4)
            if k == 4 + H:
                dve.sem_inc(bn_done, 1)
            if k == 6 + H:
                dve.wait_ge(bn_rt, 1)
                dve.reciprocal(CST[:, 6:8, 0:8], CST[:, 6:8, 0:8]).then_inc(bn_inv, 1)
        dve.wait_ge(fo_rt, 1)
        dve.wait_ge(onw_in, 16)
        st.link(dve.reciprocal(CST[:, 8:10, 0:8], CST[:, 8:10, 0:8]))
        for t in range(TT):
            for h in range(H):
                y = MIX[:, t, HW + h * DH:HW + (h + 1) * DH]
                last = stt(y, y, CST[:, 8 + t, h:h + 1], ONW[:, h * DH:(h + 1) * DH], ALU.mult, ALU.mult)
        last.then_inc(mix_fox, 1)
        for g in range(8):
            dve.wait_ge(mt_copied, g + 1)
            tt_(ML[:, 2 * g:2 * g + 2, :].rearrange("p j s -> p (j s)"), bank[:, mt_bank[g], :],
                MH[:, 2 * g:2 * g + 2, :].bitcast(F32).rearrange("p j s -> p (j s)"), ALU.subtract).then_inc(ml_done, 1)

        dve.wait_ge(mod_copied, PASSES)
        dve.wait_ge(nw_in, 16)
        stt(G1B, G1B, 0.0, NW, ALU.add, ALU.mult).then_inc(nw_used, 1)
        dve.wait_ge(late_copied, 2)
        dve.wait_ge(nw_in, 32)
        stt(SC2B, SC2B, 1.0, NW, ALU.add, ALU.mult).then_inc(nw_used, 1)
        dve.wait_ge(nw_used, 2)
        for cc in range(4):
            for tt in range(TT):
                yb = bank[:, 2 * cc + tt, :]
                dve.wait_ge(y_sq, 2 * cc + tt + 1)
                st.link(tt_(yb, yb, G1B[:, cc * CH:(cc + 1) * CH], ALU.mult))
        dve.tensor_reduce(RS[:, 2:4], SS[:, 0:8].rearrange("p (t c) -> p t c", t=TT), AX_X, ALU.add).then_inc(yg_done, 1)
        dve.wait_ge(yg_done, 1)
        dve.wait_ge(yg_done, 1)
        dve.wait_ge(y_rt, 1)
        st.link(dve.reciprocal(RS[:, 0:2], RS[:, 0:2]))
        by_j = lambda row: row.rearrange("p (q j) -> p j q", j=KC)

        def x1(tt):
            yg = bank[:, :, :].rearrange("p (c t) n -> p t c n", t=TT)[:, tt]
            xv = X[:, tt, :].rearrange("p (c n) -> p c n", c=4)
            stt(xv, yg, RS[:, tt:tt + 1], xv, ALU.mult, ALU.add).then_inc(x1_done, 1)
            dve.wait_ge(x1_done, tt + 1)

        def h2_product(tt):
            st.link(tt_(H2[:, tt], by_j(X[:, tt, :]), by_j(SC2B), ALU.mult))

        def h2(tt):
            dve.wait_ge(x1_rt, tt + 1)
            st.link(dve.reciprocal(RS[:, 6 + tt:7 + tt], RS[:, 6 + tt:7 + tt]))
            stt(H2[:, tt], H2[:, tt], RS[:, 6 + tt:7 + tt], by_j(SH2B), ALU.mult, ALU.add).then_inc(h2_done, 1)

        x1(0)
        h2_product(0)
        x1(1)
        dve.sem_inc(yg_read, 2)
        h2(0)
        h2_product(1)
        h2(1)

        def h2_turned(tt, j4):
            dve.wait_ge(h2t_psum, 4 * tt + j4 + 1)
            dve.tensor_copy(H2T[:, 4 * j4:4 * j4 + 4, tt * P:(tt + 1) * P],
                            bank[:, j4, :].rearrange("p (j s) -> p j s", j=4)).then_inc(h2t_dve, 1)

        for tt in range(TT):
            for j4 in (1, 3):
                h2_turned(tt, j4)

        i32x = IOTA[:, 0:NE]
        dve.memset(SLOT, -1.0)
        dve.memset(COEF, 0.0)
        st.link(dve.memset(CPAD, -BIG))
        for tt in range(TT):
            c = lambda n: RC[:, tt, n:n + 1]
            dve.wait_ge(lg_psum, tt + 1)
            st.link(tt_(LG[:, tt, :], bank[:, 6 + tt, 0:36], RBS, ALU.add))
            st.link(dve.tensor_copy(CPAD[:, tt, 0:NG], LG[:, tt, 0:NG]))
            st.link(dve.max(M8[:, tt, :], CPAD[:, tt, :]))
            ts_(c(0), M8[:, tt, 0:1], -1.0, None, ALU.mult).then_inc(cmax_done, 1)
            st.link(dve.max_index(etop[:, 0, :], M8[:, tt, :], CPAD[:, tt, :]))
            st.link(dve.tensor_copy(c(5), etop[:, 0, 0:1]))
            st.link(ts_(GE[:, tt, :], IOTA[:, 0:NG], c(5), None, ALU.is_equal))
            st.link(ts_(GE[:, tt, :], GE[:, tt, :], BIG, -BIG, ALU.mult, ALU.add))
            st.link(tt_(FM[:, tt, :].rearrange("p (g e) -> p g e", g=NG), LG[:, tt, NG:36].rearrange("p (g e) -> p g e", g=NG),
                        GE[:, tt, :].unsqueeze(2).to_broadcast([P, NG, EG]), ALU.add))
            st.link(dve.max(F8[:, tt, :], FM[:, tt, :]))
            tt_(c(3), F8[:, tt, 1:2], F8[:, tt, 0:1], ALU.subtract).then_inc(fdif_done, 1)
            st.link(dve.max_index(etop[:, 1, :], F8[:, tt, :], FM[:, tt, :]))
            st.link(dve.tensor_copy(RC[:, tt, 6:8], etop[:, 1, 0:2]))
            st.link(ts_(O1[:, tt, :], i32x, c(6), None, ALU.is_equal))
            st.link(ts_(O2[:, tt, :], i32x, c(7), None, ALU.is_equal))
            tt_(MK[:, tt, :], O1[:, tt, :], O2[:, tt, :], ALU.add).then_inc(mk_done, 1)
            dve.wait_ge(cexp_done, tt + 1)
            dve.wait_ge(fexp_done, tt + 1)
            st.link(stt(c(8), c(4), 1.0, c(1), ALU.add, ALU.mult))
            st.link(dve.reciprocal(c(9), c(8)))
            st.link(tt_(c(10), c(9), c(4), ALU.mult))
            st.link(ts_(CW[:, tt, :], O1[:, tt, :], c(9), None, ALU.mult))
            st.link(stt(CW[:, tt, :], O2[:, tt, :], c(10), CW[:, tt, :], ALU.mult, ALU.add))
        for tt in range(TT):
            for r in range(ROUNDS):
                last = dve.tensor_copy(COEF[:, tt, r * NE:(r + 1) * NE], CW[:, tt, :])
        st.link(last)
        dve.wait_ge(rank_psum, 1)
        dve.wait_ge(mk_done, 2)
        for tt in range(TT):
            last = stt(SLOT[:, tt, 0:NE], bank[:, 4, tt * NE:(tt + 1) * NE], 1.0, MK[:, tt, :], ALU.add, ALU.mult)
        st.link(last)
        st.link(ts_(SLOT[:, :, 0:NE], SLOT[:, :, 0:NE], -1.0, None, ALU.add))

        def gather_matrix(n):
            for tt in range(TT):
                for b in range(2):
                    last = ts_(SELG[:, tt, b * SLOTS:(b + 1) * SLOTS], IOTA, SLOT[:, tt, bass.ds(2 * n + b, 1)], None, ALU.is_equal)
            last.then_inc(selg_done, 1)

        def weight_matrix(n):
            for tt in range(TT):
                for b in range(2):
                    last = ts_(SELC[:, tt, b * SLOTS:(b + 1) * SLOTS], IOTA, SLOT[:, tt, bass.ds(2 * n + b, 1)],
                               COEF[:, tt, bass.ds(2 * n + b, 1)], ALU.is_equal, ALU.mult)
            last.then_inc(selc_done, 1)

        def add_back(g, last=False):
            for n in range(8):
                tt, cc = n // 4, n % 4
                y = YACC[:, tt, cc * CH:(cc + 1) * CH]
                dve.wait_ge(add_psum, 8 * g + (n + 1))
                tt_(y, bank[:, 6 + n % 2, :], y, ALU.add).then_inc(added, 1)
                if last and n % 4 == 3:
                    dve.wait_ge(added, 8 * g + (n + 3))
                    dve.sem_inc(sum_done, 1)

        def vector_expert(g, b, v):
            dve.wait_ge(silu_done, v + 1)
            tt_(HID[SLOTS:P, :], SG[SLOTS:P, :], bank[SLOTS:P, 2, :], ALU.mult).then_inc(hid_done, 1)
            if b == 0:
                weight_matrix(g)
                gather_matrix(g + 1)
                add_back(g)
            dve.wait_ge(er_used, 6 * v + 6)
            dve.tensor_copy(YS[SLOTS * b:SLOTS * b + SLOTS, 2 * CH:4 * CH], bank[SLOTS:P, 4:6, :].rearrange("p b n -> p (b n)")).then_inc(ye_dve, 1)

        gather_matrix(0)
        for r in range(1, ROUNDS):
            last = ts_(SLOT[:, :, r * NE:(r + 1) * NE], SLOT[:, :, 0:NE], -float(r * SLOTS), None, ALU.add)
        st.link(last)
        st.link(dve.tensor_reduce(JUNK[:, 4:5], bank[:, 4, 2 * NE:3 * NE], AX_X, ALU.max))
        dve.tensor_copy(icount[:, 0:1], JUNK[:, 4:5]).then_inc(count_done, 1)
        dve.memset(SELT, 0.0).then_inc(ct_copied, 1)
        dve.memset(YS, 0.0).then_inc(ye_dve, 1)
        dve.memset(YACC[:, 0, :], 0.0).then_inc(added, 1)
        dve.memset(YACC[:, 1, :], 0.0).then_inc(added, 1)
        dve.wait_ge(late_copied, 6)
        dve.wait_ge(nw2_in, 16)
        tt_(G2B, G2B, NW2, ALU.mult).then_inc(g2_done, 1)
        with dve.Fori(0, NP) as g:
            for b in range(2):
                vector_expert(g, b, 2 * g + b)
        most = dve.value_load(icount[0:1, 0:1], min_val=0, max_val=S)
        with dve.If(most > SLOTS):
            with dve.Fori(NP, ROUNDS * NP) as g:
                for b in range(2):
                    vector_expert(g, b, 2 * g + b)
            add_back(ROUNDS * NP, last=True)
        with dve.Else():
            add_back(NP, last=True)
        dve.wait_ge(g2_done, 1)
        st.link(tt_(YG[:, 1, :], YACC[:, 1, :], G2B, ALU.mult))
        dve.wait_ge(yg_pool, 1)
        for tt in range(TT):
            dve.wait_ge(y2_rt, tt + 1)
            st.link(dve.reciprocal(RS[:, 10 + tt:11 + tt], RS[:, 10 + tt:11 + tt]))
            for half in range(2):
                c = slice(half * HW, (half + 1) * HW)
                stt(X[:, tt, c], YG[:, tt, c], RS[:, 10 + tt:11 + tt], X[:, tt, c], ALU.mult, ALU.add).then_inc(res_done, 1)


_INS = ["x", "c", "ada_w", "ada_b", "norm_pre_mix", "norm_post_mix", "w_in", "fox_f_bias", "ret_gn_w",
        "fox_qn_w", "fox_kn_w", "fox_on_w", "w_out", "norm_pre_ffn", "norm_post_ffn",
        "router_coarse_w", "router_coarse_b", "router_fine_w", "router_fine_b", "w1", "w3", "w2"]


def kernel(**inputs):
    import numpy as _np
    import concourse.bacc as _bacc
    from concourse import mybir as _mybir
    from concourse.bass_utils import run_bass_kernel_spmd as _run

    nc = _bacc.Bacc("TRN2", target_bir_lowering=False, num_devices=1)
    arrays = {f"in_{name}_dram": _np.ascontiguousarray(inputs[name]) for name in _INS}
    arrays["shape_table_dram"], arrays["decay_table_dram"] = shape_tables()
    args = {n: nc.dram_tensor(n, v.shape, _mybir.dt.from_np(v.dtype), kind="ExternalInput").ap() for n, v in arrays.items()}
    x = arrays["in_x_dram"]
    out = nc.dram_tensor("out_dram", x.shape, _mybir.dt.from_np(x.dtype), kind="ExternalOutput").ap()
    build(nc, {n: args[f"in_{n}_dram"] for n in _INS}, args["shape_table_dram"], args["decay_table_dram"], out)
    r = _run(nc, [arrays], core_ids=[0])
    return r.results[0]["out_dram"]
```
